# Optimizing a Trainium2 kernel written in Bass

```python
import math
import jax, jax.numpy as jnp
from jax import lax
import numpy as np

D_MODEL = 1024
BATCH = 1
SEQ = 512
DEPTH = 1

HEAD_DIM = 64
N_Q_HEADS = 8
N_KV_HEADS = 2
GQA_GROUP = N_Q_HEADS // N_KV_HEADS
D_ATTN = N_Q_HEADS * HEAD_DIM
D_KV = N_KV_HEADS * HEAD_DIM
N_CONV_GROUPS = 8
D_CONV = D_MODEL - D_ATTN
D_MIX = D_ATTN + D_CONV
D_IN = D_ATTN + 2 * D_KV + 3 * D_CONV
WINDOW = 128
BLOCK = 128
CONV_WIDTH = 3
D_FF = 2816
ROPE_THETA = 10000.0
EPS = 1e-6
N_MOD = 6


def rms_norm(x, g):
    xf = x.astype(jnp.float32)
    y = xf * lax.rsqrt(jnp.mean(xf * xf, axis=-1, keepdims=True) + EPS)
    return (y * g.astype(jnp.float32)).astype(x.dtype)

def causal_dwconv3(x, w, b=None):
    s = x.shape[1]
    xp = jnp.pad(x, ((0, 0), (CONV_WIDTH - 1, 0), (0, 0)))
    y = xp[:, 0:s] * w[0] + xp[:, 1:s + 1] * w[1] + xp[:, 2:s + 2] * w[2]
    if b is not None:
        y = y + b
    return y

def rope(x, positions):
    half = HEAD_DIM // 2
    inv_freq = ROPE_THETA ** (-jnp.arange(0, half, dtype=jnp.float32) / half)
    ang = positions.astype(jnp.float32)[..., None] * inv_freq
    cos = jnp.cos(ang)[:, :, None, :]
    sin = jnp.sin(ang)[:, :, None, :]
    xf = x.astype(jnp.float32)
    x1, x2 = xf[..., :half], xf[..., half:]
    out = jnp.concatenate([x1 * cos - x2 * sin, x2 * cos + x1 * sin], axis=-1)
    return out.astype(x.dtype)

def sliding_window_attention(q, k, v, sinks):
    bsz, s = q.shape[0], q.shape[1]
    nb = s // BLOCK
    qb = q.reshape(bsz, nb, BLOCK, N_KV_HEADS, GQA_GROUP, HEAD_DIM)
    kb = k.reshape(bsz, nb, BLOCK, N_KV_HEADS, HEAD_DIM)
    vb = v.reshape(bsz, nb, BLOCK, N_KV_HEADS, HEAD_DIM)
    pad = ((0, 0), (1, 0), (0, 0), (0, 0), (0, 0))
    keys = jnp.concatenate([jnp.pad(kb, pad)[:, :-1], kb], axis=2)
    vals = jnp.concatenate([jnp.pad(vb, pad)[:, :-1], vb], axis=2)
    scores = jnp.einsum('bnqhgd,bnkhd->bnhgqk', qb, keys).astype(jnp.float32)
    scores = scores * (1.0 / math.sqrt(HEAD_DIM))
    qi = jnp.arange(BLOCK)[:, None]
    kj = jnp.arange(2 * BLOCK)[None, :]
    diff = qi + BLOCK - kj
    band = (diff >= 0) & (diff < WINDOW)
    blk = jnp.arange(nb)[:, None, None]
    valid = band[None] & ((blk > 0) | (kj[None] >= BLOCK))
    scores = jnp.where(valid[None, :, None, None], scores, -1e30)
    sink = sinks.astype(jnp.float32).reshape(1, 1, N_KV_HEADS, GQA_GROUP, 1, 1)
    sink = jnp.broadcast_to(sink, scores.shape[:-1] + (1,))
    probs = jax.nn.softmax(jnp.concatenate([scores, sink], axis=-1), axis=-1)[..., :-1]
    out = jnp.einsum('bnhgqk,bnkhd->bnqhgd', probs.astype(v.dtype), vals)
    return out.reshape(bsz, s, D_ATTN)

def first_inputs(seed: int = 0) -> dict:
    key = jax.random.key(seed)
    ks = jax.random.split(key, 20)
    f32 = jnp.float32
    nrm = lambda k, shape, scale: (jax.random.normal(k, shape, f32) * scale)
    gain = lambda k, shape: 1.0 + 0.05 * jax.random.normal(k, shape, f32)
    L = DEPTH
    return {
        "x": jax.random.normal(ks[0], (BATCH, SEQ, D_MODEL), f32),
        "c": jax.random.normal(ks[1], (BATCH, D_MODEL), f32),
        "positions": jnp.arange(SEQ, dtype=jnp.int32)[None, :]
                     + jax.random.randint(ks[2], (BATCH, 1), 0, 4096, dtype=jnp.int32),
        "ada_w": nrm(ks[3], (L, D_MODEL, N_MOD * D_MODEL), 0.5 * D_MODEL ** -0.5),
        "ada_b": nrm(ks[4], (L, N_MOD * D_MODEL), 0.02),
        "norm1_g": gain(ks[5], (L, D_MODEL)),
        "w_in": nrm(ks[6], (L, D_MODEL, D_IN), D_MODEL ** -0.5),
        "b_in": nrm(ks[7], (L, D_IN), 0.02),
        "conv_w": nrm(ks[8], (L, CONV_WIDTH, D_CONV), CONV_WIDTH ** -0.5),
        "attn_sinks": nrm(ks[9], (L, N_Q_HEADS), 0.5),
        "out_norm_attn_g": gain(ks[10], (L, D_ATTN)),
        "out_norm_conv_g": gain(ks[11], (L, D_CONV)),
        "w_o": nrm(ks[12], (L, D_MIX, D_MODEL), D_MIX ** -0.5),
        "norm2_g": gain(ks[13], (L, D_MODEL)),
        "w_up": nrm(ks[14], (L, D_MODEL, 2 * D_FF), D_MODEL ** -0.5),
        "ffn_conv_w": nrm(ks[15], (L, CONV_WIDTH, D_FF), CONV_WIDTH ** -0.5),
        "ffn_conv_b": nrm(ks[16], (L, D_FF), 0.02),
        "w_down": nrm(ks[17], (L, D_FF, D_MODEL), D_FF ** -0.5),
        "final_norm_g": gain(ks[18], (D_MODEL,)),
    }

def first_block(x, c, positions, ada_w, ada_b, norm1_g, w_in, b_in, conv_w, attn_sinks,
              out_norm_attn_g, out_norm_conv_g, w_o, norm2_g, w_up, ffn_conv_w,
              ffn_conv_b, w_down, final_norm_g):
    bsz, s, _ = x.shape
    c_act = jax.nn.silu(c)
    for l in range(DEPTH):
        mod = c_act @ ada_w[l] + ada_b[l]
        sh1, sc1, g1, sh2, sc2, g2 = [m[:, None, :] for m in jnp.split(mod, N_MOD, axis=-1)]

        h = rms_norm(x, norm1_g[l]) * (1.0 + sc1) + sh1
        proj = h @ w_in[l] + b_in[l]
        q, k, v, gb, gc, xs = jnp.split(
            proj, np.cumsum([D_ATTN, D_KV, D_KV, D_CONV, D_CONV]).tolist(), axis=-1)
        q = rope(q.reshape(bsz, s, N_Q_HEADS, HEAD_DIM), positions)
        k = rope(k.reshape(bsz, s, N_KV_HEADS, HEAD_DIM), positions)
        v = v.reshape(bsz, s, N_KV_HEADS, HEAD_DIM)
        y_attn = sliding_window_attention(q, k, v, attn_sinks[l])
        y_conv = gc * causal_dwconv3(gb * xs, conv_w[l])
        y = jnp.concatenate([rms_norm(y_attn, out_norm_attn_g[l]),
                             rms_norm(y_conv, out_norm_conv_g[l])], axis=-1)
        x = x + g1 * (y @ w_o[l])

        h = rms_norm(x, norm2_g[l]) * (1.0 + sc2) + sh2
        u = h @ w_up[l]
        gate, val = u[..., :D_FF], u[..., D_FF:]
        f = jax.nn.silu(causal_dwconv3(gate, ffn_conv_w[l], ffn_conv_b[l])) * val
        x = x + g2 * (f @ w_down[l])
    return rms_norm(x, final_norm_g)


DEPTH_2 = 2

N_MIXERS = 2
CHUNK = 64
RMS_EPS = 1e-6

RWKV_HEAD = 64
RWKV_HEADS = D_MODEL // RWKV_HEAD
DECAY_LORA = max(32, int(round(1.8 * D_MODEL ** 0.5 / 32)) * 32)
A_LORA = max(32, int(round(1.8 * D_MODEL ** 0.5 / 32)) * 32)
GATE_LORA = max(32, int(round(0.6 * D_MODEL ** 0.8 / 32)) * 32)
GN_EPS = 64e-5
N_SHIFT_MIX = 6

SGU_BLOCK = 128
D_SGU = D_MODEL
SGU_GROUPS = 8
SGU_GROUP_DIM = D_SGU // SGU_GROUPS
LN_EPS = 1e-5

D_FF_2 = -(-8 * D_MODEL // (3 * 256)) * 256

N_A = (DEPTH_2 + 1) // N_MIXERS + (0 if N_MIXERS == 2 else 0)
N_B = DEPTH_2 // N_MIXERS


def _rmsnorm(x, g):
    x32 = x.astype(jnp.float32)
    y = x32 * lax.rsqrt(jnp.mean(x32 * x32, axis=-1, keepdims=True) + RMS_EPS)
    return (y * g.astype(jnp.float32)).astype(x.dtype)

def _token_shift(x):
    return jnp.pad(x[:, :-1], ((0, 0), (1, 0), (0, 0)))

def _rwkv7_scan(r, w, k, v, a, b):
    B, T, H, N = r.shape

    def step(S, inp):
        r_t, w_t, k_t, v_t, a_t, b_t = inp
        sa = jnp.einsum('bhij,bhj->bhi', S, a_t)
        S = (S * w_t[:, :, None, :]
             + sa[..., None] * b_t[:, :, None, :]
             + v_t[..., None] * k_t[:, :, None, :])
        y = jnp.einsum('bhij,bhj->bhi', S, r_t)
        return S, y

    xs = tuple(jnp.moveaxis(t, 1, 0) for t in (r, w, k, v, a, b))
    S0 = jnp.zeros((B, H, N, N), jnp.float32)
    _, y = lax.scan(step, S0, xs)
    return jnp.moveaxis(y, 0, 1)

def _rwkv7_time_mix(x, mix, w_rkv, w0, w1, w2, a0, a1, a2, g1, g2,
                    k_k, k_a, r_k, gn_w, gn_b, w_o):
    B, T, D = x.shape
    H, N = RWKV_HEADS, RWKV_HEAD
    f32 = jnp.float32
    xx = _token_shift(x) - x
    xs = x[None] + xx[None] * mix[:, None, None, :]
    r, k, v = jnp.einsum('cbtd,cde->cbte', xs[:3], w_rkv)
    xw, xa, xg = xs[3], xs[4], xs[5]
    w_raw = (w0 + jnp.tanh(xw @ w1) @ w2).astype(f32)
    w_log = -jax.nn.softplus(-w_raw) - 0.5
    decay = jnp.exp(-jnp.exp(w_log))
    a = jax.nn.sigmoid(a0 + (xa @ a1) @ a2)
    g = jax.nn.sigmoid(xg @ g1) @ g2
    heads = lambda t: t.reshape(B, T, H, N).astype(f32)
    kk = heads(k * k_k)
    kk = kk / jnp.maximum(jnp.sqrt(jnp.sum(kk * kk, axis=-1, keepdims=True)), 1e-12)
    k = k * (1.0 + (a - 1.0) * k_a)
    r_h, k_h, v_h, a_h = heads(r), heads(k), heads(v), heads(a)
    y = _rwkv7_scan(r_h, decay.reshape(B, T, H, N), k_h, v_h, -kk, kk * a_h)
    mu = jnp.mean(y, axis=-1, keepdims=True)
    var = jnp.mean(jnp.square(y - mu), axis=-1, keepdims=True)
    y = (y - mu) * lax.rsqrt(var + GN_EPS)
    y = y * gn_w.reshape(H, N).astype(f32) + gn_b.reshape(H, N).astype(f32)
    y = y + jnp.sum(r_h * k_h * r_k.astype(f32), axis=-1, keepdims=True) * v_h
    y = y.reshape(B, T, D).astype(x.dtype)
    return (y * g) @ w_o

def _sgu_mixer(x, w_in, b_in, ln_w, ln_b, ws, bs, w_out):
    B, T, D = x.shape
    h = jax.nn.gelu(x @ w_in + b_in, approximate=False)
    u, v = jnp.split(h, 2, axis=-1)
    v32 = v.astype(jnp.float32)
    mu = jnp.mean(v32, axis=-1, keepdims=True)
    var = jnp.mean(jnp.square(v32 - mu), axis=-1, keepdims=True)
    v = ((v32 - mu) * lax.rsqrt(var + LN_EPS) * ln_w.astype(jnp.float32)
         + ln_b.astype(jnp.float32)).astype(x.dtype)
    n_blk = T // SGU_BLOCK
    vb = v.reshape(B, n_blk, SGU_BLOCK, SGU_GROUPS, SGU_GROUP_DIM)
    chunk_id = jnp.arange(SGU_BLOCK) // CHUNK
    mask = chunk_id[None, :] <= chunk_id[:, None]
    ws_m = jnp.where(mask[None], ws, jnp.zeros((), ws.dtype))
    s = jnp.einsum('gij,bnjgc->bnigc', ws_m, vb) + bs.T[None, None, :, :, None]
    s = s.reshape(B, T, D_SGU)
    return (u * s) @ w_out

def _swiglu(x, w_gate, w_up, w_down):
    return (jax.nn.silu(x @ w_gate) * (x @ w_up)) @ w_down

def second_inputs(seed: int = 0) -> dict:
    key = jax.random.key(seed)
    ks = jax.random.split(key, 32)
    D = D_MODEL
    nrm = lambda k, shape, scale: jax.random.normal(k, shape, jnp.float32) * scale
    return {
        "x": nrm(ks[0], (BATCH, SEQ, D), 1.0),
        "norm_gains": 1.0 + nrm(ks[1], (DEPTH_2, 4, D), 0.1),
        "rwkv_mix": jax.random.uniform(ks[2], (N_A, N_SHIFT_MIX, D), jnp.float32),
        "rwkv_w_rkv": nrm(ks[3], (N_A, 3, D, D), D ** -0.5),
        "rwkv_w0": jax.random.uniform(ks[4], (N_A, D), jnp.float32, -6.5, -1.5),
        "rwkv_w1": nrm(ks[5], (N_A, D, DECAY_LORA), D ** -0.5),
        "rwkv_w2": nrm(ks[6], (N_A, DECAY_LORA, D), 0.5 * DECAY_LORA ** -0.5),
        "rwkv_a0": nrm(ks[7], (N_A, D), 0.1),
        "rwkv_a1": nrm(ks[8], (N_A, D, A_LORA), D ** -0.5),
        "rwkv_a2": nrm(ks[9], (N_A, A_LORA, D), 0.5 * A_LORA ** -0.5),
        "rwkv_g1": nrm(ks[10], (N_A, D, GATE_LORA), D ** -0.5),
        "rwkv_g2": nrm(ks[11], (N_A, GATE_LORA, D), GATE_LORA ** -0.5),
        "rwkv_k_k": 0.85 + nrm(ks[12], (N_A, D), 0.05),
        "rwkv_k_a": 1.0 + nrm(ks[13], (N_A, D), 0.05),
        "rwkv_r_k": -0.04 + nrm(ks[14], (N_A, RWKV_HEADS, RWKV_HEAD), 0.02),
        "rwkv_gn_w": 1.0 + nrm(ks[15], (N_A, D), 0.1),
        "rwkv_gn_b": nrm(ks[16], (N_A, D), 0.02),
        "rwkv_w_o": nrm(ks[17], (N_A, D, D), D ** -0.5),
        "sgu_w_in": nrm(ks[18], (N_B, D, 2 * D_SGU), D ** -0.5),
        "sgu_b_in": nrm(ks[19], (N_B, 2 * D_SGU), 0.02),
        "sgu_ln_w": 1.0 + nrm(ks[20], (N_B, D_SGU), 0.1),
        "sgu_ln_b": nrm(ks[21], (N_B, D_SGU), 0.02),
        "sgu_ws": nrm(ks[22], (N_B, SGU_GROUPS, SGU_BLOCK, SGU_BLOCK), SGU_BLOCK ** -0.5),
        "sgu_bs": 1.0 + nrm(ks[23], (N_B, SGU_GROUPS, SGU_BLOCK), 0.1),
        "sgu_w_out": nrm(ks[24], (N_B, D_SGU, D), D_SGU ** -0.5),
        "ffn_w_gate": nrm(ks[25], (DEPTH_2, D, D_FF_2), D ** -0.5),
        "ffn_w_up": nrm(ks[26], (DEPTH_2, D, D_FF_2), D ** -0.5),
        "ffn_w_down": nrm(ks[27], (DEPTH_2, D_FF_2, D), D_FF_2 ** -0.5),
    }

def second_block(x, norm_gains,
              rwkv_mix, rwkv_w_rkv, rwkv_w0, rwkv_w1, rwkv_w2, rwkv_a0, rwkv_a1, rwkv_a2,
              rwkv_g1, rwkv_g2, rwkv_k_k, rwkv_k_a, rwkv_r_k, rwkv_gn_w, rwkv_gn_b, rwkv_w_o,
              sgu_w_in, sgu_b_in, sgu_ln_w, sgu_ln_b, sgu_ws, sgu_bs, sgu_w_out,
              ffn_w_gate, ffn_w_up, ffn_w_down):
    for i in range(DEPTH_2):
        j = i // N_MIXERS
        h = _rmsnorm(x, norm_gains[i, 0])
        if i % N_MIXERS == 0:
            h = _rwkv7_time_mix(h, rwkv_mix[j], rwkv_w_rkv[j], rwkv_w0[j], rwkv_w1[j],
                                rwkv_w2[j], rwkv_a0[j], rwkv_a1[j], rwkv_a2[j], rwkv_g1[j],
                                rwkv_g2[j], rwkv_k_k[j], rwkv_k_a[j], rwkv_r_k[j],
                                rwkv_gn_w[j], rwkv_gn_b[j], rwkv_w_o[j])
        else:
            h = _sgu_mixer(h, sgu_w_in[j], sgu_b_in[j], sgu_ln_w[j], sgu_ln_b[j],
                           sgu_ws[j], sgu_bs[j], sgu_w_out[j])
        x = x + _rmsnorm(h, norm_gains[i, 1])
        h = _rmsnorm(x, norm_gains[i, 2])
        h = _swiglu(h, ffn_w_gate[i], ffn_w_up[i], ffn_w_down[i])
        x = x + _rmsnorm(h, norm_gains[i, 3])
    return x


def setup_inputs(seed=0):
    out = dict(first_inputs(seed))
    for name, value in second_inputs(seed + 1).items():
        if name != "x":
            out[name + "_2"] = value
    return out


def reference(
    x, c, positions, ada_w, ada_b, norm1_g, w_in, b_in, conv_w, attn_sinks, out_norm_attn_g,
    out_norm_conv_g, w_o, norm2_g, w_up, ffn_conv_w, ffn_conv_b, w_down, final_norm_g,
    norm_gains_2, rwkv_mix_2, rwkv_w_rkv_2, rwkv_w0_2, rwkv_w1_2, rwkv_w2_2, rwkv_a0_2,
    rwkv_a1_2, rwkv_a2_2, rwkv_g1_2, rwkv_g2_2, rwkv_k_k_2, rwkv_k_a_2, rwkv_r_k_2, rwkv_gn_w_2,
    rwkv_gn_b_2, rwkv_w_o_2, sgu_w_in_2, sgu_b_in_2, sgu_ln_w_2, sgu_ln_b_2, sgu_ws_2, sgu_bs_2,
    sgu_w_out_2, ffn_w_gate_2, ffn_w_up_2, ffn_w_down_2,
):
    x = first_block(
        x, c, positions, ada_w, ada_b, norm1_g, w_in, b_in, conv_w, attn_sinks, out_norm_attn_g,
        out_norm_conv_g, w_o, norm2_g, w_up, ffn_conv_w, ffn_conv_b, w_down, final_norm_g,
    )
    return second_block(
        x, norm_gains_2, rwkv_mix_2, rwkv_w_rkv_2, rwkv_w0_2, rwkv_w1_2, rwkv_w2_2, rwkv_a0_2,
        rwkv_a1_2, rwkv_a2_2, rwkv_g1_2, rwkv_g2_2, rwkv_k_k_2, rwkv_k_a_2, rwkv_r_k_2,
        rwkv_gn_w_2, rwkv_gn_b_2, rwkv_w_o_2, sgu_w_in_2, sgu_b_in_2, sgu_ln_w_2, sgu_ln_b_2,
        sgu_ws_2, sgu_bs_2, sgu_w_out_2, ffn_w_gate_2, ffn_w_up_2, ffn_w_down_2,
    )


_drawn_inputs = setup_inputs


def setup_inputs(seed=0):
    import zlib

    import numpy as np

    out = dict(_drawn_inputs(seed))
    spreads = {}
    factors = {'attn_sinks': 3.502, 'ffn_conv_b': 6.948, 'sgu_b_in_2': 4.075, 'sgu_ln_b_2': 7.987}
    for name, (base, spread) in spreads.items():
        noise = np.random.default_rng([zlib.crc32(name.encode()), seed]).standard_normal(out[name].shape)
        drawn = base * np.exp(spread * noise) if base else spread * noise
        out[name] = __import__('jax').numpy.asarray(drawn.astype(out[name].dtype))
    for name, factor in factors.items():
        out[name] = (out[name] * factor).astype(out[name].dtype)
    return out
```

```python
from contextlib import ExitStack

import numpy as np

import concourse.bass as bass
from concourse import mybir

F32 = mybir.dt.float32
F32R = mybir.dt.float32r
I32 = mybir.dt.int32
ALU = mybir.AluOpType
ACT = mybir.ActivationFunctionType
AX_X = mybir.AxisListType.X

P = 128
T = 512
D = 1024
KD = D // P
NT = T // P
DFF = 2816
KF = DFF // P
HALF = KF // 2
HD = 64
NQ, NKV = 8, 2
DA = NQ * HD
KA = DA // P
RAW = 4
EPS = 1e-6
TWO_PI = 2 * np.pi
TURN1 = 6.28125
TURN2 = float(np.float32(round((TWO_PI - TURN1) * 2 ** 22) / 2 ** 22))
TURN3 = float(np.float32(TWO_PI - TURN1 - TURN2))
ROUND = float(1.5 * 2 ** 23)
MASKED = -1e30


class Count:

    def __init__(self, sem):
        self.sem, self.n = sem, 0

    def claim(self, n):
        self.n += n
        return self.n - n


class At:

    def __init__(self, c, u, step=0, i=0):
        self.c, self.u, self.step, self.i = c, u, step, i

    def plus(self, k):
        return At(self.c + k, self.u + k, self.step, self.i)

    @property
    def raw_slot(self):
        return self.c % RAW

    @property
    def slot(self):
        return self.u % 2

    @property
    def count(self):
        return self.u + 1 + self.i * self.step


def wait(eng, sem, value):
    if isinstance(value, int) and value <= 0:
        return
    eng.wait_ge(sem, value)


def loop(eng, n, body):
    body(0, False)
    with eng.Fori(1, n - 1) as i:
        body(i, False)
    body(n - 1, True)


def tile_at(t, k):
    if isinstance(k, int):
        return t[:, k, :]
    return t[:, bass.ds(k, 1), :].rearrange("p a n -> p (a n)")


def cols_at(t, start, n):
    return t[:, start:start + n] if isinstance(start, int) else t[:, bass.ds(start, n)]


def col_at(t, k):
    if isinstance(k, int):
        return t[:, k:k + 1]
    return t[:, bass.ds(k, 1)]


def build(nc, A, out):
    ctx = ExitStack()

    def sb(name, shape, dt=F32):
        return ctx.enter_context(nc.sbuf_tensor(name, shape, dt))

    def sem(name):
        return ctx.enter_context(nc.semaphore(name))

    def count(name):
        return Count(sem(name))

    x = sb("x", [P, KD, T])
    raw = sb("raw", [P, RAW, HALF * P])
    whi = sb("whi", [P, 2, HALF * P], F32R)
    wlo = sb("wlo", [P, 2, HALF * P], F32R)
    ident = sb("ident", [P, P])
    ones = sb("ones", [P, P])
    tmp = sb("tmp", [P, 3, T])
    sq = sb("sq", [P, 2, T])
    var = sb("var", [P, T])
    rstd = sb("rstd", [P, T])
    mod = sb("mod", [P, 6 * KD])
    gain = sb("gain", [P, KD])
    cact = sb("cact", [P, KD])
    bank = [ctx.enter_context(nc.psum_tensor(f"bank{i}", [P, T], F32)) for i in range(8)]
    NORM_BANK, ADA_BANKS = 4, (7, 6, 7)

    vec_src, col = [], {}

    def vec(name, sources, n):
        col[name] = sum(m for _, m in vec_src)
        vec_src.append((sources, n))

    def vec_rows(name, ap, n):
        vec(name, [(slice(0, P), ap)], n)

    def vec_pairs(name, ap):
        vec(name, [(slice(0, HD), ap[0:DA // 2].rearrange("(j p) -> j p", p=HD)),
                   (slice(HD, P), ap[DA // 2:DA].rearrange("(j p) -> j p", p=HD))], KA)

    flat = lambda ap: ap.rearrange("a n -> (a n)")
    rows = lambda ap: ap.rearrange("(k p) -> k p", p=P)
    vec_rows("c", rows(flat(A["c"])), KD)
    vec_rows("ada_b", rows(flat(A["ada_b"])), 6 * KD)
    vec_rows("norm1", rows(flat(A["norm1_g"])), KD)
    vec_rows("b_in", rows(flat(A["b_in"])[DA:]), 14)
    vec_pairs("bq", flat(A["b_in"])[0:DA])
    vec_rows("conv_w", A["conv_w"].rearrange("a w (k p) -> (a w k) p", p=P), 12)
    vec_rows("ga", rows(flat(A["out_norm_attn_g"])), KA)
    vec_rows("gcv", rows(flat(A["out_norm_conv_g"])), 4)
    vec_rows("norm2", rows(flat(A["norm2_g"])), KD)
    vec_rows("final", rows(A["final_norm_g"]), KD)

    vec_rows("ffn_cw", A["ffn_conv_w"].rearrange("a w (k p) -> (a w k) p", p=P), 3 * KF)
    vec_rows("ffn_cb", rows(flat(A["ffn_conv_b"])), KF)

    vec_rows("w0", rows(flat(A["rwkv_w0_2"])), KD)
    vec_rows("a0", rows(flat(A["rwkv_a0_2"])), KD)
    vec_rows("k_k", rows(flat(A["rwkv_k_k_2"])), KD)
    vec_rows("k_a", rows(flat(A["rwkv_k_a_2"])), KD)
    vec_rows("mix", A["rwkv_mix_2"].rearrange("a m (k p) -> (a m k) p", p=P), 6 * KD)
    vec_rows("r_k", A["rwkv_r_k_2"].rearrange("a (k h) n -> (a k) (h n)", h=2), KD)
    vec_rows("gn_w", rows(flat(A["rwkv_gn_w_2"])), KD)
    vec_rows("gn_b", rows(flat(A["rwkv_gn_b_2"])), KD)
    vec_rows("gains", A["norm_gains_2"].rearrange("l m (k p) -> (l m k) p", p=P), 8 * KD)
    vec_rows("sgu_b", rows(flat(A["sgu_b_in_2"])), 2 * KD)
    vec_rows("ln_w", rows(flat(A["sgu_ln_w_2"])), KD)
    vec_rows("ln_b", rows(flat(A["sgu_ln_b_2"])), KD)
    n_vec = sum(m for _, m in vec_src)
    VB = -(-n_vec // P)
    vecs = sb("vecs", [P, VB * P])

    def v(name, k=0):
        return col_at(vecs, col[name] + k)

    landed = [sem(f"raw{s}_landed") for s in range(RAW)]
    hi_ready, lo_ready = sem("hi_ready"), sem("lo_ready")
    unit_done, ada_done = sem("unit_done"), sem("ada_done")
    n_units = [0, 0]

    def raw_unit(at, kts):
        return raw[:, at.raw_slot, 0:kts * P]

    def load(sp, at, parts, freed):
        if freed is not None:
            wait(sp, *freed)
        for dst, src in parts:
            sp.dma_start(dst, src).then_inc(landed[at.raw_slot], 16)

    def unit_parts(at, w, ks, cols):
        k0, kts = ks
        src = cols_at(w[k0 * P:(k0 + kts) * P, :], *cols).rearrange("(k p) n -> p k n", p=P)
        return [(raw[:, at.raw_slot, 0:kts * P].rearrange("p (k n) -> p k n", n=P), src)]

    def split_hi(act, at, kts=KD):
        act.wait_ge(landed[at.raw_slot], landed_at(at))
        wait(act, unit_done, at.plus(-2).count)
        act.activation(whi[:, at.slot, 0:kts * P], raw_unit(at, kts), ACT.Copy).then_inc(hi_ready, 1)

    def split_lo(dve, at, kts=KD):
        dve.wait_ge(landed[at.raw_slot], landed_at(at))
        dve.wait_ge(hi_ready, at.count)
        dve.tensor_tensor(wlo[:, at.slot, 0:kts * P], raw_unit(at, kts),
                          whi[:, at.slot, 0:kts * P].bitcast(F32), ALU.subtract).then_inc(lo_ready, 1)

    def unit_products(pe, at, kts, dst, rhs_hi, rhs_lo, first, last, k_ready=None):
        pe.wait_ge(lo_ready, at.count)
        for k in range(kts):
            if k_ready is not None:
                k_ready(k)
            hi, lo = (w[:, at.slot, k * P:(k + 1) * P] for w in (whi, wlo))
            pe.matmul(dst, hi, rhs_hi(k), start=first and k == 0, stop=False)
            pe.matmul(dst, hi, rhs_lo(k), start=False, stop=False)
            mm = pe.matmul(dst, lo, rhs_hi(k), start=False, stop=last and k == kts - 1)
        mm.then_inc(unit_done, 1)

    sq_ready, sum_step = count("sq_ready"), count("sum_step")
    var_ready, std_ready, rstd_ready = count("var_ready"), count("std_ready"), count("rstd_ready")
    tmp_ready, nhi_ready, h_ready = count("tmp_ready"), count("nhi_ready"), count("h_ready")
    x_ready, x_added = count("x_ready"), count("x_added")

    class Norm:

        def __init__(self, src, n, ready, eps=EPS):
            self.src, self.n, self.ready, self.eps = src, n, ready, eps
            self.sq0, self.sum0 = sq_ready.claim(n), sum_step.claim(n)
            self.var0, self.std0, self.rstd0 = (c.claim(1) for c in (var_ready, std_ready, rstd_ready))

        def act_squares(self, act):
            for k in range(self.n):
                self.ready(act, k)
                wait(act, sum_step.sem, self.sum0 + k - 1)
                act.activation(sq[:, (self.sq0 + k) % 2, :], self.src(k), ACT.Square)\
                   .then_inc(sq_ready.sem, 1)

        def act_root(self, act):
            act.wait_ge(var_ready.sem, self.var0 + 1)
            act.activation(var[:, :], var[:, :], ACT.Sqrt).then_inc(std_ready.sem, 1)

        def pe_sums(self, pe):
            wait(pe, var_ready.sem, self.var0)
            for k in range(self.n):
                pe.wait_ge(sq_ready.sem, self.sq0 + k + 1)
                pe.matmul(bank[NORM_BANK][:, :], ones[:, :], sq[:, (self.sq0 + k) % 2, :],
                          start=k == 0, stop=k == self.n - 1).then_inc(sum_step.sem, 1)

        def dve_rstd(self, dve):
            dve.wait_ge(sum_step.sem, self.sum0 + self.n)
            dve.tensor_scalar(var[:, :], bank[NORM_BANK][:, :], 1.0 / (self.n * P), self.eps,
                              ALU.mult, ALU.add).then_inc(var_ready.sem, 1)
            dve.wait_ge(std_ready.sem, self.std0 + 1)
            dve.reciprocal(rstd[:, :], var[:, :]).then_inc(rstd_ready.sem, 1)
            dve.wait_ge(rstd_ready.sem, self.rstd0 + 1)

    class Split:

        def __init__(self, src, n, gains, shift, dst_hi, dst_lo, free):
            self.src, self.n, self.gains, self.shift = src, n, gains, shift
            self.hi, self.lo, self.free = dst_hi, dst_lo, free
            self.t0, self.hi0, self.h0 = (c.claim(n) for c in (tmp_ready, nhi_ready, h_ready))

        def dve(self, dve):
            def lower(k):
                dve.wait_ge(nhi_ready.sem, self.hi0 + k + 1)
                if self.shift is None:
                    ins = dve.tensor_tensor(self.lo(k), tmp[:, (self.t0 + k) % 3, :],
                                            self.hi(k).bitcast(F32), ALU.subtract)
                else:
                    ins = dve.scalar_tensor_tensor(self.lo(k), tmp[:, (self.t0 + k) % 3, :], self.shift(k),
                                                   self.hi(k).bitcast(F32), ALU.add, ALU.subtract)
                ins.then_inc(h_ready.sem, 1)

            self.free(dve)
            for k in range(self.n):
                wait(dve, h_ready.sem, self.h0 + k - 2)
                dve.scalar_tensor_tensor(tmp[:, (self.t0 + k) % 3, :], self.src(k), self.gains(k),
                                         rstd[:, :], ALU.mult, ALU.mult).then_inc(tmp_ready.sem, 1)
                if k == 0:
                    dve.wait_ge(tmp_ready.sem, self.t0 + 1)
                if k:
                    dve.wait_ge(tmp_ready.sem, self.t0 + k)
                    lower(k - 1)
            lower(self.n - 1)

        def act(self, act):
            self.free(act)
            for k in range(self.n):
                act.wait_ge(tmp_ready.sem, self.t0 + k + 1)
                act.activation(self.hi(k), tmp[:, (self.t0 + k) % 3, :], ACT.Identity,
                               bias=0.0 if self.shift is None else self.shift(k))\
                   .then_inc(nhi_ready.sem, 1)

        def pe_ready(self, pe):
            return lambda k: pe.wait_ge(h_ready.sem, self.h0 + k + 1)

    w_in, w_o, ada_w = (A[n].rearrange("a k n -> (a k) n") for n in ("w_in", "w_o", "ada_w"))
    order = [("ada", m) for m in range(2 * KD)]
    N_IN, N_O = 18, KD
    ada_next = 2 * KD
    for u in range(N_IN):
        order += [("in", u), ("ada", ada_next)]
        ada_next += 1
    for u in range(N_O):
        order.append(("o", u))
        n_ada = 0 if u >= 4 else 3 if u < 2 else 4
        for _ in range(n_ada):
            order.append(("ada", ada_next))
            ada_next += 1
    assert ada_next == 6 * KD
    at_in, at_ada, at_o, seq = {}, {}, {}, []
    u_next = 0
    for c, (kind, n) in enumerate(order):
        at = At(c, u_next)
        seq.append((kind, n, at))
        {"in": at_in, "o": at_o, "ada": at_ada}[kind][n] = at
        u_next += kind != "ada"
    first = [at for kind, _, at in seq if kind != "ada"]
    for n in range(2):
        first.append(At(len(seq) + n, u_next + n))
    IN0 = {"q": 0, "k": 4, "v": 5, "conv": 6}

    def in_columns(u):
        if u < 6:
            return u * P, P
        j, part = divmod(u - 6, 3)
        start = DA + 2 * NKV * HD + part * (D - DA) + j * P
        return start, P

    fixed, slot_count = {}, [0] * RAW
    for kind, n, at in seq:
        slot_count[at.raw_slot] += 32 if kind == "in" and n < 4 else 16
        fixed[at.c] = slot_count[at.raw_slot]

    def landed_at(at):
        if at.c < len(seq):
            return fixed[at.c]
        more = (at.c // RAW + 1) - (len(seq) + RAW - 1 - at.raw_slot) // RAW
        return slot_count[at.raw_slot] + more * 16 + at.i * (at.step // RAW * 16)

    def sp_first_units(sp):
        for c, (kind, n, at) in enumerate(seq):
            freed = None
            if c >= RAW:
                was, m, old = seq[c - RAW]
                freed = (ada_done, m + 1) if was == "ada" else (lo_ready, old.count)
            if kind == "ada":
                parts = unit_parts(at, ada_w, (0, KD), (n * P, P))
            elif kind == "o":
                parts = unit_parts(at, w_o, (0, KD), (n * P, P))
            elif n < 4:
                parts = [(raw[:, at.raw_slot, 0:KD * P].rearrange("p (k h d) -> p k h d", h=2, d=HD)[:, :, h, :],
                          w_in[:, (n + 4 * h) * HD:(n + 4 * h + 1) * HD].rearrange("(k p) d -> p k d", p=P))
                         for h in range(2)]
            else:
                parts = unit_parts(at, w_in, (0, KD), in_columns(n))
            load(sp, at, parts, freed)

    setup = ExitStack()

    def sbs(stage, name, shape, dt=F32):
        return stage.enter_context(nc.sbuf_tensor(name, shape, dt))

    mixer1 = ExitStack()
    h_hi = sbs(mixer1, "h_hi", [P, KD, T], F32R)
    h_lo = sbs(mixer1, "h_lo", [P, KD, T], F32R)
    rot = sbs(mixer1, "rot", [P, P])
    mask = sbs(mixer1, "mask", [P, 2 * P])
    cos_t = sbs(mixer1, "cos_t", [P, T])
    sin_t = sbs(mixer1, "sin_t", [P, T])
    sinks = sbs(mixer1, "sinks", [P, NQ])
    sinks_row = sbs(mixer1, "sinks_row", [1, NQ])
    invf = sbs(mixer1, "invf", [P, 1])
    pos_i = sbs(mixer1, "pos_i", [1, T], I32)
    pos_f = sbs(mixer1, "pos_f", [1, T])
    q_t = sbs(mixer1, "q_t", [P, KA, T])
    k_t = sbs(mixer1, "k_t", [P, T])
    v_tok = sbs(mixer1, "v_tok", [P, NT, P])
    prj = sbs(mixer1, "prj", [P, 2, T])
    s_sb = sbs(mixer1, "s_sb", [P, 2, 2, 2 * P])
    p_sb = sbs(mixer1, "p_sb", [P, 2, 2, 2 * P])
    p_t = sbs(mixer1, "p_t", [P, 2, 4 * P])
    st = sbs(mixer1, "st", [P, 2, 12])
    y_at = sbs(mixer1, "y_at", [P, KA, T])
    y_cv = sbs(mixer1, "y_cv", [P, 4, T])
    gb_sb = sbs(mixer1, "gb_sb", [P, 2, T])
    cbuf = sbs(mixer1, "cbuf", [P, 2, T + 2])
    cacc = sbs(mixer1, "cacc", [P, 2, T])
    x_tok = sbs(setup, "x_tok", [P, NT, D])
    vrow = sbs(setup, "vrow", [P, VB, P])
    ang = sbs(setup, "ang", [P, 6, T])
    setup.close()

    x_landed, vec_landed, small_landed = sem("x_landed"), sem("vec_landed"), sem("small_landed")
    const_ready, x_turned, vec_turned = sem("const_ready"), sem("x_turned"), sem("vec_turned")
    vecs_ready, small_in, small_out, angle = sem("vecs_ready"), sem("small_in"), sem("small_out"), sem("angle")
    cact_ready = sem("cact_ready")
    n_vec_dmas = 0
    VEC_PLAN = []
    for sources, n in vec_src:
        row = sum(m for _, m in vec_src[:vec_src.index((sources, n))])
        done = 0
        while done < n:
            b, r = divmod(row + done, P)
            m = min(n - done, P - r)
            for cols, ap in sources:
                VEC_PLAN.append((vrow[r:r + m, b, cols], ap[done:done + m, :]))
            done += m
    LAST_ROWS = n_vec - (VB - 1) * P
    x_ready.claim(KD)

    def sp_setup(sp):
        x_in = A["x"].rearrange("b (t p) d -> (b t) p d", p=P)
        for dst, src in VEC_PLAN:
            sp.dma_start(dst, src).then_inc(vec_landed, 16)
        for t in range(NT):
            sp.dma_start(x_tok[:, t, :], x_in[t]).then_inc(x_landed, 16)

    def act_setup_dmas(act):
        act.dma_start(pos_i[:, :], A["positions"]).then_inc(small_landed, 16)
        act.dma_start(sinks_row[:, :], A["attn_sinks"]).then_inc(small_landed, 16)
        act.dma_start(invf[:, :], A["inv_freq"]).then_inc(small_landed, 16)

    def pool_setup(pool):
        pool.memset(ident[:, :], 0.0).then_inc(const_ready, 1)
        pool.memset(ones[:, :], 1.0).then_inc(const_ready, 1)
        pool.memset(rot[:, :], 0.0).then_inc(const_ready, 1)
        pool.memset(mask[:, :], 0.0).then_inc(const_ready, 1)
        pool.wait_ge(const_ready, 4)
        pool.affine_select(out=ident[:, :], in_=ident[:, :], compare_op=ALU.not_equal, fill=1.0, base=0,
                           pattern=[[-1, P]], channel_multiplier=1).then_inc(const_ready, 1)
        lower = rot[:, :].rearrange("p (h s m) -> p h s m", h=2, s=2)
        pool.affine_select(out=lower[:, :, 0, :], in_=lower[:, :, 0, :], compare_op=ALU.not_equal, fill=-1.0,
                           base=-32, pattern=[[-HD, 2], [-1, 32]], channel_multiplier=1).then_inc(const_ready, 1)
        pool.wait_ge(const_ready, 6)
        pool.affine_select(out=lower[:, :, 1, :], in_=lower[:, :, 1, :], compare_op=ALU.not_equal, fill=1.0,
                           base=0, pattern=[[-HD, 2], [-1, 32]], channel_multiplier=1).then_inc(const_ready, 1)
        pool.affine_select(out=mask[:, :], in_=mask[:, :], compare_op=ALU.is_ge, fill=MASKED, base=P,
                           pattern=[[-1, 2 * P]], channel_multiplier=1).then_inc(const_ready, 1)
        pool.wait_ge(const_ready, 8)
        pool.affine_select(out=mask[:, :], in_=mask[:, :], compare_op=ALU.is_gt, fill=MASKED, base=0,
                           pattern=[[1, 2 * P]], channel_multiplier=-1).then_inc(const_ready, 1)
        pool.memset(cbuf[:, :, 0:2], 0.0).then_inc(const_ready, 1)

    CONSTS = 10

    def pe_setup(pe):
        pe.wait_ge(const_ready, CONSTS)
        pe.wait_ge(vec_landed, 16 * len(VEC_PLAN))
        for b in range(VB):
            m = P if b < VB - 1 else LAST_ROWS
            tr = pe.transpose(bank[5][:, b * P:b * P + m], vrow[0:m, b, :], ident[0:m, 0:m])
        tr.then_inc(vec_turned, 1)
        pe.wait_ge(x_landed, 16 * NT)
        for k in range(KD):
            wait(pe, x_ready.sem, k - 1)
            for t in range(NT):
                tr = pe.transpose(bank[k % 2][:, t * P:(t + 1) * P], x_tok[:, t, k * P:(k + 1) * P], ident[:, :])
            tr.then_inc(x_turned, 1)
        pe.wait_ge(small_in, 1)
        pe.matmul(bank[2][:, :], ones[0:1, :], pos_f[:, :], start=True, stop=True)
        pe.matmul(bank[3][:, 0:NQ], ones[0:1, :], sinks_row[:, :], start=True, stop=True).then_inc(small_out, 1)

    def act_setup(act):
        act.wait_ge(vec_turned, 1)
        act.activation(vecs[:, 0:n_vec], bank[5][:, 0:n_vec], ACT.Copy).then_inc(vecs_ready, 1)
        act.wait_ge(vecs_ready, 1)
        act.activation(cact[:, :], vecs[:, col["c"]:col["c"] + KD], ACT.Silu).then_inc(cact_ready, 1)

    def dve_setup(dve):
        dve.wait_ge(small_landed, 48)
        dve.tensor_copy(pos_f[:, :], pos_i[:, :]).then_inc(small_in, 1)
        for k in range(KD):
            dve.wait_ge(x_turned, k + 1)
            dve.tensor_copy(x[:, k, :], bank[k % 2][:, :]).then_inc(x_ready.sem, 1)
        dve.wait_ge(small_out, 1)
        dve.tensor_copy(sinks[:, :], bank[3][:, 0:NQ]).then_inc(angle, 1)
        steps = [0]

        def step(ins):
            ins.then_inc(angle, 1)
            steps[0] += 1
            dve.wait_ge(angle, steps[0] + 1)

        a = lambda n: ang[:, n, :]
        step(dve.tensor_scalar(a(0), bank[2][:, :], invf[:, 0:1], None, ALU.mult))
        for n, quarter, shift, dst in ((1, 0.0, 0.0, a(4)), (2, 0.25, float(np.pi / 2), a(5))):
            step(dve.tensor_scalar(a(n), a(0), 1 / TWO_PI, quarter, ALU.mult, ALU.add))
            step(dve.tensor_scalar(a(3), a(n), ROUND, ROUND, ALU.add, ALU.subtract))
            step(dve.scalar_tensor_tensor(a(n), a(3), -TURN1, a(0), ALU.mult, ALU.add))
            step(dve.scalar_tensor_tensor(dst, a(3), -TURN2, a(n), ALU.mult, ALU.add))
            step(dve.scalar_tensor_tensor(a(n), a(3), -TURN3, dst, ALU.mult, ALU.add))
            step(dve.tensor_scalar(a(3), a(n), shift, 3.1415925, ALU.add, ALU.min))
            step(dve.tensor_scalar(dst, a(3), -3.1415925, None, ALU.max))

    ANGLES = 16

    def act_angles(act):
        act.wait_ge(angle, ANGLES)
        act.activation(sin_t[:, :], ang[:, 4, :], ACT.Sin).then_inc(rope_ready, 1)
        act.activation(cos_t[:, :], ang[:, 5, :], ACT.Sin).then_inc(rope_ready, 1)

    rope_ready = sem("rope_ready")

    ada_evac, gain_ready = sem("ada_evac"), count("gain_ready")
    ADA_BATCH = [(0, 16), (16, 34), (34, 48)]

    def ada_products(pe, m):
        at = at_ada[m]
        batch = [n for n, (a, b) in enumerate(ADA_BATCH) if a <= m < b][0]
        if m == 0:
            pe.wait_ge(cact_ready, 1)
        if m == ADA_BATCH[2][0]:
            pe.wait_ge(ada_evac, 1)
        pe.wait_ge(landed[at.raw_slot], landed_at(at))
        for k in range(KD):
            mm = pe.matmul(bank[ADA_BANKS[batch]][:, m:m + 1], raw[:, at.raw_slot, k * P:(k + 1) * P],
                           cact[:, k:k + 1], start=k == 0, stop=k == KD - 1)
        mm.then_inc(ada_done, 1)

    def ada_add(dve, batch):
        a, b = ADA_BATCH[batch]
        dve.wait_ge(ada_done, b)
        if batch == 0:
            dve.wait_ge(vecs_ready, 1)
        ab = col["ada_b"]
        dve.tensor_tensor(mod[:, a:b], bank[ADA_BANKS[batch]][:, a:b], vecs[:, ab + a:ab + b], ALU.add)\
           .then_inc(ada_evac, 1)
        dve.wait_ge(ada_evac, batch + 1)

    def scaled_gain(dve, name, scale):
        g0 = gain_ready.claim(1)
        dve.scalar_tensor_tensor(gain[:, :], mod[:, scale * KD:(scale + 1) * KD], 1.0,
                                 vecs[:, col[name]:col[name] + KD], ALU.add, ALU.mult).then_inc(gain_ready.sem, 1)
        dve.wait_ge(gain_ready.sem, g0 + 1)

    def mod_col(part):
        return lambda k: mod[:, part * KD + k:part * KD + k + 1]

    def from_start(eng, k):
        eng.wait_ge(x_ready.sem, k + 1)

    x_tile = lambda k: x[:, k, :]
    norm1 = Norm(x_tile, KD, from_start)
    split1 = Split(x_tile, KD, lambda k: gain[:, k:k + 1], mod_col(0), lambda k: h_hi[:, k, :],
                   lambda k: h_lo[:, k, :], lambda eng: None)
    N_PRE = 6
    prj_ready, rot_done, rope_done = sem("prj_ready"), sem("rot_done"), sem("rope_done")
    vT_done, v_ready = sem("vT_done"), sem("v_ready")
    gb_ready, conv_p, conv_done = sem("gb_ready"), sem("conv_p"), sem("conv_done")
    sc_done, s_ready, stat, e_ready = sem("sc_done"), sem("s_ready"), sem("stat"), sem("e_ready")
    probs_ready, pT_done, pT_ready, pv_done, y_ready = (sem(n) for n in (
        "probs_ready", "pT_done", "pT_ready", "pv_done", "y_ready"))
    STEPS = [(2 * jj + js, n) for jj in range(2) for n in range(NT) for js in range(2)]
    SC, PT, PV, MIX = (3, 4), 7, 5, (0, 1, 2)

    def act_ahead(act, u, kts=KD):
        split_hi(act, first[u + 2], kts)

    def pe_in(pe, u):
        if u < N_PRE:
            b = u % 2
            if u >= 2:
                pe.wait_ge(prj_ready, u - 1)
        else:
            j, part = divmod(u - N_PRE, 3)
            b = MIX[part]
            if j >= 1:
                pe.wait_ge(conv_done, j)
            elif part < 2:
                pe.wait_ge(prj_ready, N_PRE)
        unit_products(pe, at_in[u], KD, bank[b][:, :], lambda k: h_hi[:, k, :], lambda k: h_lo[:, k, :],
                      True, True, split1.pe_ready(pe) if u == 0 else None)

    def act_in(act, u):
        act_ahead(act, u)
        at = at_in[u]
        if u < N_PRE:
            bias = v("bq", u) if u < 4 else v("b_in", u - 4)
            act.wait_ge(unit_done, at.count)
            if u >= 2:
                act.wait_ge(rope_done, u - 1)
            act.activation(prj[:, u % 2, :], bank[u % 2][:, :], ACT.Identity, bias=bias).then_inc(prj_ready, 1)
        elif (u - N_PRE) % 3 == 0:
            j = (u - N_PRE) // 3
            act.wait_ge(unit_done, at.count)
            wait(act, conv_p, j - 1)
            act.activation(gb_sb[:, j % 2, :], bank[MIX[0]][:, :], ACT.Identity, bias=v("b_in", 2 + j))\
               .then_inc(gb_ready, 1)

    def dve_in(dve, u):
        split_lo(dve, first[u + 2])
        at = at_in[u]
        if u >= N_PRE and (u - N_PRE) % 3 == 2:
            j = (u - N_PRE) // 3
            dve.wait_ge(unit_done, at.count)
            dve.wait_ge(gb_ready, j + 1)
            wait(dve, conv_done, j - 1)
            if j == 0:
                dve.wait_ge(rope_done, 5)
            c, acc = cbuf[:, j % 2, :], cacc[:, j % 2, :]
            dve.scalar_tensor_tensor(c[:, 2:T + 2], bank[MIX[2]][:, :], v("b_in", 10 + j), gb_sb[:, j % 2, :],
                                     ALU.add, ALU.mult).then_inc(conv_p, 1)
            dve.wait_ge(conv_p, j + 1)
            conv_taps(dve, acc, c, lambda w: v("conv_w", 4 * w + j), conv_t, 3 * j)
            dve.scalar_tensor_tensor(y_cv[:, j, :], bank[MIX[1]][:, :], v("b_in", 6 + j), acc,
                                     ALU.add, ALU.mult).then_inc(conv_done, 1)

    conv_t = sem("conv_t")

    def conv_taps(dve, acc, c, w, sem_t, base):
        dve.tensor_scalar(acc, c[:, 0:T], w(0), None, ALU.mult).then_inc(sem_t, 1)
        dve.wait_ge(sem_t, base + 1)
        dve.scalar_tensor_tensor(acc, c[:, 1:T + 1], w(1), acc, ALU.mult, ALU.add).then_inc(sem_t, 1)
        dve.wait_ge(sem_t, base + 2)
        dve.scalar_tensor_tensor(acc, c[:, 2:T + 2], w(2), acc, ALU.mult, ALU.add).then_inc(sem_t, 1)
        dve.wait_ge(sem_t, base + 3)

    def pe_rotate(pe, u):
        pe.wait_ge(prj_ready, u + 1)
        if u == 5:
            for t in range(NT):
                tr = pe.transpose(bank[PT][:, t * P:(t + 1) * P], prj[:, 1, t * P:(t + 1) * P], ident[:, :])
            tr.then_inc(vT_done, 1)
            return
        wait(pe, rope_done, u - 1)
        pe.matmul(bank[2 + u % 2][:, :], rot[:, :], prj[:, u % 2, :], start=True, stop=True).then_inc(rot_done, 1)

    def dve_rotate(dve, u):
        dve.wait_ge(rot_done, u + 1)
        if u == 0:
            dve.wait_ge(rope_ready, 2)
        dst = q_t[:, u, :] if u < 4 else k_t[:, :]
        r0 = 2 * u
        wait(dve, rope_done, u)
        dve.tensor_tensor(tmp2[:, 0, :], prj[:, u % 2, :], cos_t[:, :], ALU.mult).then_inc(rope_step, 1)
        dve.tensor_tensor(tmp2[:, 1, :], bank[2 + u % 2][:, :], sin_t[:, :], ALU.mult).then_inc(rope_step, 1)
        dve.wait_ge(rope_step, r0 + 2)
        dve.tensor_tensor(dst, tmp2[:, 0, :], tmp2[:, 1, :], ALU.add).then_inc(rope_done, 1)

    rope_step = sem("rope_step")
    tmp2 = cacc

    def pe_scores(pe, i):
        j, n = STEPS[i]
        if i == 0:
            pe.wait_ge(rope_done, 5)
        wait(pe, s_ready, 2 * i)
        k0 = max(n - 1, 0) * P
        keys = (n + 1) * P - k0
        for h in range(2):
            r = slice(h * HD, (h + 1) * HD)
            mm = pe.matmul(bank[SC[h]][:, 2 * P - keys:2 * P], q_t[r, j, n * P:(n + 1) * P],
                           k_t[r, k0:k0 + keys], start=True, stop=True)
        mm.then_inc(sc_done, 1)

    def key_range(n):
        return slice(P if n == 0 else 0, 2 * P)

    def dve_softmax_a(dve, i):
        j, n = STEPS[i]
        kr = key_range(n)
        s, m = s_sb[:, i % 2, :, kr], st[:, i % 2, :]
        dve.wait_ge(sc_done, i + 1)
        wait(dve, e_ready, 3 * (i - 1))
        wait(dve, probs_ready, 2 * (i - 1))
        for h in range(2):
            dve.scalar_tensor_tensor(s[:, h, :], bank[SC[h]][:, kr], HD ** -0.5, mask[:, kr],
                                     ALU.mult, ALU.add).then_inc(s_ready, 1)
        dve.wait_ge(s_ready, 2 * i + 2)
        dve.tensor_reduce(m[:, 0:2], s, AX_X, ALU.max).then_inc(stat, 1)
        dve.wait_ge(stat, 4 * i + 1)
        snk = sinks[:, j:j + 5:4]
        dve.tensor_tensor(m[:, 0:2], m[:, 0:2], snk, ALU.max).then_inc(stat, 1)
        dve.wait_ge(stat, 4 * i + 2)
        dve.tensor_scalar(m[:, 2:4], m[:, 0:2], -1.0, None, ALU.mult).then_inc(stat, 1)
        dve.tensor_tensor(m[:, 4:6], snk, m[:, 0:2], ALU.subtract).then_inc(stat, 1)

    def act_exp(act, i):
        j, n = STEPS[i]
        kr = key_range(n)
        m = st[:, i % 2, :]
        act.wait_ge(stat, 4 * i + 4)
        wait(act, pT_done, i - 1)
        for h in range(2):
            act.activation(p_sb[:, i % 2, h, kr], s_sb[:, i % 2, h, kr], ACT.Exp, bias=m[:, 2 + h:3 + h],
                           accum_out=m[:, 8 + h:9 + h]).then_inc(e_ready, 1)
        act.activation(m[:, 6:8], m[:, 4:6], ACT.Exp).then_inc(e_ready, 1)

    den_step = sem("den_step")

    def dve_softmax_b(dve, i):
        j, n = STEPS[i]
        kr = key_range(n)
        m = st[:, i % 2, :]
        dve.wait_ge(e_ready, 3 * i + 3)
        dve.tensor_tensor(m[:, 10:12], m[:, 8:10], m[:, 6:8], ALU.add).then_inc(den_step, 1)
        dve.wait_ge(den_step, 2 * i + 1)
        dve.reciprocal(m[:, 8:10], m[:, 10:12]).then_inc(den_step, 1)
        dve.wait_ge(den_step, 2 * i + 2)
        for h in range(2):
            dve.tensor_scalar(p_sb[:, i % 2, h, kr], p_sb[:, i % 2, h, kr], m[:, 8 + h:9 + h], None,
                              ALU.mult).then_inc(probs_ready, 1)

    def pe_turn_probs(pe, i):
        j, n = STEPS[i]
        pe.wait_ge(probs_ready, 2 * i + 2)
        if i == 0:
            pe.wait_ge(v_ready, 1)
        wait(pe, pT_ready, i)
        for h in range(2):
            for b in range(1 if n == 0 else 0, 2):
                s = 2 * h + b
                tr = pe.transpose(bank[PT][:, s * P:(s + 1) * P], p_sb[:, i % 2, h, b * P:(b + 1) * P], ident[:, :])
        tr.then_inc(pT_done, 1)

    def act_probs(act, i):
        j, n = STEPS[i]
        act.wait_ge(pT_done, i + 1)
        wait(act, pv_done, i - 1)
        kr = key_range(n)
        act.activation(p_t[:, i % 2, :].rearrange("p (h k) -> p h k", h=2)[:, :, kr],
                       bank[PT][:, :].rearrange("p (h k) -> p h k", h=2)[:, :, kr], ACT.Copy).then_inc(pT_ready, 1)

    def pe_values(pe, i):
        j, n = STEPS[i]
        pe.wait_ge(pT_ready, i + 1)
        if i % 2 == 0:
            wait(pe, y_ready, i // 2)
        r = slice(j % 2 * HD, (j % 2 + 1) * HD)
        for h in range(2):
            for b in range(1 if n == 0 else 0, 2):
                s = 2 * h + b
                mm = pe.matmul(bank[PV][r, h * P:(h + 1) * P], v_tok[:, n - 1 + b, h * HD:(h + 1) * HD],
                               p_t[:, i % 2, s * P:(s + 1) * P], start=b == 0 or n == 0, stop=b == 1)
        mm.then_inc(pv_done, 1)

    def act_values(act, i):
        if i % 2 == 1:
            j, n = STEPS[i]
            act.wait_ge(pv_done, i + 1)
            act.activation(y_at[:, j // 2:j // 2 + 3:2, n * P:(n + 1) * P],
                           bank[PV][:, 0:2 * P].rearrange("p (h t) -> p h t", h=2), ACT.Copy).then_inc(y_ready, 1)

    def pe_mixer1(pe):
        for m in range(2 * KD):
            ada_products(pe, m)
        norm1.pe_sums(pe)
        for u in range(N_PRE):
            pe_in(pe, u)
            if u >= 1:
                pe_rotate(pe, u - 1)
            ada_products(pe, 2 * KD + u)
        pe_rotate(pe, N_PRE - 1)
        pe_scores(pe, 0)
        for i in range(len(STEPS)):
            if i < 12:
                pe_in(pe, N_PRE + i)
            if i + 1 < len(STEPS):
                pe_scores(pe, i + 1)
            pe_turn_probs(pe, i)
            if i < 12:
                ada_products(pe, 2 * KD + N_PRE + i)
            pe_values(pe, i)
        norm_cv.pe_sums(pe)
        norm_at.pe_sums(pe)
        for u in range(N_O):
            at = at_o[u]
            wait(pe, o_used, u - 1)
            if u < 2:
                pe.wait_ge(conv_done, 4)
            unit_products(pe, at, KD, bank[u % 2][:, :], lambda k: h_hi[:, k, :], lambda k: h_lo[:, k, :],
                          True, True, y_split_ready(pe) if u == 0 else None)
            m = 2 * KD + N_IN + (3 * u if u < 2 else 6 + 4 * (u - 2))
            if u < 4:
                for a in range(3 if u < 2 else 4):
                    ada_products(pe, m + a)

    def act_mixer1(act):
        split_hi(act, first[0])
        split_hi(act, first[1])
        norm1.act_squares(act)
        norm1.act_root(act)
        act_angles(act)
        split1.act(act)
        for u in range(N_PRE):
            act_in(act, u)
        act.wait_ge(vT_done, 1)
        act.activation(v_tok[:, :, :], bank[PT][:, :].rearrange("p (t c) -> p t c", t=NT), ACT.Copy)\
           .then_inc(v_ready, 1)
        act_exp(act, 0)
        for i in range(len(STEPS)):
            if i < 12:
                act_in(act, N_PRE + i)
            if i + 1 < len(STEPS):
                act_exp(act, i + 1)
            act_probs(act, i)
            act_values(act, i)
        norm_cv.act_squares(act)
        norm_cv.act_root(act)
        split_cv.act(act)
        norm_at.act_squares(act)
        norm_at.act_root(act)
        split_at.act(act)
        for u in range(N_O):
            split_hi(act, first[N_IN + u + 2])

    def dve_mixer1(dve):
        split_lo(dve, first[0])
        split_lo(dve, first[1])
        ada_add(dve, 0)
        scaled_gain(dve, "norm1", 1)
        norm1.dve_rstd(dve)
        split1.dve(dve)
        for u in range(N_PRE):
            dve_in(dve, u)
            if u >= 1:
                dve_rotate(dve, u - 1)
        dve_softmax_a(dve, 0)
        dve_softmax_b(dve, 0)
        for i in range(len(STEPS)):
            if i < 12:
                dve_in(dve, N_PRE + i)
            if i + 1 < len(STEPS):
                dve_softmax_a(dve, i + 1)
                dve_softmax_b(dve, i + 1)
        norm_cv.dve_rstd(dve)
        split_cv.dve(dve)
        norm_at.dve_rstd(dve)
        split_at.dve(dve)
        ada_add(dve, 1)
        for u in range(N_O):
            split_lo(dve, first[N_IN + u + 2])
            dve.wait_ge(unit_done, at_o[u].count)
            if u == 0:
                dve.wait_ge(ada_evac, 2)
            dve.scalar_tensor_tensor(x[:, u, :], bank[u % 2][:, :], mod[:, 2 * KD + u:2 * KD + u + 1], x[:, u, :],
                                     ALU.mult, ALU.add).then_inc(o_used, 1)
        ada_add(dve, 2)
        dve.wait_ge(ada_evac, 3)

    o_used = sem("o_used")
    norm_cv = Norm(lambda k: y_cv[:, k, :], 4, lambda eng, k: eng.wait_ge(conv_done, k + 1))
    norm_at = Norm(lambda k: y_at[:, k, :], KA, lambda eng, k: eng.wait_ge(y_ready, 2 * NT))
    h_free = lambda eng: eng.wait_ge(unit_done, N_IN)
    split_cv = Split(lambda k: y_cv[:, k, :], 4, lambda k: v("gcv", k), None, lambda k: h_hi[:, KA + k, :],
                     lambda k: h_lo[:, KA + k, :], h_free)
    split_at = Split(lambda k: y_at[:, k, :], KA, lambda k: v("ga", k), None, lambda k: h_hi[:, k, :],
                     lambda k: h_lo[:, k, :], h_free)

    def y_split_ready(pe):
        return lambda k: pe.wait_ge(h_ready.sem, split_at.h0 + k + 1) if k < KA else None

    mixer1.close()

    g_copied, taps, conv_c, s_act = (count(n) for n in ("g_copied", "taps", "conv_c", "s_act"))
    ft_ready, fhi_ready, f_ready = count("ft_ready"), count("fhi_ready"), count("f_ready")
    o_ready, x_step, x_new = count("o_ready"), count("x_step"), count("x_new")
    N_UP, N_DOWN = KF // 2, KD // 2

    class Residual:

        def __init__(self, o, gains):
            self.o, self.gains = o, gains
            self.s0, self.x0 = x_step.claim(KD), x_new.claim(KD)

        def dve(self, dve):
            for k in range(KD):
                wait(dve, x_new.sem, self.x0 + k - 2)
                dve.scalar_tensor_tensor(tmp[:, k % 3, :], self.o(k), self.gains(k), rstd[:, :],
                                         ALU.mult, ALU.mult).then_inc(x_step.sem, 1)
                if k:
                    self.add(dve, k - 1)
            self.add(dve, KD - 1)

        def add(self, dve, k):
            dve.wait_ge(x_step.sem, self.s0 + k + 1)
            dve.tensor_tensor(x[:, k, :], x[:, k, :], tmp[:, k % 3, :], ALU.add).then_inc(x_new.sem, 1)

        def ready(self, eng, k):
            eng.wait_ge(x_new.sem, self.x0 + k + 1)

    class FFN:

        def __init__(self, tag, at0, x_ready_, gains, shift, w_gate, w_up, w_down, conv, out_gains, final=False):
            self.at0, self.conv, self.final = at0, conv, final
            self.w_gate, self.w_up, self.w_down = w_gate, w_up, w_down
            self.at1 = at0.plus(2 * KF)
            self.end = self.at1.plus(2 * KD)
            mem = ExitStack()
            self.f_hi = sbs(mem, f"f_hi{tag}", [P, KF, T], F32R)
            self.f_lo = sbs(mem, f"f_lo{tag}", [P, KF, T], F32R)
            if conv:
                self.gbuf = sbs(mem, "gbuf", [P, 2, T + 2])
            with ExitStack() as part:
                h_hi = sbs(part, f"fh_hi{tag}", [P, KD, T], F32R)
                h_lo = sbs(part, f"fh_lo{tag}", [P, KD, T], F32R)
            if not conv:
                self.o = sbs(mem, f"fo{tag}", [P, KD, T])
            mem.close()
            self.h_hi, self.h_lo = h_hi, h_lo
            self.norm = Norm(x_tile, KD, x_ready_)
            self.split = Split(x_tile, KD, gains, shift, lambda k: h_hi[:, k, :], lambda k: h_lo[:, k, :],
                               lambda eng: None)
            self.c0 = {c: c.claim(n) for c, n in (
                (g_copied, KF), (taps, 2 * KF), (conv_c, KF), (s_act, KF), (ft_ready, KF), (fhi_ready, KF),
                (f_ready, KF), (o_ready, KD))}
            if not conv:
                self.norm_o = Norm(lambda k: self.o[:, k, :], KD, self.o_tile_ready)
                self.res = Residual(lambda k: self.o[:, k, :], out_gains)
                self.ready = self.res.ready
            else:
                self.ready = self.o_tile_ready
                self.out_gate = out_gains

        def o_tile_ready(self, eng, k):
            eng.wait_ge(o_ready.sem, self.c0[o_ready] + k + 1)

        def at_up(self, i, k):
            return At(self.at0.c + k, self.at0.u + k, 4, i) if not isinstance(i, int) else self.at0.plus(4 * i + k)

        def at_down(self, i, k):
            return At(self.at1.c + k, self.at1.u + k, 4, i) if not isinstance(i, int) else self.at1.plus(4 * i + k)

        def sp(self, sp):
            def up(i, last):
                for k in range(4):
                    at = self.at_up(i, k)
                    w = (self.w_gate, self.w_up)[k % 2]
                    load(sp, at, unit_parts(at, w, (0, KD), (i * 2 * P + k // 2 * P, P)),
                         (lo_ready, at.plus(-RAW).count))

            def down(i, last):
                for k in range(4):
                    at = self.at_down(i, k)
                    load(sp, at, unit_parts(at, self.w_down, (k % 2 * HALF, HALF), (i * 2 * P + k // 2 * P, P)),
                         (lo_ready, at.plus(-RAW).count))

            loop(sp, N_UP, up)
            loop(sp, N_DOWN, down)

        def pe(self, pe):
            c = self.c0
            self.norm.pe_sums(pe)

            def up(i, last):
                for q in range(2):
                    p = i * 2 + q
                    if not isinstance(i, int) or p >= 2:
                        pe.wait_ge(ft_ready.sem, p + (c[ft_ready] - 1))
                    for g in range(2):
                        ready = self.split.pe_ready(pe) if isinstance(i, int) and i + q + g == 0 else None
                        unit_products(pe, self.at_up(i, 2 * q + g), KD, bank[2 * q + g][:, :],
                                      lambda k: self.h_hi[:, k, :], lambda k: self.h_lo[:, k, :], True, True, ready)

            def down(i, last):
                for q in range(2):
                    o = i * 2 + q
                    if not isinstance(i, int) or o >= 2:
                        pe.wait_ge(o_ready.sem, o + (c[o_ready] - 1))
                    for g in range(2):
                        ready = None
                        if isinstance(i, int) and i + q == 0:
                            ready = lambda k, g=g: pe.wait_ge(f_ready.sem, c[f_ready] + g * HALF + k + 1)
                        unit_products(pe, self.at_down(i, 2 * q + g), HALF, bank[q][:, :],
                                      lambda k: self.f_hi[:, g * HALF + k, :], lambda k: self.f_lo[:, g * HALF + k, :],
                                      g == 0, g == 1, ready)

            loop(pe, N_UP, up)
            loop(pe, N_DOWN, down)
            if not self.conv:
                self.norm_o.pe_sums(pe)

        def act(self, act):
            c = self.c0
            self.norm.act_squares(act)
            self.norm.act_root(act)
            self.split.act(act)
            acc, ft = sq, tmp

            def up(i, last):
                kts = HALF if last else KD
                for q in range(2):
                    p = i * 2 + q
                    far = q == 1
                    gate, up_ = self.at_up(i, 2 * q), self.at_up(i, 2 * q + 1)
                    split_hi(act, gate.plus(2), HALF if last and far else KD)
                    if self.conv:
                        act.wait_ge(unit_done, gate.count)
                        if not isinstance(i, int) or p >= 2:
                            act.wait_ge(conv_c.sem, p + (c[conv_c] - 1))
                        act.activation(self.gbuf[:, q, 2:T + 2], bank[2 * q][:, :], ACT.Copy)\
                           .then_inc(g_copied.sem, 1)
                    split_hi(act, up_.plus(2), HALF if last and far else KD)
                    if self.conv:
                        act.wait_ge(conv_c.sem, p + (c[conv_c] + 1))
                        act.activation(acc[:, q, :], acc[:, q, :], ACT.Silu,
                                       bias=col_at(vecs, p + col["ffn_cb"])).then_inc(s_act.sem, 1)
                    else:
                        act.wait_ge(unit_done, gate.count)
                        if not isinstance(i, int) or p >= 2:
                            act.wait_ge(ft_ready.sem, p + (c[ft_ready] - 1))
                        act.activation(acc[:, q, :], bank[2 * q][:, :], ACT.Silu).then_inc(s_act.sem, 1)
                    act.wait_ge(ft_ready.sem, p + (c[ft_ready] + 1))
                    act.activation(tile_at(self.f_hi, p), ft[:, q, :], ACT.Copy).then_inc(fhi_ready.sem, 1)

            def down(i, last):
                for q in range(2):
                    for g in range(2):
                        at = self.at_down(i, 2 * q + g)
                        ends = last and q == 1
                        if not (ends and self.final):
                            split_hi(act, at.plus(2), KD if ends else HALF)
                    if not self.conv:
                        o = i * 2 + q
                        act.wait_ge(unit_done, at.count)
                        act.activation(tile_at(self.o, o), bank[q][:, :], ACT.Copy).then_inc(o_ready.sem, 1)

            loop(act, N_UP, up)
            loop(act, N_DOWN, down)
            if not self.conv:
                self.norm_o.act_squares(act)
                self.norm_o.act_root(act)

        def dve(self, dve):
            c = self.c0
            acc, ft = sq, tmp
            if self.conv:
                dve.memset(self.gbuf[:, :, 0:2], 0.0).then_inc(gpad_ready, 1)
                dve.wait_ge(gpad_ready, 1)
            self.norm.dve_rstd(dve)
            self.split.dve(dve)

            def up(i, last):
                for q in range(2):
                    p = i * 2 + q
                    later = not isinstance(i, int) or p >= 2
                    gate, up_ = self.at_up(i, 2 * q), self.at_up(i, 2 * q + 1)
                    split_lo(dve, gate.plus(2), HALF if last and q == 1 else KD)
                    if self.conv:
                        dve.wait_ge(g_copied.sem, p + (c[g_copied] + 1))
                        if later:
                            dve.wait_ge(ft_ready.sem, p + (c[ft_ready] - 1))
                        b, t0 = self.gbuf[:, q, :], p * 2 + c[taps]
                        w = lambda n: col_at(vecs, p + (col["ffn_cw"] + n * KF))
                        a = acc[:, q, :]
                        dve.tensor_scalar(a, b[:, 0:T], w(0), None, ALU.mult).then_inc(taps.sem, 1)
                        dve.wait_ge(taps.sem, t0 + 1)
                        dve.scalar_tensor_tensor(a, b[:, 1:T + 1], w(1), a, ALU.mult, ALU.add).then_inc(taps.sem, 1)
                        dve.wait_ge(taps.sem, t0 + 2)
                        dve.scalar_tensor_tensor(a, b[:, 2:T + 2], w(2), a, ALU.mult, ALU.add).then_inc(conv_c.sem, 1)
                    split_lo(dve, up_.plus(2), HALF if last and q == 1 else KD)
                    dve.wait_ge(s_act.sem, p + (c[s_act] + 1))
                    dve.wait_ge(unit_done, up_.count)
                    if later:
                        dve.wait_ge(f_ready.sem, p + (c[f_ready] - 1))
                    dve.tensor_tensor(ft[:, q, :], bank[2 * q + 1][:, :], acc[:, q, :], ALU.mult)\
                       .then_inc(ft_ready.sem, 1)
                    dve.wait_ge(fhi_ready.sem, p + (c[fhi_ready] + 1))
                    dve.tensor_tensor(tile_at(self.f_lo, p), ft[:, q, :], tile_at(self.f_hi, p).bitcast(F32),
                                      ALU.subtract).then_inc(f_ready.sem, 1)

            def down(i, last):
                for q in range(2):
                    for g in range(2):
                        at = self.at_down(i, 2 * q + g)
                        ends = last and q == 1
                        if not (ends and self.final):
                            split_lo(dve, at.plus(2), KD if ends else HALF)
                    if self.conv:
                        o = i * 2 + q
                        dve.wait_ge(unit_done, at.count)
                        dve.scalar_tensor_tensor(tile_at(x, o), bank[q][:, :], col_at(mod, o + self.out_gate),
                                                 tile_at(x, o), ALU.mult, ALU.add).then_inc(o_ready.sem, 1)

            loop(dve, N_UP, up)
            loop(dve, N_DOWN, down)
            if not self.conv:
                self.norm_o.dve_rstd(dve)
                self.res.dve(dve)

    gpad_ready = sem("gpad_ready")
    w_up0 = A["w_up"].rearrange("a k n -> (a k) n")
    ffn0 = FFN("0", At(len(seq), u_next), lambda eng, k: eng.wait_ge(o_used, k + 1),
               lambda k: gain[:, k:k + 1], mod_col(3), w_up0[:, 0:DFF], w_up0[:, DFF:2 * DFF],
               A["w_down"].rearrange("a k n -> (a k) n"), True, 5 * KD)

    norm_f = Norm(x_tile, KD, ffn0.ready)
    x_normed = sem("x_normed")

    def dve_final(dve):
        norm_f.dve_rstd(dve)
        dve.wait_ge(std_ready.sem, norm_f.std0 + 1)
        for k in range(KD):
            dve.scalar_tensor_tensor(x[:, k, :], x[:, k, :], v("final", k), rstd[:, :], ALU.mult, ALU.mult)\
               .then_inc(x_normed, 1)

    def normed(eng, k):
        eng.wait_ge(x_normed, k + 1)

    W_LORA, A_LORA, G_LORA = A["rwkv_w1_2"].shape[2], A["rwkv_a1_2"].shape[2], A["rwkv_g1_2"].shape[2]
    G_REST = G_LORA - P
    CH, NCH = 64, T // 64
    tm = ExitStack()
    rkv = sbs(tm, "rkv", [P, 3 * KD, T])
    wa_hid = sbs(tm, "wa_hid", [P, T])
    g_hid = sbs(tm, "g_hid", [P, T])
    g_hid2 = sbs(tm, "g_hid2", [G_REST, T])
    cmask = sbs(tm, "cmask", [P, T])
    bones = sbs(tm, "bones", [P, P])
    eye2 = sbs(tm, "eye2", [P, CH])
    m_strict = sbs(tm, "m_strict", [P, P])
    m_incl = sbs(tm, "m_incl", [P, P])
    m_level = sbs(tm, "m_level", [P, 6, P])
    shift_mem = ExitStack()
    hb = sbs(shift_mem, "hb", [P, KD, T + 1])
    xx = sbs(shift_mem, "xx", [P, KD, T])
    with ExitStack() as part:
        loras = sbs(part, "loras", [P, KD, W_LORA + A_LORA + G_LORA])
    xs_hi = sbs(shift_mem, "xs_hi", [P, KD, T], F32R)
    xs_lo = sbs(shift_mem, "xs_lo", [P, KD, T], F32R)
    shift_mem.close()
    w1, a1, g1 = (loras[:, :, s:s + n] for s, n in (
        (0, W_LORA), (W_LORA, A_LORA), (W_LORA + A_LORA, G_LORA)))
    assert W_LORA == A_LORA == HD

    loras_landed, h2_ready, xx_ready = sem("loras_landed"), sem("h2_ready"), sem("xx_ready")
    mixed, lora_used, hid_ready = sem("mixed"), sem("lora_used"), sem("hid_ready")
    xs_mixed, xs_hi_ready, xs_ready, rkv_ready = (sem(n) for n in ("xs_mixed", "xs_hi_ready", "xs_ready", "rkv_ready"))
    norm_tm = Norm(x_tile, KD, normed)
    LORA_MIX = (3, 4, 5)
    at_rkv0 = ffn0.end
    w_rkv = A["rwkv_w_rkv_2"].rearrange("a c k n -> (a c k) n")

    def at_rkv(p, o):
        return at_rkv0.plus(8 * p + o) if isinstance(p, int) else At(at_rkv0.c + o, at_rkv0.u + o, KD, p)

    def over_projections(eng, body):
        body(0)
        with eng.Fori(1, 3) as p:
            body(p)

    def sp_time_mix(sp):
        def body(p, outs=range(KD)):
            for o in outs:
                at = at_rkv(p, o)
                if isinstance(p, int):
                    src = w_rkv[p * D:(p + 1) * D, o * P:(o + 1) * P].rearrange("(k p) n -> p k n", p=P)
                else:
                    src = w_rkv[bass.ds(p * D, D), o * P:(o + 1) * P].rearrange("(k p) n -> p k n", p=P)
                load(sp, at, [(raw[:, at.raw_slot, 0:KD * P].rearrange("p (k n) -> p k n", n=P), src)],
                     (lo_ready, at.plus(-RAW).count))

        body(0, range(RAW))
        sp.wait_ge(f_ready.sem, ffn0.c0[f_ready] + KF)
        sp.wait_ge(unit_done, ffn0.end.u)
        for src, dst in ((A["rwkv_w1_2"], w1), (A["rwkv_a1_2"], a1), (A["rwkv_g1_2"], g1)):
            sp.dma_start(dst, src.rearrange("a (k p) n -> p (a k) n", p=P)).then_inc(loras_landed, 16)
        body(0, range(RAW, KD))
        with sp.Fori(1, 3) as p:
            body(p)

    def dve_time_mix(dve):
        dve.memset(hb[:, :, 0:1], 0.0).then_inc(h2_ready, 1)
        norm_tm.dve_rstd(dve)
        for k in range(KD):
            dve.scalar_tensor_tensor(hb[:, k, 1:T + 1], x[:, k, :], v("gains", k), rstd[:, :], ALU.mult, ALU.mult)\
               .then_inc(h2_ready, 1)
            dve.wait_ge(h2_ready, k + 2)
            dve.tensor_tensor(xx[:, k, :], hb[:, k, 0:T], hb[:, k, 1:T + 1], ALU.subtract).then_inc(xx_ready, 1)
        for n, m in enumerate(LORA_MIX):
            for k in range(KD):
                s = n * KD + k
                dve.wait_ge(xx_ready, min(KD, s + 1))
                wait(dve, lora_used, s - 2)
                dve.scalar_tensor_tensor(tmp[:, s % 3, :], xx[:, k, :], v("mix", m * KD + k), hb[:, k, 1:T + 1],
                                         ALU.mult, ALU.add).then_inc(mixed, 1)

        def body(p):
            def lower(k):
                dve.wait_ge(xs_hi_ready, p * KD + (k + 1))
                dve.tensor_tensor(xs_lo[:, k, :], tmp[:, k % 2, :], xs_hi[:, k, :].bitcast(F32), ALU.subtract)\
                   .then_inc(xs_ready, 1)

            if isinstance(p, int):
                dve.wait_ge(lora_used, 3 * KD)
            dve.wait_ge(unit_done, at_rkv(p, 0).plus(-1).count)
            for k in range(KD):
                if not isinstance(p, int) or k >= 2:
                    dve.wait_ge(xs_ready, p * KD + (k - 1))
                dve.scalar_tensor_tensor(tmp[:, k % 2, :], xx[:, k, :], col_at(vecs, p * KD + (col["mix"] + k)),
                                         hb[:, k, 1:T + 1], ALU.mult, ALU.add).then_inc(xs_mixed, 1)
                if k:
                    dve.wait_ge(xs_mixed, p * KD + k)
                    lower(k - 1)
            dve.wait_ge(xs_mixed, p * KD + KD)
            lower(KD - 1)
            for o in range(KD):
                split_lo(dve, at_rkv(p, o).plus(2))

        over_projections(dve, body)

    def act_time_mix(act):
        norm_tm.act_squares(act)
        norm_tm.act_root(act)
        act.wait_ge(lora_used, KD)
        act.activation(wa_hid[0:HD, :], bank[0][0:HD, :], ACT.Tanh).then_inc(hid_ready, 1)
        act.wait_ge(lora_used, 2 * KD)
        act.activation(wa_hid[HD:P, :], bank[1][HD:P, :], ACT.Copy).then_inc(hid_ready, 1)
        act.wait_ge(lora_used, 3 * KD)
        act.activation(g_hid[:, :], bank[2][:, :], ACT.Sigmoid).then_inc(hid_ready, 1)
        act.activation(g_hid2[:, :], bank[3][0:G_REST, :], ACT.Sigmoid).then_inc(hid_ready, 1)

        def body(p):
            act.wait_ge(unit_done, at_rkv(p, 0).plus(-1).count)
            for k in range(KD):
                act.wait_ge(xs_mixed, p * KD + (k + 1))
                act.activation(xs_hi[:, k, :], tmp[:, k % 2, :], ACT.Copy).then_inc(xs_hi_ready, 1)
            for o in range(KD):
                split_hi(act, at_rkv(p, o).plus(2))
                act.wait_ge(unit_done, at_rkv(p, o).count)
                act.activation(tile_at(rkv, p * KD + o), bank[4 + o % 2][:, :], ACT.Copy).then_inc(rkv_ready, 1)

        over_projections(act, body)

    def pe_time_mix(pe):
        norm_tm.pe_sums(pe)
        pe.wait_ge(loras_landed, 48)
        for n, parts in enumerate((((bank[0][0:W_LORA, :], w1),), ((bank[1][HD:P, :], a1),),
                                   ((bank[2][:, :], g1[:, :, 0:P]), (bank[3][0:G_REST, :], g1[:, :, P:G_LORA])))):
            for k in range(KD):
                s = n * KD + k
                pe.wait_ge(mixed, s + 1)
                for dst, w in parts:
                    mm = pe.matmul(dst, w[:, k, :], tmp[:, s % 3, :], start=k == 0, stop=k == KD - 1)
                mm.then_inc(lora_used, 1)

        def body(p):
            for o in range(KD):
                at = at_rkv(p, o)
                if not isinstance(p, int) or o >= 2:
                    pe.wait_ge(rkv_ready, p * KD + (o - 1))
                unit_products(pe, at, KD, bank[4 + o % 2][:, :], lambda k: xs_hi[:, k, :], lambda k: xs_lo[:, k, :],
                              True, True, (lambda k: pe.wait_ge(xs_ready, p * KD + (k + 1))) if o == 0 else None)

        over_projections(pe, body)

    GN_EPS = 64e-5
    DECAY = -float(np.exp(-0.5))
    LEVELS = (2, 4, 8, 16, 32)
    bm = ExitStack()
    lw = sbs(bm, "lw", [P, 3, P])
    v_c = sbs(bm, "v_c", [P, T])
    L_t = sbs(bm, "L_t", [P, T])
    E_t = sbs(bm, "E_t", [P, T])
    bonus = sbs(bm, "bonus", [P, T])
    AR = sbs(bm, "AR", [P, NT, 2, P])
    B_t = sbs(bm, "B_t", [P, T])
    K_t = sbs(bm, "K_t", [P, T])
    AU = sbs(bm, "AU", [P, NT, 2, P])
    B_k = sbs(bm, "B_k", [P, NT, P])
    K_k = sbs(bm, "K_k", [P, NT, P])
    V_k = sbs(bm, "V_k", [P, NT, P])
    MT = sbs(bm, "MT", [P, 2, NT, P])
    MTb = sbs(bm, "MTb", [P, 2, NT, P])
    XT = sbs(bm, "XT", [P, 2, NT, P])
    X = sbs(bm, "X", [P, 2, NT, P])
    Z = sbs(bm, "Z", [P, 2, NT, P])
    RB = sbs(bm, "RB", [P, 2, NT, P])
    AK = sbs(bm, "AK", [P, 2, NT, P])
    RK = sbs(bm, "RK", [P, 2, NT, P])
    XAU = Z
    GT = sbs(bm, "GT", [P, NCH, 2, CH])
    HP = sbs(bm, "HP", [P, NCH, CH])
    RH = sbs(bm, "RH", [P, T])
    S = sbs(bm, "S", [P, NCH, CH])
    bm.close()

    class Steps:

        def __init__(self, sem_name, names):
            self.sem, self.names = sem(sem_name), names.split()
            assert len(set(self.names)) == len(self.names)

        def done(self, ins, name):
            ins.then_inc(self.sem, 1)
            assert name == self.names[self.seen % len(self.names)], (name, self.names[self.seen % len(self.names)])
            self.seen += 1

        seen = 0

        def wait(self, eng, j, name, before=0):
            n = self.names.index(name) + 1 - before * len(self.names)
            if isinstance(j, int) and j < before:
                return
            eng.wait_ge(self.sem, j * len(self.names) + n)

    both = lambda s: " ".join(f"{s}{e}" for e in range(2))
    masks_ready, sp_step = sem("masks_ready"), sem("sp_step")
    PEs = Steps("pe_step", "lora kk_sum bonus_sum tA tB tK tV " + " ".join(f"m{n}" for n in range(8)) + " x0 x1 "
                + " ".join(f"z{b}_0 z{b}_1 xt{b}_0 xt{b}_1" + ("" if b == 32 else f" x{b}_0 x{b}_1") for b in LEVELS)
                + " u0 u1 xau0 xau1 gh rh " + " ".join(f"s{c}" for c in range(1, NCH - 1)) + " y mean var g")
    ACTs = Steps("act_step", "sg a kk2 root eE eN eL ktB ktV " + " x0 x1 "
                 + " ".join(f"z{b}_0 z{b}_1" + ("" if b == 32 else f" x{b}_0 x{b}_1") for b in LEVELS)
                 + " u0 u1 xau0 xau1 y d2 groot")
    DVEs = Steps("dve_step", "kk ss rn kkn scan E u kp bon AT t2 BT KT RT bonus tA tK "
                 + " ".join(f"e{n}a e{n}b" for n in range(8)) + " xt0 xt1 "
                 + " ".join(f"xt{b}_0 xt{b}_1" for b in LEVELS)
                 + " gt00 gt01 gt10 gt11 hp0 hp1 rh0 rh1 S1 " + " ".join(f"S{c}" for c in range(2, NCH)) + " d gvar grstd yn yb y")
    POOLs = Steps("pool_step", "v " + " ".join(f"m{b}_0 m{b}_1" for b in LEVELS))
    sg, a_, kk = tmp[:, 0, :], tmp[:, 1, :], tmp[:, 2, :]
    kk2, eN = sq[:, 0, :], sq[:, 1, :]
    root, kp = var[:, :], rstd[:, :]
    w2, a2, g2 = (A[n].rearrange("a k n -> (a k) n") for n in ("rwkv_w2_2", "rwkv_a2_2", "rwkv_g2_2"))
    LW_FIRST, LW_ALL = 2, 4

    def pool_masks(pool):
        pool.wait_ge(unit_done, ffn0.end.u)
        n = [0]

        def step(ins):
            ins.then_inc(masks_ready, 1)
            n[0] += 1
            pool.wait_ge(masks_ready, n[0])

        step(pool.memset(cmask[:, :], 1.0))
        step(pool.memset(cmask[:, :].rearrange("p (c t) -> p c t", t=CH)[:, :, 0:1], 0.0))
        step(pool.memset(bones[:, :], 0.0))
        step(pool.memset(bones[0:HD, 0:HD], 1.0))
        step(pool.memset(bones[HD:P, HD:P], 1.0))
        step(pool.tensor_copy(eye2[0:HD, :], ident[0:HD, 0:HD]))
        step(pool.tensor_copy(eye2[HD:P, :], ident[HD:P, HD:P]))
        step(pool.affine_select(out=m_strict[:, :], in_=bones[:, :], compare_op=ALU.is_gt, fill=0.0, base=0,
                                pattern=[[1, P]], channel_multiplier=-1))
        step(pool.affine_select(out=m_incl[:, :], in_=bones[:, :], compare_op=ALU.is_ge, fill=0.0, base=0,
                                pattern=[[1, P]], channel_multiplier=-1))
        for n_, b in enumerate((1,) + LEVELS):
            m = m_level[:, n_, :].rearrange("p (g h t) -> p g h t", h=2, t=b)
            step(pool.memset(m_level[:, n_, :], 0.0))
            step(pool.memset(m[:, :, 1, :], 1.0))
            step(pool.affine_select(out=m[:, :, 1, :], in_=m[:, :, 1, :], compare_op=ALU.is_ge, fill=0.0, base=0,
                                    pattern=[[-2 * b, P // (2 * b)], [0, b]], channel_multiplier=1))
            step(pool.affine_select(out=m[:, :, 1, :], in_=m[:, :, 1, :], compare_op=ALU.is_ge, fill=0.0, base=b - 1,
                                    pattern=[[2 * b, P // (2 * b)], [0, b]], channel_multiplier=-1))

    MASKS = 9 + 4 * 6

    def over_tiles(eng, body):
        body(0)
        with eng.Fori(1, KD) as j:
            body(j)

    def r_k_v(j):
        return tile_at(rkv, j), tile_at(rkv, j + KD), tile_at(rkv, j + 2 * KD)

    def sp_blocks(sp):
        def body(j):
            if not isinstance(j, int):
                PEs.wait(sp, j, "g", before=1)
            else:
                sp.wait_ge(unit_done, at_rkv(2, KD - 1).count)
            for n, (w, r0, r1) in enumerate(((w2, 0, HD), (a2, 0, HD), (g2, 0, P), (g2, P, G_LORA))):
                dst = (lw[0:HD, 0, :], lw[HD:P, 0, :], lw[:, 1, :], lw[0:G_REST, 2, :])[n]
                sp.dma_start(dst, cols_at(w[r0:r1, :], j * P, P)).then_inc(sp_step, 16)

        over_tiles(sp, body)

    def pool_blocks(pool):
        pool.wait_ge(unit_done, at_rkv(2, KD - 1).count)

        def body(j):
            if isinstance(j, int):
                pool.wait_ge(rkv_ready, 3 * KD)
            PEs.wait(pool, j, "tV", before=1)
            POOLs.done(pool.tensor_copy(v_c[:, :], r_k_v(j)[2]), "v")
            for n, b in enumerate(LEVELS):
                for e in range(2):
                    if n == 0:
                        DVEs.wait(pool, j, "e7b")
                        PEs.wait(pool, j, f"z32_{e}", before=1)
                    else:
                        PEs.wait(pool, j, f"z{LEVELS[n - 1]}_{e}")
                    POOLs.done(pool.tensor_tensor(MTb[:, e, :, :], MT[:, e, :, :],
                                                  m_level[:, n + 1:n + 2, :].to_broadcast([P, NT, P]), ALU.mult),
                               f"m{b}_{e}")

        over_tiles(pool, body)

    def act_blocks(act):
        def body(j):
            def do(out, in_, func, name, **kw):
                ACTs.done(act.activation(out, in_, func, **kw), name)

            DVEs.wait(act, j, "y", before=1)
            PEs.wait(act, j, "lora")
            do(sg, bank[0][:, :], ACT.Sigmoid, "sg", bias=col_at(vecs, j + col["w0"]))
            do(a_, bank[1][:, :], ACT.Sigmoid, "a", bias=col_at(vecs, j + col["a0"]))
            DVEs.wait(act, j, "kk")
            do(kk2, kk, ACT.Square, "kk2")
            DVEs.wait(act, j, "ss")
            do(root, root, ACT.Sqrt, "root")
            DVEs.wait(act, j, "E")
            do(E_t[:, :], E_t[:, :], ACT.Exp, "eE", scale=DECAY)
            do(eN, L_t[:, :], ACT.Exp, "eN", scale=-DECAY)
            ACTs.wait(act, j, "eN")
            do(L_t[:, :], L_t[:, :], ACT.Exp, "eL", scale=DECAY)
            PEs.wait(act, j, "tB")
            do(B_k[:, :, :], bank[5][:, :].rearrange("p (t c) -> p t c", t=NT), ACT.Copy, "ktB")
            PEs.wait(act, j, "tV")
            do(V_k[:, :, :], bank[7][:, :].rearrange("p (t c) -> p t c", t=NT), ACT.Copy, "ktV")
            as4 = lambda b: bank[b][:, :].rearrange("p (t c) -> p t c", t=NT)
            for e in range(2):
                PEs.wait(act, j, f"x{e}")
                do(X[:, e, :, :], as4(4 + e), ACT.Copy, f"x{e}")
            for b in LEVELS:
                for e in range(2):
                    PEs.wait(act, j, f"z{b}_{e}")
                    do(Z[:, e, :, :], as4(e), ACT.Copy, f"z{b}_{e}")
                if b != 32:
                    for e in range(2):
                        PEs.wait(act, j, f"x{b}_{e}")
                        do(X[:, e, :, :], as4(4 + e), ACT.Copy, f"x{b}_{e}")
            for e in range(2):
                PEs.wait(act, j, f"u{e}")
                do(AU[:, :, e, CH:P], bank[4 + e][:, 0:NT * CH].rearrange("p (t c) -> p t c", t=NT), ACT.Copy, f"u{e}")
            for e in range(2):
                PEs.wait(act, j, f"xau{e}")
                do(XAU[:, e, :, :], as4(e), ACT.Copy, f"xau{e}")
            PEs.wait(act, j, "y")
            do(sg, bank[6][:, :], ACT.Copy, "y")
            DVEs.wait(act, j, "d")
            do(kk2, a_, ACT.Square, "d2")
            DVEs.wait(act, j, "gvar")
            do(root, root, ACT.Sqrt, "groot")

        over_tiles(act, body)

    def dve_blocks(dve):
        dve.wait_ge(masks_ready, MASKS)
        dve.wait_ge(unit_done, at_rkv(2, KD - 1).count)
        dve.memset(GT[:, :, :, :], 0.0).then_inc(lvl1, 1)
        dve.wait_ge(lvl1, 1)

        def body(j):
            r, k, vv = r_k_v(j)
            vc = lambda name: col_at(vecs, j + col[name])

            def tt(out, a, b, op, name):
                DVEs.done(dve.tensor_tensor(out, a, b, op), name)

            def stt(out, a, s, b, op0, op1, name):
                DVEs.done(dve.scalar_tensor_tensor(out, a, s, b, op0, op1), name)

            own = lambda name: DVEs.wait(dve, j, name)
            DVEs.wait(dve, j, "y", before=1)
            if isinstance(j, int):
                dve.wait_ge(rkv_ready, 3 * KD)
            DVEs.done(dve.tensor_scalar(kk, k, vc("k_k"), None, ALU.mult), "kk")
            PEs.wait(dve, j, "kk_sum")
            DVEs.done(dve.tensor_scalar(root, bank[2][:, :], 1e-24, None, ALU.max), "ss")
            ACTs.wait(dve, j, "root")
            DVEs.done(dve.reciprocal(kp, root), "rn")
            own("rn")
            tt(kk, kk, kp, ALU.mult, "kkn")
            ACTs.wait(dve, j, "a")
            DVEs.done(dve.tensor_tensor_scan(L_t[:, :], cmask[:, :], sg, 0.0, ALU.mult, ALU.add), "scan")
            own("scan")
            tt(E_t[:, :], L_t[:, :], sg, ALU.subtract, "E")
            DVEs.done(dve.tensor_scalar(root, a_, 1.0, vc("k_a"), ALU.subtract, ALU.mult), "u")
            own("u")
            stt(kp, root, 1.0, k, ALU.add, ALU.mult, "kp")
            own("kp")
            PEs.wait(dve, j, "kk_sum")
            stt(kk2, r, vc("r_k"), kp, ALU.mult, ALU.mult, "bon")
            ACTs.wait(dve, j, "eE")
            stt(AR[:, :, 0, :], kk.rearrange("p (t c) -> p t c", t=NT), -1.0,
                E_t[:, :].rearrange("p (t c) -> p t c", t=NT), ALU.mult, ALU.mult, "AT")
            own("E")
            tt(sg, kk, a_, ALU.mult, "t2")
            own("t2")
            ACTs.wait(dve, j, "eN")
            tt(B_t[:, :], sg, eN, ALU.mult, "BT")
            tt(K_t[:, :], kp, eN, ALU.mult, "KT")
            ACTs.wait(dve, j, "eL")
            tt(AR[:, :, 1, :], r.rearrange("p (t c) -> p t c", t=NT),
               L_t[:, :].rearrange("p (t c) -> p t c", t=NT), ALU.mult, "RT")
            PEs.wait(dve, j, "bonus_sum")
            tt(bonus[:, :], bank[3][:, :], vv, ALU.mult, "bonus")
            PEs.wait(dve, j, "tA")
            DVEs.done(dve.tensor_copy(AU[:, :, :, 0:CH], bank[4][:, :].rearrange("p (t e c) -> p t e c", t=NT, e=2)), "tA")
            PEs.wait(dve, j, "tK")
            DVEs.done(dve.tensor_copy(K_k[:, :, :], bank[6][:, :].rearrange("p (t c) -> p t c", t=NT)), "tK")
            for n in range(8):
                of_b, e, pair = n < 4, n // 2 % 2, n % 2
                PEs.wait(dve, j, f"m{n}")
                two = bank[n][:, :].rearrange("p (t h c) -> p t h c", t=2, h=2)
                ts = slice(2 * pair, 2 * pair + 2)
                strict = m_strict[:, :].rearrange("p (o c) -> p o c", o=1).to_broadcast([P, 2, P])
                incl = m_incl[:, :].rearrange("p (o c) -> p o c", o=1).to_broadcast([P, 2, P])
                tt((MT if of_b else AK)[:, e, ts, :], two[:, :, 0, :], strict, ALU.mult, f"e{n}a")
                tt((RB if of_b else RK)[:, e, ts, :], two[:, :, 1, :], incl, ALU.mult, f"e{n}b")
            m1 = m_level[:, 0:1, :].to_broadcast([P, NT, P])
            idb = ident[:, :].rearrange("p (o c) -> p o c", o=1).to_broadcast([P, NT, P])
            own("e7b")
            for e in range(2):
                dve.tensor_tensor(XT[:, e, :, :], MT[:, e, :, :], m1, ALU.mult).then_inc(lvl1, 1)
            for e in range(2):
                dve.wait_ge(lvl1, j * 2 + (e + 2))
                tt(XT[:, e, :, :], XT[:, e, :, :], idb, ALU.add, f"xt{e}")
            as4 = lambda b: bank[b][:, :].rearrange("p (t c) -> p t c", t=NT)
            for b in LEVELS:
                for e in range(2):
                    PEs.wait(dve, j, f"xt{b}_{e}")
                    tt(XT[:, e, :, :], as4(2 + e), XT[:, e, :, :], ALU.add, f"xt{b}_{e}")
            half = lambda t_, p_: t_[:, :, :].rearrange("q (t p) c -> q t p c", p=2)[:, :, p_, :]
            PEs.wait(dve, j, "gh")
            for p_ in range(2):
                for e in range(2):
                    q = slice(e * HD, (e + 1) * HD)
                    eye = eye2[q, :].rearrange("p (o c) -> p o c", o=1).to_broadcast([HD, NT, CH])
                    tt(GT[q, :, e, :].rearrange("q (t p) c -> q t p c", p=2)[:, :, p_, :],
                       bank[p_][q, 0:NT * CH].rearrange("q (t c) -> q t c", t=NT), eye, ALU.add, f"gt{p_}{e}")
            for p_ in range(2):
                ends = L_t[:, :].rearrange("q (t p c) -> q t p c", t=NT, p=2)[:, :, p_, CH - 1:CH]
                tt(half(HP, p_), bank[p_][:, NT * CH:].rearrange("q (t c) -> q t c", t=NT),
                   ends.to_broadcast([P, NT, CH]), ALU.mult, f"hp{p_}")
            PEs.wait(dve, j, "rh")
            for p_ in range(2):
                cols = slice(p_ * CH, (p_ + 1) * CH)
                tt(RH[:, :].rearrange("q (t c) -> q t c", t=NT)[:, :, cols],
                   bank[2 + p_][:, 0:NT * CH].rearrange("q (t c) -> q t c", t=NT), AR[:, :, 1, cols], ALU.add, f"rh{p_}")
            own("hp0")
            DVEs.done(dve.tensor_copy(S[:, 1, :], HP[:, 0, :]), "S1")
            own("hp1")
            for c in range(1, NCH - 1):
                PEs.wait(dve, j, f"s{c}")
                end = c * CH + CH - 1
                stt(S[:, c + 1, :], bank[7][:, 0:CH], L_t[:, end:end + 1], HP[:, c, :], ALU.mult, ALU.add, f"S{c + 1}")
            PEs.wait(dve, j, "mean")
            stt(a_, bank[0][:, :], -1.0 / HD, sg, ALU.mult, ALU.add, "d")
            PEs.wait(dve, j, "var")
            DVEs.done(dve.tensor_scalar(root, bank[1][:, :], 1.0 / HD, GN_EPS, ALU.mult, ALU.add), "gvar")
            ACTs.wait(dve, j, "groot")
            DVEs.done(dve.reciprocal(kp, root), "grstd")
            own("grstd")
            stt(kk, a_, vc("gn_w"), kp, ALU.mult, ALU.mult, "yn")
            own("yn")
            stt(sg, kk, vc("gn_b"), bonus[:, :], ALU.add, ALU.add, "yb")
            own("yb")
            PEs.wait(dve, j, "g")
            tt(r, sg, bank[2][:, :], ALU.mult, "y")

        over_tiles(dve, body)

    lvl1 = sem("lvl1")

    def pe_blocks(pe):
        pe.wait_ge(masks_ready, MASKS)

        def body(j):
            r, k, vv = r_k_v(j)
            mm = pe.matmul
            hr = [slice(0, HD), slice(HD, P)]
            ACTs.wait(pe, j, "groot", before=1)
            DVEs.wait(pe, j, "y", before=1)
            if isinstance(j, int):
                pe.wait_ge(hid_ready, 4)
            pe.wait_ge(sp_step, j * 64 + 64)
            mm(bank[0][:, :], lw[0:HD, 0, :], wa_hid[0:HD, :], start=True, stop=True)
            PEs.done(mm(bank[1][:, :], lw[HD:P, 0, :], wa_hid[HD:P, :], start=True, stop=True), "lora")
            ACTs.wait(pe, j, "kk2")
            PEs.done(mm(bank[2][:, :], bones[:, :], kk2, start=True, stop=True), "kk_sum")
            DVEs.wait(pe, j, "bon")
            PEs.done(mm(bank[3][:, :], bones[:, :], kk2, start=True, stop=True), "bonus_sum")

            def turn(b, src, name):
                for t in range(NT):
                    tr = pe.transpose(bank[b][:, t * P:(t + 1) * P], src(t), ident[:, :])
                PEs.done(tr, name)

            DVEs.wait(pe, j, "AT")
            turn(4, lambda t: AR[:, t, 0, :], "tA")
            DVEs.wait(pe, j, "BT")
            turn(5, lambda t: B_t[:, t * P:(t + 1) * P], "tB")
            DVEs.wait(pe, j, "KT")
            turn(6, lambda t: K_t[:, t * P:(t + 1) * P], "tK")
            POOLs.wait(pe, j, "v")
            turn(7, lambda t: v_c[:, t * P:(t + 1) * P], "tV")
            DVEs.wait(pe, j, "bonus")
            for n in range(8):
                of_b, e, pair = n < 4, n // 2 % 2, n % 2
                if n == 4:
                    DVEs.wait(pe, j, "tK")
                    ACTs.wait(pe, j, "ktV")
                for t in range(2 * pair, 2 * pair + 2):
                    lhs = (B_t if of_b else K_t)[hr[e], t * P:(t + 1) * P]
                    m = mm(bank[n][:, (t % 2) * 2 * P:(t % 2 + 1) * 2 * P], lhs,
                           AR[hr[e], t, :, :].rearrange("p h c -> p (h c)"), start=True, stop=True)
                PEs.done(m, f"m{n}")
            for e in range(2):
                DVEs.wait(pe, j, f"xt{e}")
                turn(4 + e, lambda t: XT[:, e, t, :], f"x{e}")
            for b in LEVELS:
                for e in range(2):
                    POOLs.wait(pe, j, f"m{b}_{e}")
                    ACTs.wait(pe, j, f"x{e}" if b == 2 else f"x{b // 2}_{e}")
                    for t in range(NT):
                        m = mm(bank[e][:, t * P:(t + 1) * P], MTb[:, e, t, :], X[:, e, t, :], start=True, stop=True)
                    PEs.done(m, f"z{b}_{e}")
                for e in range(2):
                    ACTs.wait(pe, j, f"z{b}_{e}")
                    for t in range(NT):
                        m = mm(bank[2 + e][:, t * P:(t + 1) * P], Z[:, e, t, :], XT[:, e, t, :], start=True, stop=True)
                    PEs.done(m, f"xt{b}_{e}")
                if b != 32:
                    for e in range(2):
                        DVEs.wait(pe, j, f"xt{b}_{e}")
                        turn(4 + e, lambda t: XT[:, e, t, :], f"x{b}_{e}")
            for e in range(2):
                for t in range(NT):
                    m = mm(bank[4 + e][:, t * CH:(t + 1) * CH], AK[:, e, t, :], V_k[:, t, hr[e]], start=True, stop=True)
                PEs.done(m, f"u{e}")
            for e in range(2):
                DVEs.wait(pe, j, f"xt32_{e}")
                ACTs.wait(pe, j, f"u{e}")
                for t in range(NT):
                    m = mm(bank[e][:, t * P:(t + 1) * P], XT[:, e, t, :], AU[:, t, e, :], start=True, stop=True)
                PEs.done(m, f"xau{e}")
            def local(e, t):
                cs = slice(t * P, (t + 1) * P)
                mm(bank[6][hr[e], cs], XAU[:, e, t, CH:P], RB[:, e, t, :], start=t == 0, stop=False,
                   skip_group_check=True)
                mm(bank[6][hr[e], cs], V_k[:, t, hr[e]], RK[:, e, t, :], start=False, stop=False,
                   skip_group_check=True)

            ACTs.wait(pe, j, "xau1")
            local(0, 0)
            local(1, 0)
            for out in ("gh", "rh"):
                for e in range(2):
                    for t in range(NT):
                        for p_ in range(2):
                            q, cs = hr[p_], slice(t * CH, (t + 1) * CH)
                            if out == "gh":
                                xa, xu = XAU[q, e, t, 0:CH], XAU[q, e, t, CH:P]
                                mm(bank[p_][hr[e], cs], xa, B_k[q, t, hr[e]], start=True, stop=True)
                                hs = slice(NT * CH + t * CH, NT * CH + (t + 1) * CH)
                                mm(bank[p_][hr[e], hs], B_k[q, t, hr[e]], xu, start=True, stop=False)
                                m = mm(bank[p_][hr[e], hs], K_k[q, t, hr[e]], V_k[q, t, hr[e]], start=False, stop=True)
                            else:
                                m = mm(bank[2 + p_][hr[e], cs], XAU[q, e, t, 0:CH], RB[q, e, t, hr[p_]],
                                       start=True, stop=True)
                PEs.done(m, out)

            for c in range(1, NCH):
                DVEs.wait(pe, j, f"S{c}")
                if c == 1:
                    DVEs.wait(pe, j, "rh1")
                if c < NCH - 1:
                    PEs.done(mm(bank[7][:, 0:CH], GT[:, c, :, :].rearrange("p e c -> p (e c)"), S[:, c, :],
                                start=True, stop=True), f"s{c}")
                if c % 2 == 1 and c > 1:
                    local(0, c // 2)
                    local(1, c // 2)
                for e in range(2):
                    m = mm(bank[6][hr[e], c * CH:(c + 1) * CH], S[hr[e], c, :], RH[hr[e], c * CH:(c + 1) * CH],
                           start=False, stop=c == NCH - 1, skip_group_check=True)
            PEs.done(m, "y")
            ACTs.wait(pe, j, "y")
            PEs.done(mm(bank[0][:, :], bones[:, :], sg, start=True, stop=True), "mean")
            ACTs.wait(pe, j, "d2")
            PEs.done(mm(bank[1][:, :], bones[:, :], kk2, start=True, stop=True), "var")
            mm(bank[2][:, :], lw[:, 1, :], g_hid[:, :], start=True, stop=False)
            PEs.done(mm(bank[2][:, :], lw[0:G_REST, 2, :], g_hid2[:, :], start=False, stop=True), "g")

        over_tiles(pe, body)

    ys_hi_ready, ys_ready = count("ys_hi_ready"), count("ys_ready")

    class Project:

        def __init__(self, mem, tag, at0, w, hi, lo, y_split, gains):
            self.at0, self.w, self.hi, self.lo, self.y_split = at0, w, hi, lo, y_split
            self.end = at0.plus(KD)
            self.o = sbs(mem, f"po{tag}", [P, KD, T])
            self.o0 = o_ready.claim(KD)
            self.norm_o = Norm(lambda k: self.o[:, k, :], KD, lambda eng, k: eng.wait_ge(o_ready.sem, self.o0 + k + 1))
            self.res = Residual(lambda k: self.o[:, k, :], gains)
            self.ready = self.res.ready

        def sp(self, sp, outs=range(KD)):
            for o in outs:
                at = self.at0.plus(o)
                load(sp, at, unit_parts(at, self.w, (0, KD), (o * P, P)), (lo_ready, at.plus(-RAW).count))

        def act(self, act):
            for o in range(KD):
                at = self.at0.plus(o)
                split_hi(act, at.plus(2))
                act.wait_ge(unit_done, at.count)
                act.activation(self.o[:, o, :], bank[o % 2][:, :], ACT.Copy).then_inc(o_ready.sem, 1)
            self.norm_o.act_squares(act)
            self.norm_o.act_root(act)

        def dve(self, dve):
            for o in range(KD):
                split_lo(dve, self.at0.plus(o + 2))
            self.norm_o.dve_rstd(dve)
            self.res.dve(dve)

        def pe(self, pe):
            for o in range(KD):
                wait(pe, o_ready.sem, self.o0 + o - 1)
                unit_products(pe, self.at0.plus(o), KD, bank[o % 2][:, :], lambda k: self.hi[:, k, :],
                              lambda k: self.lo[:, k, :], True, True,
                              (lambda k: self.y_split(pe, k)) if o == 0 else None)
            self.norm_o.pe_sums(pe)

    gains_of = lambda n: (lambda k: v("gains", n * KD + k))
    ys_hi = sbs(tm, "ys_hi", [P, KD, T], F32R)
    ys_lo = sbs(tm, "ys_lo", [P, KD, T], F32R)
    y0, yhi0 = ys_ready.claim(KD), ys_hi_ready.claim(KD)
    out_tm = Project(tm, "1", at_rkv0.plus(3 * KD), A["rwkv_w_o_2"].rearrange("a k n -> (a k) n"), ys_hi, ys_lo,
                     lambda eng, k: eng.wait_ge(ys_ready.sem, y0 + k + 1), gains_of(1))
    tm.close()

    def act_split_y(act):
        DVEs.wait(act, KD - 1, "y")
        PEs.wait(act, KD - 1, "g")
        for k in range(KD):
            act.activation(ys_hi[:, k, :], rkv[:, k, :], ACT.Copy).then_inc(ys_hi_ready.sem, 1)

    def dve_split_y(dve):
        DVEs.wait(dve, KD - 1, "y")
        PEs.wait(dve, KD - 1, "g")
        for k in range(KD):
            dve.wait_ge(ys_hi_ready.sem, yhi0 + k + 1)
            dve.tensor_tensor(ys_lo[:, k, :], rkv[:, k, :], ys_hi[:, k, :].bitcast(F32), ALU.subtract)\
               .then_inc(ys_ready.sem, 1)

    wg2, wu2, wd2 = A["ffn_w_gate_2"], A["ffn_w_up_2"], A["ffn_w_down_2"]
    ffn1 = FFN("1", out_tm.end, out_tm.ready, gains_of(2), None, wg2[0], wu2[0], wd2[0], False, gains_of(3))

    gu = ExitStack()
    gh_hi = sbs(gu, "gh_hi", [P, KD, T], F32R)
    gh_lo = sbs(gu, "gh_lo", [P, KD, T], F32R)
    uv = sbs(gu, "uv", [P, 2 * KD, T])
    v_tk = sbs(gu, "v_tk", [P, NT, D])
    ws_in = sbs(gu, "ws_in", [P, KD, P])
    wsT = sbs(gu, "wsT", [P, KD, P])
    bs_row = sbs(gu, "bs_row", [1, KD * P])
    bs = sbs(gu, "bs", [P, KD, P])
    LN_EPS = 1e-5
    gs_landed, wsT_done, wsT_ready, bs_done, bs_ready = (sem(n) for n in (
        "gs_landed", "wsT_done", "wsT_ready", "bs_done", "bs_ready"))
    uv_ready, mean_done, v_centred, v_scaled, vn_ready = (sem(n) for n in (
        "uv_ready", "mean_done", "v_centred", "v_scaled", "vn_ready"))
    vt_done, vt_ready, s_done, s_biased = (sem(n) for n in ("vt_done", "vt_ready", "s_done", "s_biased"))
    us_ready, us_hi, us_split = sem("us_ready"), sem("us_hi"), sem("us_split")
    norm_g = Norm(x_tile, KD, ffn1.ready)
    split_g = Split(x_tile, KD, gains_of(4), None, lambda k: gh_hi[:, k, :], lambda k: gh_lo[:, k, :], lambda eng: None)
    norm_v = Norm(lambda k: uv[:, KD + k, :], KD, lambda eng, k: eng.wait_ge(v_centred, k + 1), eps=LN_EPS)
    at_g0 = ffn1.end
    at_g = lambda i, k: at_g0.plus(4 * i + k) if isinstance(i, int) else At(at_g0.c + k, at_g0.u + k, 4, i)
    w_gu = A["sgu_w_in_2"].rearrange("a k n -> (a k) n")
    N_GU = 2 * KD // 4
    out_gu = Project(gu, "2", at_g0.plus(2 * KD), A["sgu_w_out_2"].rearrange("a k n -> (a k) n"), gh_hi, gh_lo,
                     lambda eng, k: eng.wait_ge(us_split, k + 1), gains_of(5))
    gu.close()

    def sp_gate(sp):
        def body(i, last):
            for k in range(4):
                at = at_g(i, k)
                load(sp, at, unit_parts(at, w_gu, (0, KD), (i * 4 * P + k * P, P)), (lo_ready, at.plus(-RAW).count))

        body(0, False)
        sp.wait_ge(unit_done, ffn1.end.u)
        ffn1.ready(sp, KD - 1)
        sp.dma_start(ws_in[:, :, :], A["sgu_ws_2"].rearrange("a g i j -> i (a g) j")).then_inc(gs_landed, 16)
        sp.dma_start(bs_row[:, :], A["sgu_bs_2"].rearrange("a g i -> a (g i)")).then_inc(gs_landed, 16)
        with sp.Fori(1, N_GU) as i:
            body(i, False)

    def pe_gate(pe):
        norm_g.pe_sums(pe)
        pe.wait_ge(gs_landed, 32)
        for h in range(2):
            for g in range(KD // 2):
                tr = pe.transpose(bank[5 + h][:, g * P:(g + 1) * P], ws_in[:, h * (KD // 2) + g, :], ident[:, :])
            tr.then_inc(wsT_done, 1)
        for h in range(2):
            b = (7, 4)[h]
            if h:
                pe.wait_ge(var_ready.sem, norm_g.var0 + 1)
            pe.matmul(bank[b][:, :], ones[0:1, :], bs_row[:, h * T:(h + 1) * T], start=True, stop=True)\
              .then_inc(bs_done, 1)

        def body(i, last):
            for k in range(4):
                if not isinstance(i, int) or i:
                    pe.wait_ge(uv_ready, i * 4 + (k - 3))
                ready = split_g.pe_ready(pe) if isinstance(i, int) and i + k == 0 else None
                unit_products(pe, at_g(i, k), KD, bank[k][:, :], lambda k: gh_hi[:, k, :], lambda k: gh_lo[:, k, :],
                              True, True, ready)

        loop(pe, N_GU, body)
        for k in range(KD):
            pe.wait_ge(uv_ready, KD + k + 1)
            if k == 0:
                pe.wait_ge(wsT_ready, 2)
            mm = pe.matmul(bank[5][:, :], ones[:, :], uv[:, KD + k, :], start=k == 0, stop=k == KD - 1)
        mm.then_inc(mean_done, 1)
        norm_v.pe_sums(pe)
        for k in range(KD + 1):
            if k < KD:
                pe.wait_ge(vn_ready, k + 1)
                wait(pe, vt_ready, k - 1)
                for t in range(NT):
                    tr = pe.transpose(bank[k % 2][:, t * P:(t + 1) * P], uv[:, KD + k, t * P:(t + 1) * P], ident[:, :])
                tr.then_inc(vt_done, 1)
            if k:
                g = k - 1
                pe.wait_ge(vt_ready, g + 1)
                wait(pe, s_biased, g - 1)
                for t in range(NT):
                    mm = pe.matmul(bank[2 + g % 2][:, t * P:(t + 1) * P], v_tk[:, t, g * P:(g + 1) * P], wsT[:, g, :],
                                   start=True, stop=True)
                mm.then_inc(s_done, 1)
        out_gu.pe(pe)

    def act_gate(act):
        norm_g.act_squares(act)
        norm_g.act_root(act)
        split_g.act(act)
        for h in range(2):
            act.wait_ge(wsT_done, h + 1)
            act.activation(wsT[:, h * 4:(h + 1) * 4, :], bank[5 + h][:, :].rearrange("p (g c) -> p g c", c=P), ACT.Copy)\
               .then_inc(wsT_ready, 1)
        for h in range(2):
            act.wait_ge(bs_done, h + 1)
            act.activation(bs[:, h * 4:(h + 1) * 4, :], bank[(7, 4)[h]][:, :].rearrange("p (g c) -> p g c", c=P), ACT.Copy)\
               .then_inc(bs_ready, 1)

        def body(i, last):
            for k in range(4):
                split_hi(act, at_g(i, k).plus(2))
                act.wait_ge(unit_done, at_g(i, k).count)
                act.activation(tile_at(uv, i * 4 + k), bank[k][:, :], ACT.Gelu, bias=col_at(vecs, i * 4 + (col["sgu_b"] + k)))\
                   .then_inc(uv_ready, 1)

        loop(act, N_GU, body)
        norm_v.act_squares(act)
        norm_v.act_root(act)
        for k in range(KD):
            act.wait_ge(v_scaled, k + 1)
            act.activation(uv[:, KD + k, :], tmp[:, k % 3, :], ACT.Identity, bias=v("ln_b", k)).then_inc(vn_ready, 1)
        for k in range(KD + 1):
            if k < KD:
                act.wait_ge(vt_done, k + 1)
                act.activation(v_tk[:, :, k * P:(k + 1) * P], bank[k % 2][:, :].rearrange("p (t c) -> p t c", t=NT),
                               ACT.Copy).then_inc(vt_ready, 1)
            if k:
                g = k - 1
                act.wait_ge(us_ready, g + 1)
                act.activation(gh_hi[:, g, :], tmp[:, g % 3, :], ACT.Copy).then_inc(us_hi, 1)
        out_gu.act(act)

    def dve_gate(dve):
        norm_g.dve_rstd(dve)
        split_g.dve(dve)
        dve.wait_ge(wsT_ready, 2)
        dve.memset(wsT[CH:P, :, 0:CH], 0.0).then_inc(bs_ready, 1)

        def body(i, last):
            for k in range(4):
                split_lo(dve, at_g(i, k).plus(2))

        loop(dve, N_GU, body)
        dve.wait_ge(mean_done, 1)
        for k in range(KD):
            dve.scalar_tensor_tensor(uv[:, KD + k, :], bank[5][:, :], -1.0 / D, uv[:, KD + k, :], ALU.mult, ALU.add)\
               .then_inc(v_centred, 1)
        norm_v.dve_rstd(dve)
        for k in range(KD):
            wait(dve, vn_ready, k - 2)
            dve.scalar_tensor_tensor(tmp[:, k % 3, :], uv[:, KD + k, :], v("ln_w", k), rstd[:, :], ALU.mult, ALU.mult)\
               .then_inc(v_scaled, 1)
        dve.wait_ge(vn_ready, KD)
        dve.wait_ge(bs_ready, 3)

        def lower(g):
            dve.wait_ge(us_hi, g + 1)
            dve.tensor_tensor(gh_lo[:, g, :], tmp[:, g % 3, :], gh_hi[:, g, :].bitcast(F32), ALU.subtract)\
               .then_inc(us_split, 1)

        for g in range(KD):
            dve.wait_ge(s_done, g + 1)
            wait(dve, us_split, g - 2)
            t = tmp[:, g % 3, :].rearrange("p (t c) -> p t c", t=NT)
            dve.tensor_tensor(t, bank[2 + g % 2][:, :].rearrange("p (t c) -> p t c", t=NT),
                              bs[:, g:g + 1, :].to_broadcast([P, NT, P]), ALU.add).then_inc(s_biased, 1)
            dve.wait_ge(s_biased, g + 1)
            dve.tensor_tensor(tmp[:, g % 3, :], tmp[:, g % 3, :], uv[:, g, :], ALU.mult).then_inc(us_ready, 1)
            if g:
                lower(g - 1)
        dve.wait_ge(us_ready, KD)
        lower(KD - 1)
        out_gu.dve(dve)

    ffn2 = FFN("2", out_gu.end, out_gu.ready, gains_of(6), None, wg2[1], wu2[1], wd2[1], False, gains_of(7), final=True)

    with ExitStack() as part:
        x_out = sbs(part, "x_out", [P, NT, D])
    out_turned, out_copied, out_landed = sem("out_turned"), sem("out_copied"), sem("out_landed")

    def pe_out(pe):
        for n in range(2 * NT):
            t, h = divmod(n, 2)
            if n < 2:
                ffn2.ready(pe, (n + 1) * (KD // 2) - 1)
            wait(pe, out_copied, n - 3)
            for k in range(KD // 2):
                tr = pe.transpose(bank[n % 4][:, k * P:(k + 1) * P], x[:, h * (KD // 2) + k, t * P:(t + 1) * P], ident[:, :])
            tr.then_inc(out_turned, 1)

    def act_out(act):
        for n in range(2 * NT):
            act.wait_ge(out_turned, n + 1)
            act.activation(x_out[:, n // 2, n % 2 * T:(n % 2 + 1) * T], bank[n % 4][:, :], ACT.Copy).then_inc(out_copied, 1)

    def sp_out(sp):
        dst = out.rearrange("b (t p) d -> (b t) p d", p=P)
        for t in range(NT):
            sp.wait_ge(out_copied, 2 * t + 2)
            sp.dma_start(dst[t], x_out[:, t, :]).then_inc(out_landed, 16)
        sp.wait_ge(out_landed, 16 * NT)

    block = ctx.enter_context(nc.Block())

    @block.sync
    def _(sp):
        sp_setup(sp)
        sp_first_units(sp)
        ffn0.sp(sp)
        sp_time_mix(sp)
        out_tm.sp(sp, range(RAW))
        sp_blocks(sp)
        out_tm.sp(sp, range(RAW, KD))
        ffn1.sp(sp)
        sp_gate(sp)
        out_gu.sp(sp)
        ffn2.sp(sp)
        sp_out(sp)

    @block.gpsimd
    def _(pool):
        pool_setup(pool)
        pool_masks(pool)
        pool_blocks(pool)

    @block.scalar
    def _(act):
        act_setup_dmas(act)
        act_setup(act)
        act_mixer1(act)
        ffn0.act(act)
        norm_f.act_squares(act)
        norm_f.act_root(act)
        act_time_mix(act)
        act_blocks(act)
        act_split_y(act)
        out_tm.act(act)
        ffn1.act(act)
        act_gate(act)
        ffn2.act(act)
        act_out(act)

    @block.vector
    def _(dve):
        dve_setup(dve)
        dve_mixer1(dve)
        scaled_gain(dve, "norm2", 4)
        ffn0.dve(dve)
        dve_final(dve)
        dve_time_mix(dve)
        dve_blocks(dve)
        dve_split_y(dve)
        out_tm.dve(dve)
        ffn1.dve(dve)
        dve_gate(dve)
        ffn2.dve(dve)

    @block.tensor
    def _(pe):
        pe_setup(pe)
        pe_mixer1(pe)
        ffn0.pe(pe)
        norm_f.pe_sums(pe)
        pe_time_mix(pe)
        pe_blocks(pe)
        out_tm.pe(pe)
        ffn1.pe(pe)
        pe_gate(pe)
        ffn2.pe(pe)
        pe_out(pe)

    return ctx


_INS = ["x", "c", "positions", "ada_w", "ada_b", "norm1_g", "w_in", "b_in", "conv_w", "attn_sinks",
        "out_norm_attn_g", "out_norm_conv_g", "w_o", "norm2_g", "w_up", "ffn_conv_w", "ffn_conv_b", "w_down",
        "final_norm_g", "norm_gains_2", "rwkv_mix_2", "rwkv_w_rkv_2", "rwkv_w0_2", "rwkv_w1_2", "rwkv_w2_2",
        "rwkv_a0_2", "rwkv_a1_2", "rwkv_a2_2", "rwkv_g1_2", "rwkv_g2_2", "rwkv_k_k_2", "rwkv_k_a_2",
        "rwkv_r_k_2", "rwkv_gn_w_2", "rwkv_gn_b_2", "rwkv_w_o_2", "sgu_w_in_2", "sgu_b_in_2", "sgu_ln_w_2",
        "sgu_ln_b_2", "sgu_ws_2", "sgu_bs_2", "sgu_w_out_2", "ffn_w_gate_2", "ffn_w_up_2", "ffn_w_down_2"]
ROPE_THETA = 10000.0


def kernel(**inputs):
    import numpy as _np
    import concourse.bacc as _bacc
    from concourse import mybir as _mybir
    from concourse.bass_utils import run_bass_kernel_spmd as _run

    arrays = {name: _np.ascontiguousarray(inputs[name]) for name in _INS}
    half = HD // 2
    inv = ROPE_THETA ** (-_np.arange(half, dtype=_np.float32) / _np.float32(half))
    arrays["inv_freq"] = _np.tile(inv.astype(_np.float32), P // half).reshape(P, 1)

    nc = _bacc.Bacc("TRN2", target_bir_lowering=False, num_devices=1)
    A = {name: nc.dram_tensor(f"in_{name}_dram", a.shape, _mybir.dt.from_np(a.dtype), kind="ExternalInput").ap()
         for name, a in arrays.items()}
    out = nc.dram_tensor("out_0_dram", (1, T, D), F32, kind="ExternalOutput").ap()
    with build(nc, A, out):
        pass
    r = _run(nc, [{f"in_{name}_dram": a for name, a in arrays.items()}], core_ids=[0])
    return r.results[0]["out_0_dram"]
```

```python
from contextlib import ExitStack

import numpy as np

import concourse.bass as bass
from concourse import mybir

F32 = mybir.dt.float32
F32R = mybir.dt.float32r
I32 = mybir.dt.int32
ALU = mybir.AluOpType
ACT = mybir.ActivationFunctionType
AX_X = mybir.AxisListType.X

P = 128
T = 512
D = 1024
KD = D // P
NT = T // P
DFF = 2816
KF = DFF // P
HALF = KF // 2
HD = 64
NQ, NKV = 8, 2
DA = NQ * HD
KA = DA // P
RAW = 4
EPS = 1e-6
TWO_PI = 2 * np.pi
TURN1 = 6.28125
TURN2 = float(np.float32(round((TWO_PI - TURN1) * 2 ** 22) / 2 ** 22))
TURN3 = float(np.float32(TWO_PI - TURN1 - TURN2))
ROUND = float(1.5 * 2 ** 23)
MASKED = -1e30


class Count:

    def __init__(self, sem):
        self.sem, self.n = sem, 0

    def claim(self, n):
        self.n += n
        return self.n - n


class At:

    def __init__(self, c, u, step=0, i=0):
        self.c, self.u, self.step, self.i = c, u, step, i

    def plus(self, k):
        return At(self.c + k, self.u + k, self.step, self.i)

    @property
    def raw_slot(self):
        return self.c % RAW

    @property
    def slot(self):
        return self.u % 2

    @property
    def count(self):
        return self.u + 1 + self.i * self.step


def wait(eng, sem, value):
    if isinstance(value, int) and value <= 0:
        return
    eng.wait_ge(sem, value)


def loop(eng, n, body):
    body(0, False)
    with eng.Fori(1, n - 1) as i:
        body(i, False)
    body(n - 1, True)


def tile_at(t, k):
    if isinstance(k, int):
        return t[:, k, :]
    return t[:, bass.ds(k, 1), :].rearrange("p a n -> p (a n)")


def cols_at(t, start, n):
    return t[:, start:start + n] if isinstance(start, int) else t[:, bass.ds(start, n)]


def col_at(t, k):
    if isinstance(k, int):
        return t[:, k:k + 1]
    return t[:, bass.ds(k, 1)]


def build(nc, A, out):
    ctx = ExitStack()

    def sb(name, shape, dt=F32):
        return ctx.enter_context(nc.sbuf_tensor(name, shape, dt))

    def sem(name):
        return ctx.enter_context(nc.semaphore(name))

    def count(name):
        return Count(sem(name))

    x = sb("x", [P, KD, T])
    raw = sb("raw", [P, RAW, HALF * P])
    whi = sb("whi", [P, 2, HALF * P], F32R)
    wlo = sb("wlo", [P, 2, HALF * P], F32R)
    ident = sb("ident", [P, P])
    ones = sb("ones", [P, P])
    tmp = sb("tmp", [P, 3, T])
    sq = sb("sq", [P, 2, T])
    sq_sum = sb("sq_sum", [P, T])
    var = sb("var", [P, T])
    rstd = sb("rstd", [P, T])
    mod = sb("mod", [P, 6 * KD])
    gain = sb("gain", [P, KD])
    cact = sb("cact", [P, KD])
    bank = [ctx.enter_context(nc.psum_tensor(f"bank{i}", [P, T], F32)) for i in range(8)]
    NORM_BANK, ADA_BANKS = 4, (7, 6, 6)

    vec_src, col = [], {}

    def vec(name, sources, n):
        col[name] = sum(m for _, m in vec_src)
        vec_src.append((sources, n))

    def vec_rows(name, ap, n):
        vec(name, [(slice(0, P), ap)], n)

    def vec_pairs(name, ap):
        vec(name, [(slice(0, HD), ap[0:DA // 2].rearrange("(j p) -> j p", p=HD)),
                   (slice(HD, P), ap[DA // 2:DA].rearrange("(j p) -> j p", p=HD))], KA)

    flat = lambda ap: ap.rearrange("a n -> (a n)")
    rows = lambda ap: ap.rearrange("(k p) -> k p", p=P)
    vec_rows("ada_b", rows(flat(A["ada_b"])), 6 * KD)
    vec_rows("norm1", rows(flat(A["norm1_g"])), KD)
    vec_rows("b_in", rows(flat(A["b_in"])[DA:]), 14)
    vec_pairs("bq", flat(A["b_in"])[0:DA])
    vec_rows("conv_w", A["conv_w"].rearrange("a w (k p) -> (a w k) p", p=P), 12)
    vec_rows("ga", rows(flat(A["out_norm_attn_g"])), KA)
    vec_rows("gcv", rows(flat(A["out_norm_conv_g"])), 4)
    vec_rows("norm2", rows(flat(A["norm2_g"])), KD)
    vec_rows("final", rows(A["final_norm_g"]), KD)

    vec_rows("ffn_cw", A["ffn_conv_w"].rearrange("a w (k p) -> (a w k) p", p=P), 3 * KF)
    vec_rows("ffn_cb", rows(flat(A["ffn_conv_b"])), KF)

    vec_rows("w0", rows(flat(A["rwkv_w0_2"])), KD)
    vec_rows("a0", rows(flat(A["rwkv_a0_2"])), KD)
    vec_rows("k_k", rows(flat(A["rwkv_k_k_2"])), KD)
    vec_rows("k_a", rows(flat(A["rwkv_k_a_2"])), KD)
    vec_rows("mix", A["rwkv_mix_2"].rearrange("a m (k p) -> (a m k) p", p=P), 6 * KD)
    vec_rows("r_k", A["rwkv_r_k_2"].rearrange("a (k h) n -> (a k) (h n)", h=2), KD)
    vec_rows("gn_w", rows(flat(A["rwkv_gn_w_2"])), KD)
    vec_rows("gn_b", rows(flat(A["rwkv_gn_b_2"])), KD)
    vec_rows("gains", A["norm_gains_2"].rearrange("l m (k p) -> (l m k) p", p=P), 8 * KD)
    vec_rows("sgu_b", rows(flat(A["sgu_b_in_2"])), 2 * KD)
    vec_rows("ln_w", rows(flat(A["sgu_ln_w_2"])), KD)
    vec_rows("ln_b", rows(flat(A["sgu_ln_b_2"])), KD)
    n_vec = sum(m for _, m in vec_src)
    VB = -(-n_vec // P)
    vecs = sb("vecs", [P, VB * P])

    def v(name, k=0):
        return col_at(vecs, col[name] + k)

    landed = [sem(f"raw{s}_landed") for s in range(RAW)]
    hi_ready, lo_ready = sem("hi_ready"), sem("lo_ready")
    unit_done, ada_done = sem("unit_done"), sem("ada_done")
    n_units = [0, 0]

    def raw_unit(at, kts):
        return raw[:, at.raw_slot, 0:kts * P]

    def load(sp, at, parts, freed):
        if freed is not None:
            wait(sp, *freed)
        for dst, src in parts:
            sp.dma_start(dst, src).then_inc(landed[at.raw_slot], 16)

    def unit_parts(at, w, ks, cols):
        k0, kts = ks
        src = cols_at(w[k0 * P:(k0 + kts) * P, :], *cols).rearrange("(k p) n -> p k n", p=P)
        return [(raw[:, at.raw_slot, 0:kts * P].rearrange("p (k n) -> p k n", n=P), src)]

    def split_hi(act, at, kts=KD):
        act.wait_ge(landed[at.raw_slot], landed_at(at))
        wait(act, unit_done, at.plus(-2).count)
        act.activation(whi[:, at.slot, 0:kts * P], raw_unit(at, kts), ACT.Copy).then_inc(hi_ready, 1)

    def split_lo(dve, at, kts=KD):
        dve.wait_ge(landed[at.raw_slot], landed_at(at))
        dve.wait_ge(hi_ready, at.count)
        dve.tensor_tensor(wlo[:, at.slot, 0:kts * P], raw_unit(at, kts),
                          whi[:, at.slot, 0:kts * P].bitcast(F32), ALU.subtract).then_inc(lo_ready, 1)

    def unit_products(pe, at, kts, dst, rhs_hi, rhs_lo, first, last, k_ready=None, ks=None):
        ks = range(kts) if ks is None else ks
        if ks[0] == 0:
            pe.wait_ge(lo_ready, at.count)
        for k in ks:
            if k_ready is not None:
                k_ready(k)
            hi, lo = (w[:, at.slot, k * P:(k + 1) * P] for w in (whi, wlo))
            pe.matmul(dst, hi, rhs_hi(k), start=first and k == 0, stop=False)
            pe.matmul(dst, hi, rhs_lo(k), start=False, stop=False)
            mm = pe.matmul(dst, lo, rhs_hi(k), start=False, stop=last and k == kts - 1)
        if ks[-1] == kts - 1:
            mm.then_inc(unit_done, 1)

    sq_ready, acc_step, sum_step = count("sq_ready"), count("acc_step"), count("sum_step")
    var_ready, std_ready, rstd_ready = count("var_ready"), count("std_ready"), count("rstd_ready")
    tmp_ready, nhi_ready, h_ready = count("tmp_ready"), count("nhi_ready"), count("h_ready")
    x_ready, x_added = count("x_ready"), count("x_added")

    class Norm:

        def __init__(self, src, n, ready, eps=EPS):
            self.src, self.n, self.ready, self.eps = src, n, ready, eps
            self.sq0, self.acc0 = sq_ready.claim(n), acc_step.claim(n - 2)
            self.sum0, self.var0, self.std0, self.rstd0 = (
                c.claim(1) for c in (sum_step, var_ready, std_ready, rstd_ready))

        def act_slot_free(self, act, k):
            if not isinstance(k, int):
                act.wait_ge(acc_step.sem, k + (self.acc0 - 1))
            elif k >= 2:
                act.wait_ge(acc_step.sem, self.acc0 + max(1, k - 2))
            else:
                wait(act, sum_step.sem, self.sum0)

        def act_square(self, act, k):
            self.ready(act, k)
            self.act_slot_free(act, k)
            act.activation(sq[:, k % 2, :], self.src(k), ACT.Square).then_inc(sq_ready.sem, 1)

        def act_square_of(self, act, src, parity):
            act.activation(sq[:, parity, :], src, ACT.Square).then_inc(sq_ready.sem, 1)

        def act_squares(self, act):
            for k in range(self.n):
                self.act_square(act, k)

        def pool_sum(self, pool):
            wait(pool, sum_step.sem, self.sum0)
            for k in range(1, self.n - 1):
                pool.wait_ge(sq_ready.sem, self.sq0 + k + 1)
                wait(pool, acc_step.sem, self.acc0 + k - 1)
                pool.tensor_tensor(sq_sum[:, :], sq[:, 0, :] if k == 1 else sq_sum[:, :], sq[:, k % 2, :], ALU.add)\
                    .then_inc(acc_step.sem, 1)

        def act_root(self, act):
            act.wait_ge(var_ready.sem, self.var0 + 1)
            act.activation(var[:, :], var[:, :], ACT.Sqrt).then_inc(std_ready.sem, 1)

        def pe_sums(self, pe):
            wait(pe, var_ready.sem, self.var0)
            pe.wait_ge(acc_step.sem, self.acc0 + self.n - 2)
            pe.matmul(bank[NORM_BANK][:, :], ones[:, :], sq_sum[:, :], start=True, stop=False)
            pe.wait_ge(sq_ready.sem, self.sq0 + self.n)
            pe.matmul(bank[NORM_BANK][:, :], ones[:, :], sq[:, (self.n - 1) % 2, :], start=False, stop=True)\
              .then_inc(sum_step.sem, 1)

        def dve_rstd(self, dve):
            dve.wait_ge(sum_step.sem, self.sum0 + 1)
            dve.tensor_scalar(var[:, :], bank[NORM_BANK][:, :], 1.0 / (self.n * P), self.eps,
                              ALU.mult, ALU.add).then_inc(var_ready.sem, 1)
            dve.wait_ge(std_ready.sem, self.std0 + 1)
            dve.reciprocal(rstd[:, :], var[:, :]).then_inc(rstd_ready.sem, 1)
            dve.wait_ge(rstd_ready.sem, self.rstd0 + 1)

    class Split:

        def __init__(self, src, n, gains, shift, dst_hi, dst_lo, free):
            self.src, self.n, self.gains, self.shift = src, n, gains, shift
            self.hi, self.lo, self.free = dst_hi, dst_lo, free
            self.t0, self.hi0, self.h0 = (c.claim(n) for c in (tmp_ready, nhi_ready, h_ready))

        def dve(self, dve):
            def lower(k):
                dve.wait_ge(nhi_ready.sem, self.hi0 + k + 1)
                if self.shift is None:
                    ins = dve.tensor_tensor(self.lo(k), tmp[:, (self.t0 + k) % 3, :],
                                            self.hi(k).bitcast(F32), ALU.subtract)
                else:
                    ins = dve.scalar_tensor_tensor(self.lo(k), tmp[:, (self.t0 + k) % 3, :], self.shift(k),
                                                   self.hi(k).bitcast(F32), ALU.add, ALU.subtract)
                ins.then_inc(h_ready.sem, 1)

            self.free(dve)
            for k in range(self.n):
                wait(dve, h_ready.sem, self.h0 + k - 2)
                dve.scalar_tensor_tensor(tmp[:, (self.t0 + k) % 3, :], self.src(k), self.gains(k),
                                         rstd[:, :], ALU.mult, ALU.mult).then_inc(tmp_ready.sem, 1)
                if k == 0:
                    dve.wait_ge(tmp_ready.sem, self.t0 + 1)
                if k:
                    dve.wait_ge(tmp_ready.sem, self.t0 + k)
                    lower(k - 1)
            lower(self.n - 1)

        def act(self, act):
            self.free(act)
            for k in range(self.n):
                act.wait_ge(tmp_ready.sem, self.t0 + k + 1)
                act.activation(self.hi(k), tmp[:, (self.t0 + k) % 3, :], ACT.Identity,
                               bias=0.0 if self.shift is None else self.shift(k))\
                   .then_inc(nhi_ready.sem, 1)

        def pe_ready(self, pe):
            return lambda k: pe.wait_ge(h_ready.sem, self.h0 + k + 1)

    w_in, w_o, ada_w = (A[n].rearrange("a k n -> (a k) n") for n in ("w_in", "w_o", "ada_w"))
    order = [("ada", m) for m in range(2 * KD)]
    N_IN, N_O = 18, KD
    ada_next = 2 * KD
    for u in range(N_IN):
        order += [("in", u), ("ada", ada_next)]
        ada_next += 1
    for u in range(N_O):
        order.append(("o", u))
        n_ada = 0 if u >= 4 else 3 if u < 2 else 4
        for _ in range(n_ada):
            order.append(("ada", ada_next))
            ada_next += 1
    assert ada_next == 6 * KD
    at_in, at_ada, at_o, seq = {}, {}, {}, []
    u_next = 0
    for c, (kind, n) in enumerate(order):
        at = At(c, u_next)
        seq.append((kind, n, at))
        {"in": at_in, "o": at_o, "ada": at_ada}[kind][n] = at
        u_next += kind != "ada"
    first = [at for kind, _, at in seq if kind != "ada"]
    for n in range(2):
        first.append(At(len(seq) + n, u_next + n))
    IN0 = {"q": 0, "k": 4, "v": 5, "conv": 6}

    def in_columns(u):
        if u < 6:
            return u * P, P
        j, part = divmod(u - 6, 3)
        start = DA + 2 * NKV * HD + part * (D - DA) + j * P
        return start, P

    fixed, slot_count = {}, [0] * RAW
    for kind, n, at in seq:
        slot_count[at.raw_slot] += 32 if kind == "in" and n < 4 else 16
        fixed[at.c] = slot_count[at.raw_slot]

    def landed_at(at):
        if at.c < len(seq):
            return fixed[at.c]
        more = (at.c // RAW + 1) - (len(seq) + RAW - 1 - at.raw_slot) // RAW
        return slot_count[at.raw_slot] + more * 16 + at.i * (at.step // RAW * 16)

    def sp_first_units(sp):
        for c, (kind, n, at) in enumerate(seq):
            freed = None
            if c >= RAW:
                was, m, old = seq[c - RAW]
                freed = (ada_done, m + 1) if was == "ada" else (lo_ready, old.count)
            if kind == "ada":
                part, k = divmod(n, KD)
                parts = [(raw[:, at.raw_slot, 0:D], ada_w[k * P:(k + 1) * P, part * D:(part + 1) * D])]
            elif kind == "o":
                parts = unit_parts(at, w_o, (0, KD), (n * P, P))
            elif n < 4:
                parts = [(raw[:, at.raw_slot, 0:KD * P].rearrange("p (k h d) -> p k h d", h=2, d=HD)[:, :, h, :],
                          w_in[:, (n + 4 * h) * HD:(n + 4 * h + 1) * HD].rearrange("(k p) d -> p k d", p=P))
                         for h in range(2)]
            else:
                parts = unit_parts(at, w_in, (0, KD), in_columns(n))
            load(sp, at, parts, freed)

    setup = ExitStack()

    def sbs(stage, name, shape, dt=F32):
        return stage.enter_context(nc.sbuf_tensor(name, shape, dt))

    mixer1 = ExitStack()
    h_hi = sbs(mixer1, "h_hi", [P, KD, T], F32R)
    h_lo = sbs(mixer1, "h_lo", [P, KD, T], F32R)
    rot = sbs(mixer1, "rot", [P, P])
    mask = sbs(mixer1, "mask", [P, 2 * P])
    cos_t = sbs(mixer1, "cos_t", [P, T])
    sin_t = sbs(mixer1, "sin_t", [P, T])
    sinks = sbs(mixer1, "sinks", [P, NQ])
    sinks_row = sbs(mixer1, "sinks_row", [1, NQ])
    c_row = sbs(mixer1, "c_row", [KD, P])
    invf = sbs(mixer1, "invf", [P, 1])
    pos_i = sbs(mixer1, "pos_i", [1, T], I32)
    pos_f = sbs(mixer1, "pos_f", [1, T])
    q_t = sbs(mixer1, "q_t", [P, KA, T])
    k_t = sbs(mixer1, "k_t", [P, T])
    v_tok = sbs(mixer1, "v_tok", [P, NT, P])
    prj = sbs(mixer1, "prj", [P, 2, T])
    s_sb = sbs(mixer1, "s_sb", [P, 2, 2, 2 * P])
    p_sb = sbs(mixer1, "p_sb", [P, 2, 2, 2 * P])
    p_t = sbs(mixer1, "p_t", [P, 2, 4 * P])
    st = sbs(mixer1, "st", [P, 2, 12])
    y_at = sbs(mixer1, "y_at", [P, KA, T])
    y_cv = sbs(mixer1, "y_cv", [P, 4, T])
    gb_sb = sbs(mixer1, "gb_sb", [P, 2, T])
    cbuf = sbs(mixer1, "cbuf", [P, 2, T + 2])
    cacc = sbs(mixer1, "cacc", [P, 2, T])
    ada_acc = sbs(mixer1, "ada_acc", [P, 2, D])
    x_tok = sbs(setup, "x_tok", [P, NT, D])
    vrow = sbs(setup, "vrow", [P, VB, P])
    setup.close()
    ang = [y_at[:, n, :] for n in range(4)] + [y_cv[:, n, :] for n in range(2)]

    x_landed, vec_landed, small_landed = sem("x_landed"), sem("vec_landed"), sem("small_landed")
    const_ready, x_turned, vec_turned = sem("const_ready"), sem("x_turned"), sem("vec_turned")
    vecs_ready, small_in, small_out, angle = sem("vecs_ready"), sem("small_in"), sem("small_out"), sem("angle")
    cact_ready, c_landed, c_turned = sem("cact_ready"), sem("c_landed"), sem("c_turned")
    n_vec_dmas = 0
    VEC_PLAN = []
    for sources, n in vec_src:
        row = sum(m for _, m in vec_src[:vec_src.index((sources, n))])
        done = 0
        while done < n:
            b, r = divmod(row + done, P)
            m = min(n - done, P - r)
            for cols, ap in sources:
                VEC_PLAN.append((vrow[r:r + m, b, cols], ap[done:done + m, :]))
            done += m
    LAST_ROWS = n_vec - (VB - 1) * P
    x_ready.claim(KD)

    def act_setup_dmas(act):
        x_in = A["x"].rearrange("b (t p) d -> (b t) p d", p=P)
        act.dma_start(c_row[:, :], A["c"].rearrange("b (k p) -> (b k) p", p=P)).then_inc(c_landed, 16)
        act.dma_start(pos_i[:, :], A["positions"]).then_inc(small_landed, 16)
        act.dma_start(sinks_row[:, :], A["attn_sinks"]).then_inc(small_landed, 16)
        act.dma_start(invf[:, :], A["inv_freq"]).then_inc(small_landed, 16)
        for t in range(NT):
            act.dma_start(x_tok[:, t, :], x_in[t]).then_inc(x_landed, 16)
        act.wait_ge(c_turned, 1)
        act.activation(cact[:, :], bank[4][:, 0:KD], ACT.Silu).then_inc(cact_ready, 1)
        for dst, src in VEC_PLAN:
            act.dma_start(dst, src).then_inc(vec_landed, 16)

    def pool_setup(pool):
        pool.memset(ident[:, :], 0.0).then_inc(const_ready, 1)
        pool.memset(ones[:, :], 1.0).then_inc(const_ready, 1)
        pool.memset(rot[:, :], 0.0).then_inc(const_ready, 1)
        pool.memset(mask[:, :], 0.0).then_inc(const_ready, 1)
        pool.wait_ge(const_ready, 4)
        pool.affine_select(out=ident[:, :], in_=ident[:, :], compare_op=ALU.not_equal, fill=1.0, base=0,
                           pattern=[[-1, P]], channel_multiplier=1).then_inc(const_ready, 1)
        lower = rot[:, :].rearrange("p (h s m) -> p h s m", h=2, s=2)
        pool.affine_select(out=lower[:, :, 0, :], in_=lower[:, :, 0, :], compare_op=ALU.not_equal, fill=-1.0,
                           base=-32, pattern=[[-HD, 2], [-1, 32]], channel_multiplier=1).then_inc(const_ready, 1)
        pool.wait_ge(const_ready, 6)
        pool.affine_select(out=lower[:, :, 1, :], in_=lower[:, :, 1, :], compare_op=ALU.not_equal, fill=1.0,
                           base=0, pattern=[[-HD, 2], [-1, 32]], channel_multiplier=1).then_inc(const_ready, 1)
        pool.affine_select(out=mask[:, :], in_=mask[:, :], compare_op=ALU.is_ge, fill=MASKED, base=P,
                           pattern=[[-1, 2 * P]], channel_multiplier=1).then_inc(const_ready, 1)
        pool.wait_ge(const_ready, 8)
        pool.affine_select(out=mask[:, :], in_=mask[:, :], compare_op=ALU.is_gt, fill=MASKED, base=0,
                           pattern=[[1, 2 * P]], channel_multiplier=-1).then_inc(const_ready, 1)
        pool.memset(cbuf[:, :, 0:2], 0.0).then_inc(const_ready, 1)

    CONSTS = 10

    def pe_setup(pe):
        pe.wait_ge(const_ready, CONSTS)
        pe.wait_ge(c_landed, 16)
        pe.transpose(bank[4][:, 0:KD], c_row[:, :], ident[0:KD, 0:KD]).then_inc(c_turned, 1)
        pe.wait_ge(small_in, 1)
        pe.matmul(bank[2][:, :], ones[0:1, :], pos_f[:, :], start=True, stop=True)
        pe.matmul(bank[3][:, 0:NQ], ones[0:1, :], sinks_row[:, :], start=True, stop=True).then_inc(small_out, 1)
        pe.wait_ge(x_landed, 16 * NT)
        for k in range(KD):
            wait(pe, x_ready.sem, k - 1)
            for t in range(NT):
                tr = pe.transpose(bank[k % 2][:, t * P:(t + 1) * P], x_tok[:, t, k * P:(k + 1) * P], ident[:, :])
            tr.then_inc(x_turned, 1)
        pe.wait_ge(vec_landed, 16 * len(VEC_PLAN))
        for b in range(VB):
            m = P if b < VB - 1 else LAST_ROWS
            tr = pe.transpose(bank[5][:, b * P:b * P + m], vrow[0:m, b, :], ident[0:m, 0:m])
        tr.then_inc(vec_turned, 1)

    def act_setup(act):
        for k in range(KD):
            act.wait_ge(x_turned, k + 1)
            act.activation(x[:, k, :], bank[k % 2][:, :], ACT.Copy).then_inc(x_ready.sem, 1)
        act.wait_ge(vec_turned, 1)
        act.activation(vecs[:, 0:n_vec], bank[5][:, 0:n_vec], ACT.Copy).then_inc(vecs_ready, 1)

    def dve_positions(dve):
        dve.wait_ge(small_landed, 48)
        dve.tensor_copy(pos_f[:, :], pos_i[:, :]).then_inc(small_in, 1)

    def dve_angles(dve):
        dve.wait_ge(small_out, 1)
        dve.tensor_copy(sinks[:, :], bank[3][:, 0:NQ]).then_inc(angle, 1)
        steps = [0]

        def step(ins):
            ins.then_inc(angle, 1)
            steps[0] += 1
            dve.wait_ge(angle, steps[0] + 1)

        a = lambda n: ang[n]
        step(dve.tensor_scalar(a(0), bank[2][:, :], invf[:, 0:1], None, ALU.mult))
        for n, quarter, shift, dst in ((1, 0.0, 0.0, a(4)), (2, 0.25, float(np.pi / 2), a(5))):
            step(dve.tensor_scalar(a(n), a(0), 1 / TWO_PI, quarter, ALU.mult, ALU.add))
            step(dve.tensor_scalar(a(3), a(n), ROUND, ROUND, ALU.add, ALU.subtract))
            step(dve.scalar_tensor_tensor(a(n), a(3), -TURN1, a(0), ALU.mult, ALU.add))
            step(dve.scalar_tensor_tensor(dst, a(3), -TURN2, a(n), ALU.mult, ALU.add))
            step(dve.scalar_tensor_tensor(a(n), a(3), -TURN3, dst, ALU.mult, ALU.add))
            step(dve.tensor_scalar(a(3), a(n), shift, 3.1415925, ALU.add, ALU.min))
            step(dve.tensor_scalar(dst, a(3), -3.1415925, None, ALU.max))

    ANGLES = 16

    def act_angles(act):
        act.wait_ge(angle, ANGLES)
        act.activation(sin_t[:, :], ang[4], ACT.Sin).then_inc(rope_ready, 1)
        act.activation(cos_t[:, :], ang[5], ACT.Sin).then_inc(rope_ready, 1)

    rope_ready = sem("rope_ready")

    ada_scaled = sem("ada_scaled")
    ada_evac, ada_sum, gain_ready = sem("ada_evac"), sem("ada_sum"), count("gain_ready")
    ADA_EARLY = 2
    ADA_BATCH = [(0, 2), (2, 3), (3, 6)]

    def ada_accumulate(eng, m):
        at = at_ada[m]
        part, k = divmod(m, KD)
        acc, rows_, c_ = ada_acc[:, part % 2, :], raw[:, at.raw_slot, 0:D], cact[:, k:k + 1]
        if m % (KD * ADA_EARLY) == 0:
            eng.wait_ge(cact_ready, 1)
        if part >= 2 and k == 0:
            eng.wait_ge(ada_sum, part - 1)
        eng.wait_ge(landed[at.raw_slot], landed_at(at))
        wait(eng, ada_done, m)
        if k == 0:
            ins = eng.tensor_scalar(acc, rows_, c_, None, ALU.mult)
        elif part < ADA_EARLY:
            ins = eng.scalar_tensor_tensor(acc, rows_, c_, acc, ALU.mult, ALU.add)
        else:
            n = (part - ADA_EARLY) * (KD - 1) + k
            eng.tensor_scalar(rows_, rows_, c_, None, ALU.mult).then_inc(ada_scaled, 1)
            eng.wait_ge(ada_scaled, n)
            ins = eng.tensor_tensor(acc, acc, rows_, ALU.add)
        ins.then_inc(ada_done, 1)

    def ada_sums(pe, part):
        pe.wait_ge(ada_done, (part + 1) * KD)
        batch = [n for n, (a, b) in enumerate(ADA_BATCH) if a <= part < b][0]
        if part == ADA_BATCH[2][0]:
            pe.wait_ge(ada_evac, 2)
        for n in range(KD):
            m = part * KD + n
            mm = pe.matmul(bank[ADA_BANKS[batch]][:, m:m + 1], ada_acc[:, part % 2, n * P:(n + 1) * P],
                           ones[:, 0:1], start=True, stop=True)
        mm.then_inc(ada_sum, 1)

    def ada_add(dve, batch):
        a, b = ADA_BATCH[batch]
        dve.wait_ge(ada_sum, b)
        if batch == 0:
            dve.wait_ge(vecs_ready, 1)
        ab, a, b = col["ada_b"], a * KD, b * KD
        dve.tensor_tensor(mod[:, a:b], bank[ADA_BANKS[batch]][:, a:b], vecs[:, ab + a:ab + b], ALU.add)\
           .then_inc(ada_evac, 1)
        dve.wait_ge(ada_evac, batch + 1)

    def scaled_gain(dve, name, scale):
        g0 = gain_ready.claim(1)
        dve.scalar_tensor_tensor(gain[:, :], mod[:, scale * KD:(scale + 1) * KD], 1.0,
                                 vecs[:, col[name]:col[name] + KD], ALU.add, ALU.mult).then_inc(gain_ready.sem, 1)
        dve.wait_ge(gain_ready.sem, g0 + 1)

    def mod_col(part):
        return lambda k: mod[:, part * KD + k:part * KD + k + 1]

    def from_start(eng, k):
        eng.wait_ge(x_ready.sem, k + 1)

    x_tile = lambda k: x[:, k, :]
    norm1 = Norm(x_tile, KD, from_start)
    split1 = Split(x_tile, KD, lambda k: gain[:, k:k + 1], mod_col(0), lambda k: h_hi[:, k, :],
                   lambda k: h_lo[:, k, :], lambda eng: None)
    N_PRE = 6
    prj_ready, rot_done, rope_done = sem("prj_ready"), sem("rot_done"), sem("rope_done")
    vT_done, v_ready = sem("vT_done"), sem("v_ready")
    gb_ready, conv_p, conv_done = sem("gb_ready"), sem("conv_p"), sem("conv_done")
    sc_done, s_ready, stat, e_ready = sem("sc_done"), sem("s_ready"), sem("stat"), sem("e_ready")
    probs_ready, pT_done, pT_ready, pv_done, y_ready = (sem(n) for n in (
        "probs_ready", "pT_done", "pT_ready", "pv_done", "y_ready"))
    STEPS = [(2 * jj + js, n) for jj in range(2) for n in range(NT) for js in range(2)]
    SC, PT, PV, MIX = (3, 4), 7, 5, (0, 1, 2)

    def act_ahead(act, u, kts=KD):
        split_hi(act, first[u + 2], kts)

    def pe_in(pe, u, ks=range(KD)):
        if u < N_PRE:
            b = u % 2
            if u >= 2:
                pe.wait_ge(prj_ready, u - 1)
        else:
            j, part = divmod(u - N_PRE, 3)
            b = MIX[part]
            if j >= 1:
                pe.wait_ge(conv_done, j)
            elif part < 2:
                pe.wait_ge(prj_ready, N_PRE)
        unit_products(pe, at_in[u], KD, bank[b][:, :], lambda k: h_hi[:, k, :], lambda k: h_lo[:, k, :],
                      True, True, split1.pe_ready(pe) if u == 0 else None, ks)

    def act_in(act, u):
        act_ahead(act, u)
        at = at_in[u]
        if u < N_PRE:
            bias = v("bq", u) if u < 4 else v("b_in", u - 4)
            act.wait_ge(unit_done, at.count)
            if u >= 2:
                act.wait_ge(rope_done, u - 1)
            act.activation(prj[:, u % 2, :], bank[u % 2][:, :], ACT.Identity, bias=bias).then_inc(prj_ready, 1)
        elif (u - N_PRE) % 3 == 0:
            j = (u - N_PRE) // 3
            act.wait_ge(unit_done, at.count)
            wait(act, conv_p, j - 1)
            act.activation(gb_sb[:, j % 2, :], bank[MIX[0]][:, :], ACT.Identity, bias=v("b_in", 2 + j))\
               .then_inc(gb_ready, 1)

    def dve_in(dve, u):
        split_lo(dve, first[u + 2])
        at = at_in[u]
        if u >= N_PRE and (u - N_PRE) % 3 == 2:
            j = (u - N_PRE) // 3
            dve.wait_ge(unit_done, at.count)
            dve.wait_ge(gb_ready, j + 1)
            wait(dve, conv_done, j - 1)
            if j == 0:
                dve.wait_ge(rope_done, 5)
            c, acc = cbuf[:, j % 2, :], cacc[:, j % 2, :]
            dve.scalar_tensor_tensor(c[:, 2:T + 2], bank[MIX[2]][:, :], v("b_in", 10 + j), gb_sb[:, j % 2, :],
                                     ALU.add, ALU.mult).then_inc(conv_p, 1)
            dve.wait_ge(conv_p, j + 1)
            conv_taps(dve, acc, c, lambda w: v("conv_w", 4 * w + j), conv_t, 3 * j)
            dve.scalar_tensor_tensor(y_cv[:, j, :], bank[MIX[1]][:, :], v("b_in", 6 + j), acc,
                                     ALU.add, ALU.mult).then_inc(conv_done, 1)

    conv_t = sem("conv_t")

    def conv_taps(dve, acc, c, w, sem_t, base):
        dve.tensor_scalar(acc, c[:, 0:T], w(0), None, ALU.mult).then_inc(sem_t, 1)
        dve.wait_ge(sem_t, base + 1)
        dve.scalar_tensor_tensor(acc, c[:, 1:T + 1], w(1), acc, ALU.mult, ALU.add).then_inc(sem_t, 1)
        dve.wait_ge(sem_t, base + 2)
        dve.scalar_tensor_tensor(acc, c[:, 2:T + 2], w(2), acc, ALU.mult, ALU.add).then_inc(sem_t, 1)
        dve.wait_ge(sem_t, base + 3)

    def pe_rotate(pe, u):
        pe.wait_ge(prj_ready, u + 1)
        if u == 5:
            for t in range(NT):
                tr = pe.transpose(bank[PT][:, t * P:(t + 1) * P], prj[:, 1, t * P:(t + 1) * P], ident[:, :])
            tr.then_inc(vT_done, 1)
            return
        wait(pe, rope_done, u - 1)
        pe.matmul(bank[2 + u % 2][:, :], rot[:, :], prj[:, u % 2, :], start=True, stop=True).then_inc(rot_done, 1)

    def dve_rotate(dve, u):
        dve.wait_ge(rot_done, u + 1)
        if u == 0:
            dve.wait_ge(rope_ready, 2)
        dst = q_t[:, u, :] if u < 4 else k_t[:, :]
        r0 = 2 * u
        wait(dve, rope_done, u)
        dve.tensor_tensor(tmp2[:, 0, :], prj[:, u % 2, :], cos_t[:, :], ALU.mult).then_inc(rope_step, 1)
        dve.tensor_tensor(tmp2[:, 1, :], bank[2 + u % 2][:, :], sin_t[:, :], ALU.mult).then_inc(rope_step, 1)
        dve.wait_ge(rope_step, r0 + 2)
        dve.tensor_tensor(dst, tmp2[:, 0, :], tmp2[:, 1, :], ALU.add).then_inc(rope_done, 1)

    rope_step = sem("rope_step")
    tmp2 = cacc

    def pe_scores(pe, i):
        j, n = STEPS[i]
        if i == 0:
            pe.wait_ge(rope_done, 5)
        wait(pe, s_ready, 2 * i)
        k0 = max(n - 1, 0) * P
        keys = (n + 1) * P - k0
        for h in range(2):
            r = slice(h * HD, (h + 1) * HD)
            mm = pe.matmul(bank[SC[h]][:, 2 * P - keys:2 * P], q_t[r, j, n * P:(n + 1) * P],
                           k_t[r, k0:k0 + keys], start=True, stop=True)
        mm.then_inc(sc_done, 1)

    def key_range(n):
        return slice(P if n == 0 else 0, 2 * P)

    def dve_softmax_a(dve, i):
        j, n = STEPS[i]
        kr = key_range(n)
        s, m = s_sb[:, i % 2, :, kr], st[:, i % 2, :]
        dve.wait_ge(sc_done, i + 1)
        wait(dve, e_ready, 3 * (i - 1))
        wait(dve, probs_ready, 2 * (i - 1))
        for h in range(2):
            dve.scalar_tensor_tensor(s[:, h, :], bank[SC[h]][:, kr], HD ** -0.5, mask[:, kr],
                                     ALU.mult, ALU.add).then_inc(s_ready, 1)
        dve.wait_ge(s_ready, 2 * i + 2)
        dve.tensor_reduce(m[:, 0:2], s, AX_X, ALU.max).then_inc(stat, 1)
        dve.wait_ge(stat, 4 * i + 1)
        snk = sinks[:, j:j + 5:4]
        dve.tensor_tensor(m[:, 0:2], m[:, 0:2], snk, ALU.max).then_inc(stat, 1)
        dve.wait_ge(stat, 4 * i + 2)
        dve.tensor_scalar(m[:, 2:4], m[:, 0:2], -1.0, None, ALU.mult).then_inc(stat, 1)
        dve.tensor_tensor(m[:, 4:6], snk, m[:, 0:2], ALU.subtract).then_inc(stat, 1)

    def act_exp(act, i):
        j, n = STEPS[i]
        kr = key_range(n)
        m = st[:, i % 2, :]
        act.wait_ge(stat, 4 * i + 4)
        wait(act, pT_done, i - 1)
        for h in range(2):
            act.activation(p_sb[:, i % 2, h, kr], s_sb[:, i % 2, h, kr], ACT.Exp, bias=m[:, 2 + h:3 + h],
                           accum_out=m[:, 8 + h:9 + h]).then_inc(e_ready, 1)
        act.activation(m[:, 6:8], m[:, 4:6], ACT.Exp).then_inc(e_ready, 1)

    den_step = sem("den_step")

    def dve_softmax_b(dve, i):
        j, n = STEPS[i]
        kr = key_range(n)
        m = st[:, i % 2, :]
        dve.wait_ge(e_ready, 3 * i + 3)
        dve.tensor_tensor(m[:, 10:12], m[:, 8:10], m[:, 6:8], ALU.add).then_inc(den_step, 1)
        dve.wait_ge(den_step, 2 * i + 1)
        dve.reciprocal(m[:, 8:10], m[:, 10:12]).then_inc(den_step, 1)
        dve.wait_ge(den_step, 2 * i + 2)
        for h in range(2):
            dve.tensor_scalar(p_sb[:, i % 2, h, kr], p_sb[:, i % 2, h, kr], m[:, 8 + h:9 + h], None,
                              ALU.mult).then_inc(probs_ready, 1)

    def pe_turn_probs(pe, i):
        j, n = STEPS[i]
        pe.wait_ge(probs_ready, 2 * i + 2)
        if i == 0:
            pe.wait_ge(v_ready, 1)
        wait(pe, pT_ready, i)
        for h in range(2):
            for b in range(1 if n == 0 else 0, 2):
                s = 2 * h + b
                tr = pe.transpose(bank[PT][:, s * P:(s + 1) * P], p_sb[:, i % 2, h, b * P:(b + 1) * P], ident[:, :])
        tr.then_inc(pT_done, 1)

    def act_probs(act, i):
        j, n = STEPS[i]
        act.wait_ge(pT_done, i + 1)
        wait(act, pv_done, i - 1)
        kr = key_range(n)
        act.activation(p_t[:, i % 2, :].rearrange("p (h k) -> p h k", h=2)[:, :, kr],
                       bank[PT][:, :].rearrange("p (h k) -> p h k", h=2)[:, :, kr], ACT.Copy).then_inc(pT_ready, 1)

    def pe_values(pe, i):
        j, n = STEPS[i]
        pe.wait_ge(pT_ready, i + 1)
        if i % 2 == 0:
            wait(pe, y_ready, i // 2)
        r = slice(j % 2 * HD, (j % 2 + 1) * HD)
        for h in range(2):
            for b in range(1 if n == 0 else 0, 2):
                s = 2 * h + b
                mm = pe.matmul(bank[PV][r, h * P:(h + 1) * P], v_tok[:, n - 1 + b, h * HD:(h + 1) * HD],
                               p_t[:, i % 2, s * P:(s + 1) * P], start=b == 0 or n == 0, stop=b == 1)
        mm.then_inc(pv_done, 1)

    def act_values(act, i):
        if i % 2 == 1:
            j, n = STEPS[i]
            act.wait_ge(pv_done, i + 1)
            act.activation(y_at[:, j // 2:j // 2 + 3:2, n * P:(n + 1) * P],
                           bank[PV][:, 0:2 * P].rearrange("p (h t) -> p h t", h=2), ACT.Copy).then_inc(y_ready, 1)

    KS = (N_IN - N_PRE) * KD // len(STEPS)

    def pieces(i):
        tiles = [divmod(s, KD) for s in range(i * KS, (i + 1) * KS)]
        return [(N_PRE + u, [k for n, k in tiles if n == u]) for u in sorted({n for n, _ in tiles})]

    def ended(i):
        return [u for u, ks in pieces(i) if ks[-1] == KD - 1]

    def pe_mixer1(pe):
        for part in range(ADA_EARLY):
            ada_sums(pe, part)
        norm1.pe_sums(pe)
        for u in range(N_PRE):
            pe_in(pe, u)
            if u >= 1:
                pe_rotate(pe, u - 1)
        pe_rotate(pe, N_PRE - 1)
        pe_scores(pe, 0)
        for i in range(len(STEPS)):
            for u, ks in pieces(i):
                pe_in(pe, u, ks)
            if i + 1 < len(STEPS):
                pe_scores(pe, i + 1)
            if i:
                pe_values(pe, i - 1)
            pe_turn_probs(pe, i)
            if i in (4, 11):
                ada_sums(pe, 2 + (i > 4))
        pe_values(pe, len(STEPS) - 1)
        norm_cv.pe_sums(pe)
        norm_at.pe_sums(pe)
        for u in range(N_O):
            at = at_o[u]
            wait(pe, o_used, u - 1)
            if u < 2:
                pe.wait_ge(conv_done, 4)
            unit_products(pe, at, KD, bank[u % 2][:, :], lambda k: h_hi[:, k, :], lambda k: h_lo[:, k, :],
                          True, True, y_split_ready(pe) if u == 0 else None)
            if u in (4, 7):
                ada_sums(pe, 4 + (u > 4))

    def act_mixer1(act):
        split_hi(act, first[0])
        split_hi(act, first[1])
        norm1.act_squares(act)
        norm1.act_root(act)
        act_angles(act)
        split1.act(act)
        for u in range(N_PRE):
            act_in(act, u)
        act.wait_ge(vT_done, 1)
        act.activation(v_tok[:, :, :], bank[PT][:, :].rearrange("p (t c) -> p t c", t=NT), ACT.Copy)\
           .then_inc(v_ready, 1)
        act_exp(act, 0)
        for i in range(len(STEPS)):
            for u in ended(i):
                act_in(act, u)
            if i + 1 < len(STEPS):
                act_exp(act, i + 1)
            if i:
                act_values(act, i - 1)
            act_probs(act, i)
        act_values(act, len(STEPS) - 1)
        norm_cv.act_squares(act)
        norm_cv.act_root(act)
        split_cv.act(act)
        norm_at.act_squares(act)
        norm_at.act_root(act)
        split_at.act(act)
        for u in range(N_O):
            split_hi(act, first[N_IN + u + 2])
            ffn0.norm.act_square(act, u)

    def dve_mixer1(dve):
        dve_positions(dve)
        for m in range(ADA_EARLY * KD):
            if m == KD:
                dve_angles(dve)
            ada_accumulate(dve, m)
        split_lo(dve, first[0])
        ada_add(dve, 0)
        scaled_gain(dve, "norm1", 1)
        norm1.dve_rstd(dve)
        split_lo(dve, first[1])
        split1.dve(dve)
        for u in range(N_PRE):
            dve_in(dve, u)
            if u >= 1:
                dve_rotate(dve, u - 1)
        dve_softmax_a(dve, 0)
        dve_softmax_b(dve, 0)
        for i in range(len(STEPS)):
            for u in ended(i):
                dve_in(dve, u)
            if i + 1 < len(STEPS):
                dve_softmax_a(dve, i + 1)
                dve_softmax_b(dve, i + 1)
            if i == 6:
                ada_add(dve, 1)
        norm_cv.dve_rstd(dve)
        split_cv.dve(dve)
        norm_at.dve_rstd(dve)
        split_at.dve(dve)
        for u in range(N_O):
            split_lo(dve, first[N_IN + u + 2])
            dve.wait_ge(unit_done, at_o[u].count)
            if u == 0:
                dve.wait_ge(ada_evac, 2)
            dve.scalar_tensor_tensor(x[:, u, :], bank[u % 2][:, :], mod[:, 2 * KD + u:2 * KD + u + 1], x[:, u, :],
                                     ALU.mult, ALU.add).then_inc(o_used, 1)
        ada_add(dve, 2)
        dve.wait_ge(ada_evac, 3)

    o_used = sem("o_used")
    norm_cv = Norm(lambda k: y_cv[:, k, :], 4, lambda eng, k: eng.wait_ge(conv_done, k + 1))
    norm_at = Norm(lambda k: y_at[:, k, :], KA, lambda eng, k: eng.wait_ge(y_ready, 2 * NT))
    h_free = lambda eng: eng.wait_ge(unit_done, N_IN)
    split_cv = Split(lambda k: y_cv[:, k, :], 4, lambda k: v("gcv", k), None, lambda k: h_hi[:, KA + k, :],
                     lambda k: h_lo[:, KA + k, :], h_free)
    split_at = Split(lambda k: y_at[:, k, :], KA, lambda k: v("ga", k), None, lambda k: h_hi[:, k, :],
                     lambda k: h_lo[:, k, :], h_free)

    def y_split_ready(pe):
        return lambda k: pe.wait_ge(h_ready.sem, split_at.h0 + k + 1) if k < KA else None

    mixer1.close()

    g_copied, taps, conv_c, s_act = (count(n) for n in ("g_copied", "taps", "conv_c", "s_act"))
    ft_ready, fhi_ready, f_ready = count("ft_ready"), count("fhi_ready"), count("f_ready")
    o_ready, x_step, x_new = count("o_ready"), count("x_step"), count("x_new")
    N_UP, N_DOWN = KF // 2, KD // 2

    class Residual:

        def __init__(self, o, gains):
            self.o, self.gains = o, gains
            self.s0, self.x0 = x_step.claim(KD), x_new.claim(KD)

        def dve(self, dve):
            for k in range(KD):
                wait(dve, x_new.sem, self.x0 + k - 2)
                dve.scalar_tensor_tensor(tmp[:, k % 3, :], self.o(k), self.gains(k), rstd[:, :],
                                         ALU.mult, ALU.mult).then_inc(x_step.sem, 1)
                if k:
                    self.add(dve, k - 1)
            self.add(dve, KD - 1)

        def add(self, dve, k):
            dve.wait_ge(x_step.sem, self.s0 + k + 1)
            dve.tensor_tensor(x[:, k, :], x[:, k, :], tmp[:, k % 3, :], ALU.add).then_inc(x_new.sem, 1)

        def ready(self, eng, k):
            eng.wait_ge(x_new.sem, self.x0 + k + 1)

    class FFN:

        def __init__(self, tag, at0, x_ready_, gains, shift, w_gate, w_up, w_down, conv, out_gains, final=False):
            self.at0, self.conv, self.final = at0, conv, final
            self.w_gate, self.w_up, self.w_down = w_gate, w_up, w_down
            self.at1 = at0.plus(2 * KF)
            self.end = self.at1.plus(2 * KD)
            mem = ExitStack()
            self.f_hi = sbs(mem, f"f_hi{tag}", [P, KF, T], F32R)
            self.f_lo = sbs(mem, f"f_lo{tag}", [P, KF, T], F32R)
            if conv:
                self.gbuf = sbs(mem, "gbuf", [P, 2, T + 2])
            with ExitStack() as part:
                h_hi = sbs(part, f"fh_hi{tag}", [P, KD, T], F32R)
                h_lo = sbs(part, f"fh_lo{tag}", [P, KD, T], F32R)
            if not conv:
                self.o = sbs(mem, f"fo{tag}", [P, KD, T])
            mem.close()
            self.h_hi, self.h_lo = h_hi, h_lo
            self.norm = Norm(x_tile, KD, x_ready_)
            self.split = Split(x_tile, KD, gains, shift, lambda k: h_hi[:, k, :], lambda k: h_lo[:, k, :],
                               lambda eng: None)
            self.c0 = {c: c.claim(n) for c, n in (
                (g_copied, KF), (taps, 2 * KF), (conv_c, KF), (s_act, KF), (ft_ready, KF), (fhi_ready, KF),
                (f_ready, KF), (o_ready, KD))}
            if not conv:
                self.norm_o = Norm(lambda k: tile_at(self.o, k), KD, self.o_tile_ready)
                self.res = Residual(lambda k: self.o[:, k, :], out_gains)
                self.ready = self.res.ready
            else:
                self.ready = self.o_tile_ready
                self.norm_o = Norm(lambda k: tile_at(x, k), KD, self.o_tile_ready)
                self.out_gate = out_gains

        def o_tile_ready(self, eng, k):
            eng.wait_ge(o_ready.sem, k + (self.c0[o_ready] + 1))

        def at_up(self, i, k):
            return At(self.at0.c + k, self.at0.u + k, 4, i) if not isinstance(i, int) else self.at0.plus(4 * i + k)

        def at_down(self, i, k):
            return At(self.at1.c + k, self.at1.u + k, 4, i) if not isinstance(i, int) else self.at1.plus(4 * i + k)

        def sp(self, sp):
            def up(i, last):
                for k in range(4):
                    at = self.at_up(i, k)
                    w = (self.w_gate, self.w_up)[k % 2]
                    load(sp, at, unit_parts(at, w, (0, KD), (i * 2 * P + k // 2 * P, P)),
                         (lo_ready, at.plus(-RAW).count))

            def down(i, last):
                for k in range(4):
                    at = self.at_down(i, k)
                    load(sp, at, unit_parts(at, self.w_down, (k % 2 * HALF, HALF), (i * 2 * P + k // 2 * P, P)),
                         (lo_ready, at.plus(-RAW).count))

            loop(sp, N_UP, up)
            loop(sp, N_DOWN, down)

        def pe(self, pe):
            c = self.c0
            self.norm.pe_sums(pe)

            def up(i, last):
                for q in range(2):
                    p = i * 2 + q
                    if not isinstance(i, int) or p >= 2:
                        pe.wait_ge(ft_ready.sem, p + (c[ft_ready] - 1))
                    for g in range(2):
                        ready = self.split.pe_ready(pe) if isinstance(i, int) and i + q + g == 0 else None
                        unit_products(pe, self.at_up(i, 2 * q + g), KD, bank[2 * q + g][:, :],
                                      lambda k: self.h_hi[:, k, :], lambda k: self.h_lo[:, k, :], True, True, ready)

            def down(i, last):
                for q in range(2):
                    o = i * 2 + q
                    if not isinstance(i, int) or o >= 2:
                        pe.wait_ge(o_ready.sem, o + (c[o_ready] - 1))
                        if not self.conv:
                            pe.wait_ge(sq_ready.sem, o + (self.norm_o.sq0 - 1))
                    for g in range(2):
                        ready = None
                        if isinstance(i, int) and i + q == 0:
                            ready = lambda k, g=g: pe.wait_ge(f_ready.sem, c[f_ready] + g * HALF + k + 1)
                        unit_products(pe, self.at_down(i, 2 * q + g), HALF, bank[q][:, :],
                                      lambda k: self.f_hi[:, g * HALF + k, :], lambda k: self.f_lo[:, g * HALF + k, :],
                                      g == 0, g == 1, ready)

            loop(pe, N_UP, up)
            loop(pe, N_DOWN, down)
            self.norm_o.pe_sums(pe)

        def act(self, act):
            c = self.c0
            if not self.conv:
                self.norm.act_squares(act)
            self.norm.act_root(act)
            self.split.act(act)
            acc, ft = sq, tmp

            def up(i, last):
                kts = HALF if last else KD
                for q in range(2):
                    p = i * 2 + q
                    far = q == 1
                    gate, up_ = self.at_up(i, 2 * q), self.at_up(i, 2 * q + 1)
                    split_hi(act, gate.plus(2), HALF if last and far else KD)
                    if self.conv:
                        act.wait_ge(unit_done, gate.count)
                        if not isinstance(i, int) or p >= 2:
                            act.wait_ge(conv_c.sem, p + (c[conv_c] - 1))
                        act.activation(self.gbuf[:, q, 2:T + 2], bank[2 * q][:, :], ACT.Copy)\
                           .then_inc(g_copied.sem, 1)
                    split_hi(act, up_.plus(2), HALF if last and far else KD)
                    if self.conv:
                        act.wait_ge(conv_c.sem, p + (c[conv_c] + 1))
                        act.activation(acc[:, q, :], acc[:, q, :], ACT.Silu,
                                       bias=col_at(vecs, p + col["ffn_cb"])).then_inc(s_act.sem, 1)
                    else:
                        act.wait_ge(unit_done, gate.count)
                        if not isinstance(i, int) or p >= 2:
                            act.wait_ge(ft_ready.sem, p + (c[ft_ready] - 1))
                        act.activation(acc[:, q, :], bank[2 * q][:, :], ACT.Silu).then_inc(s_act.sem, 1)
                    act.wait_ge(ft_ready.sem, p + (c[ft_ready] + 1))
                    act.activation(tile_at(self.f_hi, p), ft[:, q, :], ACT.Copy).then_inc(fhi_ready.sem, 1)

            def down(i, last):
                for q in range(2):
                    o = i * 2 + q
                    lagging = self.conv and not (isinstance(o, int) and o == 0)
                    if lagging:
                        self.o_tile_ready(act, o - 1)
                        self.norm_o.act_slot_free(act, o - 1)
                    for g in range(2):
                        at = self.at_down(i, 2 * q + g)
                        ends = last and q == 1
                        if not (ends and self.final):
                            split_hi(act, at.plus(2), KD if ends else HALF)
                    if lagging:
                        self.norm_o.act_square_of(act, tile_at(x, o - 1), 1 - q)
                    if not self.conv:
                        act.wait_ge(unit_done, at.count)
                        act.activation(tile_at(self.o, o), bank[q][:, :], ACT.Copy).then_inc(o_ready.sem, 1)
                        self.norm_o.act_slot_free(act, o)
                        self.norm_o.act_square_of(act, bank[q][:, :], q)
                if last and self.conv:
                    self.norm_o.act_square(act, KD - 1)

            loop(act, N_UP, up)
            loop(act, N_DOWN, down)
            self.norm_o.act_root(act)

        def dve(self, dve):
            c = self.c0
            acc, ft = sq, tmp
            if self.conv:
                dve.memset(self.gbuf[:, :, 0:2], 0.0).then_inc(gpad_ready, 1)
                dve.wait_ge(gpad_ready, 1)
            self.norm.dve_rstd(dve)
            self.split.dve(dve)

            def up(i, last):
                for q in range(2):
                    p = i * 2 + q
                    later = not isinstance(i, int) or p >= 2
                    gate, up_ = self.at_up(i, 2 * q), self.at_up(i, 2 * q + 1)
                    split_lo(dve, gate.plus(2), HALF if last and q == 1 else KD)
                    if self.conv:
                        dve.wait_ge(g_copied.sem, p + (c[g_copied] + 1))
                        if later:
                            dve.wait_ge(ft_ready.sem, p + (c[ft_ready] - 1))
                        b, t0 = self.gbuf[:, q, :], p * 2 + c[taps]
                        w = lambda n: col_at(vecs, p + (col["ffn_cw"] + n * KF))
                        a = acc[:, q, :]
                        dve.tensor_scalar(a, b[:, 0:T], w(0), None, ALU.mult).then_inc(taps.sem, 1)
                        dve.wait_ge(taps.sem, t0 + 1)
                        dve.scalar_tensor_tensor(a, b[:, 1:T + 1], w(1), a, ALU.mult, ALU.add).then_inc(taps.sem, 1)
                        dve.wait_ge(taps.sem, t0 + 2)
                        dve.scalar_tensor_tensor(a, b[:, 2:T + 2], w(2), a, ALU.mult, ALU.add).then_inc(conv_c.sem, 1)
                    split_lo(dve, up_.plus(2), HALF if last and q == 1 else KD)
                    dve.wait_ge(s_act.sem, p + (c[s_act] + 1))
                    dve.wait_ge(unit_done, up_.count)
                    if later:
                        dve.wait_ge(f_ready.sem, p + (c[f_ready] - 1))
                    dve.tensor_tensor(ft[:, q, :], bank[2 * q + 1][:, :], acc[:, q, :], ALU.mult)\
                       .then_inc(ft_ready.sem, 1)
                    dve.wait_ge(fhi_ready.sem, p + (c[fhi_ready] + 1))
                    dve.tensor_tensor(tile_at(self.f_lo, p), ft[:, q, :], tile_at(self.f_hi, p).bitcast(F32),
                                      ALU.subtract).then_inc(f_ready.sem, 1)

            def down(i, last):
                for q in range(2):
                    for g in range(2):
                        at = self.at_down(i, 2 * q + g)
                        ends = last and q == 1
                        if not (ends and self.final):
                            split_lo(dve, at.plus(2), KD if ends else HALF)
                    if self.conv:
                        o = i * 2 + q
                        dve.wait_ge(unit_done, at.count)
                        dve.scalar_tensor_tensor(tile_at(x, o), bank[q][:, :], col_at(mod, o + self.out_gate),
                                                 tile_at(x, o), ALU.mult, ALU.add).then_inc(o_ready.sem, 1)

            loop(dve, N_UP, up)
            loop(dve, N_DOWN, down)
            if not self.conv:
                self.norm_o.dve_rstd(dve)
                self.res.dve(dve)

    gpad_ready = sem("gpad_ready")
    w_up0 = A["w_up"].rearrange("a k n -> (a k) n")
    ffn0 = FFN("0", At(len(seq), u_next), lambda eng, k: eng.wait_ge(o_used, k + 1),
               lambda k: gain[:, k:k + 1], mod_col(3), w_up0[:, 0:DFF], w_up0[:, DFF:2 * DFF],
               A["w_down"].rearrange("a k n -> (a k) n"), True, 5 * KD)

    norm_f = ffn0.norm_o
    x_normed = sem("x_normed")

    def dve_final(dve):
        norm_f.dve_rstd(dve)
        dve.wait_ge(std_ready.sem, norm_f.std0 + 1)
        for k in range(KD):
            dve.scalar_tensor_tensor(x[:, k, :], x[:, k, :], v("final", k), rstd[:, :], ALU.mult, ALU.mult)\
               .then_inc(x_normed, 1)

    def normed(eng, k):
        eng.wait_ge(x_normed, k + 1)

    W_LORA, A_LORA, G_LORA = A["rwkv_w1_2"].shape[2], A["rwkv_a1_2"].shape[2], A["rwkv_g1_2"].shape[2]
    G_REST = G_LORA - P
    CH, NCH = 64, T // 64
    tm = ExitStack()
    rkv = sbs(tm, "rkv", [P, 3 * KD, T])
    wa_hid = sbs(tm, "wa_hid", [P, T])
    g_hid = sbs(tm, "g_hid", [P, T])
    g_hid2 = sbs(tm, "g_hid2", [G_REST, T])
    cmask = sbs(tm, "cmask", [P, T])
    bones = sbs(tm, "bones", [P, P])
    eye2 = sbs(tm, "eye2", [P, CH])
    m_strict = sbs(tm, "m_strict", [P, P])
    m_incl = sbs(tm, "m_incl", [P, P])
    m_level = sbs(tm, "m_level", [P, 6, P])
    shift_mem = ExitStack()
    hb = sbs(shift_mem, "hb", [P, KD, T + 1])
    xx = sbs(shift_mem, "xx", [P, KD, T])
    with ExitStack() as part:
        loras = sbs(part, "loras", [P, KD, W_LORA + A_LORA + G_LORA])
    xs_hi = sbs(shift_mem, "xs_hi", [P, KD, T], F32R)
    xs_lo = sbs(shift_mem, "xs_lo", [P, KD, T], F32R)
    shift_mem.close()
    w1, a1, g1 = (loras[:, :, s:s + n] for s, n in (
        (0, W_LORA), (W_LORA, A_LORA), (W_LORA + A_LORA, G_LORA)))
    assert W_LORA == A_LORA == HD

    loras_landed, h2_ready, xx_ready = sem("loras_landed"), sem("h2_ready"), sem("xx_ready")
    mixed, lora_used, hid_ready = sem("mixed"), sem("lora_used"), sem("hid_ready")
    xs_mixed, xs_hi_ready, xs_ready, rkv_ready = (sem(n) for n in ("xs_mixed", "xs_hi_ready", "xs_ready", "rkv_ready"))
    norm_tm = Norm(x_tile, KD, normed)
    LORA_MIX = (3, 4, 5)
    at_rkv0 = ffn0.end
    w_rkv = A["rwkv_w_rkv_2"].rearrange("a c k n -> (a c k) n")

    def at_rkv(p, o):
        return at_rkv0.plus(8 * p + o) if isinstance(p, int) else At(at_rkv0.c + o, at_rkv0.u + o, KD, p)

    def over_projections(eng, body):
        body(0)
        with eng.Fori(1, 3) as p:
            body(p)

    def sp_time_mix(sp):
        def body(p, outs=range(KD)):
            for o in outs:
                at = at_rkv(p, o)
                if isinstance(p, int):
                    src = w_rkv[p * D:(p + 1) * D, o * P:(o + 1) * P].rearrange("(k p) n -> p k n", p=P)
                else:
                    src = w_rkv[bass.ds(p * D, D), o * P:(o + 1) * P].rearrange("(k p) n -> p k n", p=P)
                load(sp, at, [(raw[:, at.raw_slot, 0:KD * P].rearrange("p (k n) -> p k n", n=P), src)],
                     (lo_ready, at.plus(-RAW).count))

        body(0, range(RAW))
        sp.wait_ge(f_ready.sem, ffn0.c0[f_ready] + KF)
        sp.wait_ge(unit_done, ffn0.end.u)
        for src, dst in ((A["rwkv_w1_2"], w1), (A["rwkv_a1_2"], a1), (A["rwkv_g1_2"], g1)):
            sp.dma_start(dst, src.rearrange("a (k p) n -> p (a k) n", p=P)).then_inc(loras_landed, 16)
        body(0, range(RAW, KD))
        with sp.Fori(1, 3) as p:
            body(p)

    def dve_time_mix(dve):
        dve.memset(hb[:, :, 0:1], 0.0).then_inc(h2_ready, 1)
        norm_tm.dve_rstd(dve)
        for k in range(KD):
            dve.scalar_tensor_tensor(hb[:, k, 1:T + 1], x[:, k, :], v("gains", k), rstd[:, :], ALU.mult, ALU.mult)\
               .then_inc(h2_ready, 1)
            dve.wait_ge(h2_ready, k + 2)
            dve.tensor_tensor(xx[:, k, :], hb[:, k, 0:T], hb[:, k, 1:T + 1], ALU.subtract).then_inc(xx_ready, 1)
        for n, m in enumerate(LORA_MIX):
            for k in range(KD):
                s = n * KD + k
                dve.wait_ge(xx_ready, min(KD, s + 1))
                wait(dve, lora_used, s - 2)
                dve.scalar_tensor_tensor(tmp[:, s % 3, :], xx[:, k, :], v("mix", m * KD + k), hb[:, k, 1:T + 1],
                                         ALU.mult, ALU.add).then_inc(mixed, 1)

        def body(p):
            def lower(k):
                dve.wait_ge(xs_hi_ready, p * KD + (k + 1))
                dve.tensor_tensor(xs_lo[:, k, :], tmp[:, k % 2, :], xs_hi[:, k, :].bitcast(F32), ALU.subtract)\
                   .then_inc(xs_ready, 1)

            if isinstance(p, int):
                dve.wait_ge(lora_used, 3 * KD)
            dve.wait_ge(unit_done, at_rkv(p, 0).plus(-1).count)
            for k in range(KD):
                if not isinstance(p, int) or k >= 2:
                    dve.wait_ge(xs_ready, p * KD + (k - 1))
                dve.scalar_tensor_tensor(tmp[:, k % 2, :], xx[:, k, :], col_at(vecs, p * KD + (col["mix"] + k)),
                                         hb[:, k, 1:T + 1], ALU.mult, ALU.add).then_inc(xs_mixed, 1)
                if k:
                    dve.wait_ge(xs_mixed, p * KD + k)
                    lower(k - 1)
            dve.wait_ge(xs_mixed, p * KD + KD)
            lower(KD - 1)
            for o in range(KD):
                split_lo(dve, at_rkv(p, o).plus(2))

        over_projections(dve, body)

    def act_time_mix(act):
        norm_tm.act_squares(act)
        norm_tm.act_root(act)
        act.wait_ge(lora_used, KD)
        act.activation(wa_hid[0:HD, :], bank[0][0:HD, :], ACT.Tanh).then_inc(hid_ready, 1)
        act.wait_ge(lora_used, 2 * KD)
        act.activation(wa_hid[HD:P, :], bank[1][HD:P, :], ACT.Copy).then_inc(hid_ready, 1)
        act.wait_ge(lora_used, 3 * KD)
        act.activation(g_hid[:, :], bank[2][:, :], ACT.Sigmoid).then_inc(hid_ready, 1)
        act.activation(g_hid2[:, :], bank[3][0:G_REST, :], ACT.Sigmoid).then_inc(hid_ready, 1)

        def body(p):
            act.wait_ge(unit_done, at_rkv(p, 0).plus(-1).count)
            for k in range(KD):
                act.wait_ge(xs_mixed, p * KD + (k + 1))
                act.activation(xs_hi[:, k, :], tmp[:, k % 2, :], ACT.Copy).then_inc(xs_hi_ready, 1)
            for o in range(KD):
                split_hi(act, at_rkv(p, o).plus(2))
                act.wait_ge(unit_done, at_rkv(p, o).count)
                act.activation(tile_at(rkv, p * KD + o), bank[4 + o % 2][:, :], ACT.Copy).then_inc(rkv_ready, 1)

        over_projections(act, body)

    def pe_time_mix(pe):
        norm_tm.pe_sums(pe)
        pe.wait_ge(loras_landed, 48)
        for n, parts in enumerate((((bank[0][0:W_LORA, :], w1),), ((bank[1][HD:P, :], a1),),
                                   ((bank[2][:, :], g1[:, :, 0:P]), (bank[3][0:G_REST, :], g1[:, :, P:G_LORA])))):
            for k in range(KD):
                s = n * KD + k
                pe.wait_ge(mixed, s + 1)
                for dst, w in parts:
                    mm = pe.matmul(dst, w[:, k, :], tmp[:, s % 3, :], start=k == 0, stop=k == KD - 1)
                mm.then_inc(lora_used, 1)

        def body(p):
            for o in range(KD):
                at = at_rkv(p, o)
                if not isinstance(p, int) or o >= 2:
                    pe.wait_ge(rkv_ready, p * KD + (o - 1))
                unit_products(pe, at, KD, bank[4 + o % 2][:, :], lambda k: xs_hi[:, k, :], lambda k: xs_lo[:, k, :],
                              True, True, (lambda k: pe.wait_ge(xs_ready, p * KD + (k + 1))) if o == 0 else None)

        over_projections(pe, body)

    GN_EPS = 64e-5
    DECAY = -float(np.exp(-0.5))
    LEVELS = (2, 4, 8, 16, 32)
    bm = ExitStack()
    lw = sbs(bm, "lw", [P, P])
    lg = sbs(bm, "lg", [P, 2, P])
    L_t = sbs(bm, "L_t", [P, T])
    E_t = sbs(bm, "E_t", [P, T])
    y_sb = sbs(bm, "y_sb", [P, T])
    ends = sbs(bm, "ends", [P, NCH])
    nk_sb = sbs(bm, "nk_sb", [P, 2 * NT])
    ng_sb = sbs(bm, "ng_sb", [P, 2 * NT])
    AR = sbs(bm, "AR", [P, NT, 2, P])
    B_t = sbs(bm, "B_t", [P, T])
    K_t = sbs(bm, "K_t", [P, T])
    AU = sbs(bm, "AU", [P, NT, 2, P])
    B_k = sbs(bm, "B_k", [P, NT, P])
    K_k = sbs(bm, "K_k", [P, NT, P])
    V_k = sbs(bm, "V_k", [P, NT, P])
    MT = sbs(bm, "MT", [P, 2, NT, P])
    MTb = sbs(bm, "MTb", [P, 2, NT, P])
    XT = sbs(bm, "XT", [P, 2, NT, P])
    X = sbs(bm, "X", [P, 2, NT, P])
    Z = sbs(bm, "Z", [P, 2, NT, P])
    RB = sbs(bm, "RB", [P, 2, NT, P])
    AK = sbs(bm, "AK", [P, 2, NT, P])
    RK = sbs(bm, "RK", [P, 2, NT, P])
    XAU = Z
    GT = sbs(bm, "GT", [P, NCH, 2, CH])
    HP = sbs(bm, "HP", [P, NCH, CH])
    RH = sbs(bm, "RH", [P, T])
    S = sbs(bm, "S", [P, NCH, CH])
    bm.close()

    class Round:

        def __init__(self, i, off=0):
            self.i, self.off = i, off

        def plus(self, n):
            return self.i + (self.off + n)

    class Steps:

        def __init__(self, sem_name, names):
            self.sem, self.names, self.seen = sem(sem_name), names.split(), 0

        def done(self, ins, name):
            ins.then_inc(self.sem, 1)
            assert name == self.names[self.seen % len(self.names)], (name, self.names[self.seen % len(self.names)])
            self.seen += 1

        def wait(self, eng, j, name, before=0):
            n = (j.off - before) * len(self.names) + self.names.index(name) + 1
            wait(eng, self.sem, j.i * len(self.names) + n)

    masks_ready, lw_landed, lg_landed = sem("masks_ready"), sem("lw_landed"), sem("lg_landed")
    turned = "tA tB tK tV"
    PEa = Steps("pe_pre", f"lora kk_sum kk_bc bonus_sum {turned} " + " ".join(f"m{n}" for n in range(6)) + " x0 x1 m6 m7")
    PEb = Steps("pe_core", " ".join(f"z{b}_0 z{b}_1 xt{b}_0 xt{b}_1" + ("" if b == 32 else f" x{b}_0 x{b}_1")
                                    for b in LEVELS)
                + " u0 u1 xau0 xau1 gh rh " + " ".join(f"s{c}" for c in range(1, NCH - 1)) + " y")
    PEc = Steps("pe_post", "mean var bc g")
    ACTa = Steps("act_pre", "sg a kk2 eE eN eL root ktB ktV x0 x1")
    ACTb = Steps("act_core", " ".join(f"z{b}_0 z{b}_1" + ("" if b == 32 else f" x{b}_0 x{b}_1") for b in LEVELS)
                 + " u0 u1 xau0 xau1 y")
    ACTc = Steps("act_post", "d2 root")
    DVEa = Steps("dve_pre", "kk scan E u kp nk rn spread kkn t2 bon AT BT KT bonus RT tA tK "
                 + " ".join(f"e{n}a e{n}b" for n in range(4)) + " l0 l1 xt0 xt1 "
                + " ".join(f"e{n}a e{n}b" for n in range(4, 8)))
    DVEb = Steps("dve_core", " ".join(f"xt{b}_0 xt{b}_1" for b in LEVELS)
                 + " gt00 gt01 gt10 gt11 hp0 hp1 rh0 rh1 S1 " + " ".join(f"S{c}" for c in range(2, NCH)))
    DVEc = Steps("dve_post", "d gvar grstd spread yn yb y")
    POOLa, POOLb = Steps("pool_pre", "v"), Steps("pool_core", " ".join(f"m{b}_0 m{b}_1" for b in LEVELS))
    sg, a_, kk = tmp[:, 0, :], tmp[:, 1, :], tmp[:, 2, :]
    kk2, eN = sq[:, 0, :], sq[:, 1, :]
    d2, kp, v_c = var[:, :], rstd[:, :], sq_sum
    w2, a2, g2 = (A[n].rearrange("a k n -> (a k) n") for n in ("rwkv_w2_2", "rwkv_a2_2", "rwkv_g2_2"))

    def pool_masks(pool):
        pool.wait_ge(unit_done, ffn0.end.u)
        n = [0]

        def step(ins):
            ins.then_inc(masks_ready, 1)
            n[0] += 1
            pool.wait_ge(masks_ready, n[0])

        step(pool.memset(cmask[:, :], 1.0))
        step(pool.memset(cmask[:, :].rearrange("p (c t) -> p c t", t=CH)[:, :, 0:1], 0.0))
        step(pool.memset(bones[:, :], 0.0))
        step(pool.memset(bones[0:HD, 0:HD], 1.0))
        step(pool.memset(bones[HD:P, HD:P], 1.0))
        step(pool.tensor_copy(eye2[0:HD, :], ident[0:HD, 0:HD]))
        step(pool.tensor_copy(eye2[HD:P, :], ident[HD:P, HD:P]))
        step(pool.affine_select(out=m_strict[:, :], in_=bones[:, :], compare_op=ALU.is_gt, fill=0.0, base=0,
                                pattern=[[1, P]], channel_multiplier=-1))
        step(pool.affine_select(out=m_incl[:, :], in_=bones[:, :], compare_op=ALU.is_ge, fill=0.0, base=0,
                                pattern=[[1, P]], channel_multiplier=-1))
        for n_, b in enumerate((1,) + LEVELS):
            m = m_level[:, n_, :].rearrange("p (g h t) -> p g h t", h=2, t=b)
            step(pool.memset(m_level[:, n_, :], 0.0))
            step(pool.memset(m[:, :, 1, :], 1.0))
            step(pool.affine_select(out=m[:, :, 1, :], in_=m[:, :, 1, :], compare_op=ALU.is_ge, fill=0.0, base=0,
                                    pattern=[[-2 * b, P // (2 * b)], [0, b]], channel_multiplier=1))
            step(pool.affine_select(out=m[:, :, 1, :], in_=m[:, :, 1, :], compare_op=ALU.is_ge, fill=0.0, base=b - 1,
                                    pattern=[[2 * b, P // (2 * b)], [0, b]], channel_multiplier=-1))

    MASKS = 9 + 4 * 6

    REGION_FREE = lambda eng: eng.wait_ge(unit_done, at_rkv(2, KD - 1).count)

    def over_tiles(eng, body):
        body(Round(0), False, True)
        with eng.Fori(1, KD - 1) as j:
            body(Round(j), True, True)
        body(Round(KD - 1), True, False)

    def r_k_v(j):
        return tile_at(rkv, j.plus(0)), tile_at(rkv, j.plus(KD)), tile_at(rkv, j.plus(2 * KD))

    def nxt(j):
        return Round(j.i, j.off + 1)

    def prv(j):
        return Round(j.i, j.off - 1)

    by_tile = lambda t_: t_.rearrange("p (t c) -> p t c", t=NT)
    bank4 = lambda b: by_tile(bank[b][:, :])
    hr = [slice(0, HD), slice(HD, P)]
    M_BANK = (2, 3, 4, 5, 0, 1, 2, 3)

    def sp_blocks(sp):
        def low(j):
            PEa.wait(sp, j, "lora", before=1)
            for w, dst in ((w2, lw[0:HD, :]), (a2, lw[HD:P, :])):
                sp.dma_start(dst, cols_at(w, j.plus(0) * P, P)).then_inc(lw_landed, 16)

        def body(j, before, after):
            if after:
                low(nxt(j))
            PEc.wait(sp, j, "g", before=1)
            for r0, r1, n in ((0, P, 0), (P, G_LORA, 1)):
                sp.dma_start(lg[0:r1 - r0, n, :], cols_at(g2[r0:r1, :], j.plus(0) * P, P)).then_inc(lg_landed, 16)

        REGION_FREE(sp)
        low(Round(0))
        over_tiles(sp, body)

    def pool_blocks(pool):
        REGION_FREE(pool)
        pool.wait_ge(rkv_ready, 3 * KD)

        def pre(j):
            PEa.wait(pool, j, "tV", before=1)
            POOLa.done(pool.tensor_copy(v_c[:, :], r_k_v(j)[2]), "v")

        def body(j, before, after):
            if after:
                pre(nxt(j))
            for n, b in enumerate(LEVELS):
                for e in range(2):
                    if n == 0:
                        DVEa.wait(pool, j, "e3b")
                        PEb.wait(pool, j, f"z32_{e}", before=1)
                    else:
                        PEb.wait(pool, j, f"z{LEVELS[n - 1]}_{e}")
                    POOLb.done(pool.tensor_tensor(MTb[:, e, :, :], MT[:, e, :, :],
                                                  m_level[:, n + 1:n + 2, :].to_broadcast([P, NT, P]), ALU.mult),
                               f"m{b}_{e}")

        pre(Round(0))
        over_tiles(pool, body)

    def act_sigmoids(act, j):
        PEa.wait(act, j, "lora")
        for out, b, name, c in ((sg, 6, "sg", "w0"), (a_, 7, "a", "a0")):
            DVEa.wait(act, j, "t2" if name == "sg" else "t2", before=1)
            ACTa.done(act.activation(out, bank[b][:, :], ACT.Sigmoid, bias=col_at(vecs, j.plus(col[c]))), name)
        DVEa.wait(act, j, "kk")
        PEa.wait(act, j, "bonus_sum", before=1)
        ACTa.done(act.activation(kk2, kk, ACT.Square), "kk2")

    def act_exps(act, j):
        DVEa.wait(act, j, "E")
        DVEa.wait(act, j, "KT", before=1)
        for out, src, scale, name in ((E_t[:, :], E_t[:, :], DECAY, "eE"), (eN, L_t[:, :], -DECAY, "eN"),
                                      (L_t[:, :], L_t[:, :], DECAY, "eL")):
            if name == "eL":
                ACTa.wait(act, j, "eN")
            ACTa.done(act.activation(out, src, ACT.Exp, scale=scale), name)

    def act_pre_root(act, j):
        DVEa.wait(act, j, "nk")
        ACTa.done(act.activation(nk_sb[:, :], nk_sb[:, :], ACT.Sqrt), "root")

    def act_turned(act, j):
        PEa.wait(act, j, "tB")
        ACTa.done(act.activation(B_k[:, :, :], bank4(5), ACT.Copy), "ktB")
        PEa.wait(act, j, "tV")
        ACTa.done(act.activation(V_k[:, :, :], bank4(1), ACT.Copy), "ktV")

    def act_x0(act, j):
        for e in range(2):
            PEa.wait(act, j, f"x{e}")
            ACTa.done(act.activation(X[:, e, :, :], bank4(4 + e), ACT.Copy), f"x{e}")

    def act_z(act, j, b):
        for e in range(2):
            PEb.wait(act, j, f"z{b}_{e}")
            ACTb.done(act.activation(Z[:, e, :, :], bank4(e), ACT.Copy), f"z{b}_{e}")

    def act_x(act, j, b):
        for e in range(2):
            PEb.wait(act, j, f"x{b}_{e}")
            ACTb.done(act.activation(X[:, e, :, :], bank4(4 + e), ACT.Copy), f"x{b}_{e}")

    def act_post_square(act, j):
        DVEc.wait(act, j, "d")
        ACTc.done(act.activation(d2, y_sb[:, :], ACT.Square), "d2")

    def act_post_root(act, j):
        DVEc.wait(act, j, "gvar")
        ACTc.done(act.activation(ng_sb[:, :], ng_sb[:, :], ACT.Sqrt), "root")

    def act_blocks(act):
        def body(j, before, after):
            act_z(act, j, 2)
            if after:
                act_sigmoids(act, nxt(j))
            act_x(act, j, 2)
            act_z(act, j, 4)
            if after:
                act_exps(act, nxt(j))
            act_x(act, j, 4)
            if before:
                act_post_square(act, prv(j))
            act_z(act, j, 8)
            if after:
                act_pre_root(act, nxt(j))
            act_x(act, j, 8)
            if before:
                act_post_root(act, prv(j))
            act_z(act, j, 16)
            act_x(act, j, 16)
            act_z(act, j, 32)
            for e in range(2):
                PEb.wait(act, j, f"u{e}")
                ACTb.done(act.activation(AU[:, :, e, CH:P], by_tile(bank[4 + e][:, 0:NT * CH]), ACT.Copy), f"u{e}")
            for e in range(2):
                PEb.wait(act, j, f"xau{e}")
                ACTb.done(act.activation(XAU[:, e, :, :], bank4(e), ACT.Copy), f"xau{e}")
            if after:
                act_turned(act, nxt(j))
            PEb.wait(act, j, "y")
            DVEc.wait(act, j, "y", before=1)
            ACTb.done(act.activation(y_sb[:, :], bank[6][:, :], ACT.Copy), "y")
            if after:
                act_x0(act, nxt(j))

        first_ = Round(0)
        act_sigmoids(act, first_)
        act_exps(act, first_)
        act_pre_root(act, first_)
        act_turned(act, first_)
        act_x0(act, first_)
        over_tiles(act, body)
        act_post_square(act, Round(KD - 1))
        act_post_root(act, Round(KD - 1))

    by_head = lambda t_: t_.rearrange("p (n c) -> p n c", c=HD)
    over_head = lambda t_: t_[:, :].rearrange("p (n o) -> p n o", o=1).to_broadcast([P, 2 * NT, HD])

    def dve_kk(dve, j):
        DVEa.done(dve.tensor_scalar(kk, r_k_v(j)[1], col_at(vecs, j.plus(col["k_k"])), None, ALU.mult), "kk")

    def dve_decay(dve, j):
        ACTa.wait(dve, j, "sg")
        DVEa.done(dve.tensor_tensor_scan(L_t[:, :], cmask[:, :], sg, 0.0, ALU.mult, ALU.add), "scan")
        DVEa.wait(dve, j, "scan")
        DVEa.done(dve.tensor_tensor(E_t[:, :], L_t[:, :], sg, ALU.subtract), "E")
        ACTa.wait(dve, j, "a")
        DVEa.done(dve.tensor_scalar(kp, a_, 1.0, col_at(vecs, j.plus(col["k_a"])), ALU.subtract, ALU.mult), "u")
        DVEa.wait(dve, j, "u")
        DVEa.done(dve.scalar_tensor_tensor(kp, kp, 1.0, r_k_v(j)[1], ALU.add, ALU.mult), "kp")

    def dve_kk_square(dve, j):
        PEa.wait(dve, j, "kk_sum")
        DVEa.done(dve.tensor_scalar(nk_sb[:, :], bank[7][:, 0:2 * NT], 1e-24, None, ALU.max), "nk")

    def dve_kk_rstd(dve, j):
        ACTa.wait(dve, j, "root")
        DVEa.done(dve.reciprocal(nk_sb[:, :], nk_sb[:, :]), "rn")
        DVEa.wait(dve, j, "rn")
        DVEa.done(dve.tensor_copy(by_head(sg), over_head(nk_sb)), "spread")

    def dve_normed(dve, j):
        PEa.wait(dve, j, "kk_bc")
        DVEa.done(dve.tensor_tensor(kk, kk, bank[7][:, :], ALU.mult), "kkn")
        DVEa.wait(dve, j, "kkn")
        DVEa.done(dve.tensor_tensor(sg, kk, a_, ALU.mult), "t2")
        PEa.wait(dve, j, "kk_sum")
        DVEa.done(dve.scalar_tensor_tensor(kk2, r_k_v(j)[0], col_at(vecs, j.plus(col["r_k"])), kp,
                                           ALU.mult, ALU.mult), "bon")

    def dve_scaled(dve, j):
        ACTa.wait(dve, j, "eL")
        DVEa.done(dve.scalar_tensor_tensor(AR[:, :, 0, :], by_tile(kk), -1.0, by_tile(E_t[:, :]),
                                           ALU.mult, ALU.mult), "AT")
        DVEa.wait(dve, j, "t2")
        DVEa.done(dve.tensor_tensor(B_t[:, :], sg, eN, ALU.mult), "BT")
        DVEa.done(dve.tensor_tensor(K_t[:, :], kp, eN, ALU.mult), "KT")

    def dve_bonus(dve, j):
        v = r_k_v(j)[2]
        PEa.wait(dve, j, "bonus_sum")
        POOLa.wait(dve, j, "v")
        DVEa.done(dve.tensor_tensor(v, bank[7][:, :], v, ALU.mult), "bonus")

    def dve_r(dve, j):
        DVEa.done(dve.tensor_tensor(AR[:, :, 1, :], by_tile(r_k_v(j)[0]), by_tile(L_t[:, :]), ALU.mult), "RT")

    def dve_turned(dve, j, name):
        PEa.wait(dve, j, name)
        if name == "tA":
            ins = dve.tensor_copy(AU[:, :, :, 0:CH], bank[4][:, :].rearrange("p (t e c) -> p t e c", t=NT, e=2))
        else:
            ins = dve.tensor_copy(K_k[:, :, :], bank4(0))
        DVEa.done(ins, name)

    def dve_masked(dve, j, ns):
        for n in ns:
            of_b, e, pair = n < 4, n // 2 % 2, n % 2
            PEa.wait(dve, j, f"m{n}")
            two = bank[M_BANK[n]][:, :].rearrange("p (t h c) -> p t h c", t=2, h=2)
            ts = slice(2 * pair, 2 * pair + 2)
            for h, dst, m, name in ((0, MT if of_b else AK, m_strict, "a"), (1, RB if of_b else RK, m_incl, "b")):
                DVEa.done(dve.tensor_tensor(dst[:, e, ts, :], two[:, :, h, :],
                                            m[:, :].rearrange("p (o c) -> p o c", o=1).to_broadcast([P, 2, P]),
                                            ALU.mult), f"e{n}{name}")

    def dve_level1(dve, j):
        DVEa.wait(dve, j, "e3b")
        for e in range(2):
            DVEa.done(dve.tensor_tensor(XT[:, e, :, :], MT[:, e, :, :], m_level[:, 0:1, :].to_broadcast([P, NT, P]),
                                        ALU.mult), f"l{e}")
        for e in range(2):
            DVEa.wait(dve, j, f"l{e}")
            DVEa.done(dve.tensor_tensor(XT[:, e, :, :], XT[:, e, :, :],
                                        ident[:, :].rearrange("p (o c) -> p o c", o=1).to_broadcast([P, NT, P]),
                                        ALU.add), f"xt{e}")

    def dve_xt(dve, j, b):
        for e in range(2):
            PEb.wait(dve, j, f"xt{b}_{e}")
            DVEb.done(dve.tensor_tensor(XT[:, e, :, :], bank4(2 + e), XT[:, e, :, :], ALU.add), f"xt{b}_{e}")

    def dve_post_centre(dve, j):
        PEc.wait(dve, j, "mean")
        DVEc.done(dve.scalar_tensor_tensor(y_sb[:, :], bank[6][:, :], -1.0 / HD, y_sb[:, :], ALU.mult, ALU.add), "d")

    def dve_post_var(dve, j):
        PEc.wait(dve, j, "var")
        DVEc.done(dve.tensor_scalar(ng_sb[:, :], bank[6][:, 0:2 * NT], 1.0 / HD, GN_EPS, ALU.mult, ALU.add), "gvar")

    def dve_post_rstd(dve, j):
        ACTc.wait(dve, j, "root")
        DVEc.done(dve.reciprocal(ng_sb[:, :], ng_sb[:, :]), "grstd")
        DVEc.wait(dve, j, "grstd")
        DVEc.done(dve.tensor_copy(by_head(d2), over_head(ng_sb)), "spread")

    def dve_post_norm(dve, j):
        PEc.wait(dve, j, "bc")
        vc = lambda name: col_at(vecs, j.plus(col[name]))
        DVEc.done(dve.scalar_tensor_tensor(y_sb[:, :], y_sb[:, :], vc("gn_w"), bank[6][:, :], ALU.mult, ALU.mult), "yn")
        DVEc.wait(dve, j, "yn")
        DVEc.done(dve.scalar_tensor_tensor(y_sb[:, :], y_sb[:, :], vc("gn_b"), r_k_v(j)[2], ALU.add, ALU.add), "yb")

    def dve_post_gate(dve, j):
        PEc.wait(dve, j, "g")
        DVEc.wait(dve, j, "yb")
        DVEc.done(dve.tensor_tensor(r_k_v(j)[0], y_sb[:, :], bank[6][:, :], ALU.mult), "y")

    def dve_ends(dve, j):
        ACTa.wait(dve, j, "eL")
        DVEb.wait(dve, j, f"S{NCH - 1}", before=1)
        dve.tensor_copy(ends[:, :], L_t[:, :].rearrange("q (c t) -> q c t", c=NCH)[:, :, CH - 1])\
           .then_inc(ends_ready, 1)

    def dve_blocks(dve):
        def body(j, before, after):
            if after:
                dve_kk(dve, nxt(j))
            dve_xt(dve, j, 2)
            if after:
                dve_decay(dve, nxt(j))
            if before:
                dve_post_centre(dve, prv(j))
            dve_xt(dve, j, 4)
            if after:
                dve_kk_square(dve, nxt(j))
            dve_xt(dve, j, 8)
            if before:
                dve_post_var(dve, prv(j))
            if after:
                dve_kk_rstd(dve, nxt(j))
            if before:
                dve_post_rstd(dve, prv(j))
            dve_xt(dve, j, 16)
            if after:
                dve_normed(dve, nxt(j))
            if before:
                dve_post_norm(dve, prv(j))
            dve_xt(dve, j, 32)
            if after:
                dve_scaled(dve, nxt(j))
            if before:
                dve_post_gate(dve, prv(j))
            if after:
                dve_bonus(dve, nxt(j))
            half = lambda t_, p_: t_[:, :, :].rearrange("q (t p) c -> q t p c", p=2)[:, :, p_, :]
            PEb.wait(dve, j, "gh")
            for p_ in range(2):
                for e in range(2):
                    q = hr[e]
                    eye = eye2[q, :].rearrange("p (o c) -> p o c", o=1).to_broadcast([HD, NT, CH])
                    DVEb.done(dve.tensor_tensor(GT[q, :, e, :].rearrange("q (t p) c -> q t p c", p=2)[:, :, p_, :],
                                                by_tile(bank[p_][q, 0:NT * CH]), eye, ALU.add), f"gt{p_}{e}")
            dve.wait_ge(ends_ready, j.plus(1))
            for p_ in range(2):
                e_ = ends[:, :].rearrange("q (t p o) -> q t p o", p=2, o=1)[:, :, p_, :]
                DVEb.done(dve.tensor_tensor(half(HP, p_), by_tile(bank[p_][:, NT * CH:]),
                                            e_.to_broadcast([P, NT, CH]), ALU.mult), f"hp{p_}")
            PEb.wait(dve, j, "rh")
            for p_ in range(2):
                cols = slice(p_ * CH, (p_ + 1) * CH)
                DVEb.done(dve.tensor_tensor(by_tile(RH[:, :])[:, :, cols], by_tile(bank[2 + p_][:, 0:NT * CH]),
                                            AR[:, :, 1, cols], ALU.add), f"rh{p_}")
            DVEb.wait(dve, j, "hp1")
            DVEb.done(dve.tensor_copy(S[:, 1, :], HP[:, 0, :]), "S1")
            DVEb.wait(dve, j, "rh1")
            if after:
                dve_r(dve, nxt(j))
            for c in range(1, NCH - 1):
                PEb.wait(dve, j, f"s{c}")
                DVEb.done(dve.scalar_tensor_tensor(S[:, c + 1, :], bank[7][:, 0:CH], ends[:, c:c + 1], HP[:, c, :],
                                                   ALU.mult, ALU.add), f"S{c + 1}")
                if after:
                    if c == 1:
                        dve_turned(dve, nxt(j), "tA")
                    elif c == 2:
                        dve_turned(dve, nxt(j), "tK")
                    elif c < NCH - 2:
                        dve_masked(dve, nxt(j), {3: (0,), 4: (1,), 5: (2, 3)}[c])
            if after:
                dve_ends(dve, nxt(j))
                dve_level1(dve, nxt(j))
                dve_masked(dve, nxt(j), (4, 5, 6, 7))

        dve.wait_ge(masks_ready, MASKS)
        REGION_FREE(dve)
        dve.wait_ge(rkv_ready, 3 * KD)
        dve.memset(GT[:, :, :, :], 0.0).then_inc(gt_zero, 1)
        dve.wait_ge(gt_zero, 1)
        j = Round(0)
        dve_kk(dve, j)
        dve_decay(dve, j)
        dve_kk_square(dve, j)
        dve_kk_rstd(dve, j)
        dve_normed(dve, j)
        dve_scaled(dve, j)
        dve_bonus(dve, j)
        dve_r(dve, j)
        dve_turned(dve, j, "tA")
        dve_turned(dve, j, "tK")
        dve_ends(dve, j)
        dve_masked(dve, j, range(4))
        dve_level1(dve, j)
        dve_masked(dve, j, range(4, 8))
        over_tiles(dve, body)
        j = Round(KD - 1)
        dve_post_centre(dve, j)
        dve_post_var(dve, j)
        dve_post_rstd(dve, j)
        dve_post_norm(dve, j)
        dve_post_gate(dve, j)

    ends_ready, gt_zero = sem("ends_ready"), sem("gt_zero")

    def pe_low(pe, j):
        ACTb.wait(pe, j, "y", before=2)
        DVEb.wait(pe, j, f"S{NCH - 1}", before=2)
        wait(pe, lw_landed, j.plus(1) * 32)
        pe.matmul(bank[6][:, :], lw[0:HD, :], wa_hid[0:HD, :], start=True, stop=True)
        PEa.done(pe.matmul(bank[7][:, :], lw[HD:P, :], wa_hid[HD:P, :], start=True, stop=True), "lora")

    def pe_head_sums(pe, b, src):
        for t in range(NT):
            mm = pe.matmul(bank[b][:, 2 * t:2 * t + 2], src[:, t * P:(t + 1) * P], bones[:, 0:P:HD], start=True, stop=True)
        return mm

    def pe_head_spread(pe, b, src):
        for t in range(NT):
            mm = pe.matmul(bank[b][:, t * P:(t + 1) * P], src[:, t * P:(t + 1) * P], ident[:, :],
                           start=True, stop=True)
        return mm

    def pe_kk_sum(pe, j):
        ACTa.wait(pe, j, "kk2")
        PEa.done(pe_head_sums(pe, 7, kk2), "kk_sum")

    def pe_kk_spread(pe, j):
        DVEa.wait(pe, j, "spread")
        PEa.done(pe_head_spread(pe, 7, sg), "kk_bc")

    def pe_bonus(pe, j):
        DVEa.wait(pe, j, "bon")
        PEa.done(pe.matmul(bank[7][:, :], bones[:, :], kk2, start=True, stop=True), "bonus_sum")

    def pe_turn(pe, b, src):
        for t in range(NT):
            tr = pe.transpose(bank[b][:, t * P:(t + 1) * P], src(t), ident[:, :])
        return tr

    def pe_turn_ab(pe, j):
        DVEa.wait(pe, j, "KT")
        ACTb.wait(pe, j, "u1", before=1)
        PEa.done(pe_turn(pe, 4, lambda t: AR[:, t, 0, :]), "tA")
        PEa.done(pe_turn(pe, 5, lambda t: B_t[:, t * P:(t + 1) * P]), "tB")

    def pe_turn_kv(pe, j):
        DVEb.wait(pe, j, "hp1", before=1)
        POOLa.wait(pe, j, "v")
        PEa.done(pe_turn(pe, 0, lambda t: K_t[:, t * P:(t + 1) * P]), "tK")
        PEa.done(pe_turn(pe, 1, lambda t: v_c[:, t * P:(t + 1) * P]), "tV")

    def pe_products(pe, j, ns):
        for n in ns:
            of_b, e, pair = n < 4, n // 2 % 2, n % 2
            if n == 0:
                DVEa.wait(pe, j, "RT")
                DVEb.wait(pe, j, "rh1", before=1)
            engine, name = ((None, None), (None, None), (DVEa, "tA"), (ACTa, "ktB"), (DVEa, "tK"), (ACTa, "ktV"),
                            (DVEa, "e0b"), (DVEa, "e1b"))[n]
            if engine is not None:
                engine.wait(pe, j, name)
            for t in range(2 * pair, 2 * pair + 2):
                lhs = (B_t if of_b else K_t)[hr[e], t * P:(t + 1) * P]
                m = pe.matmul(bank[M_BANK[n]][:, (t % 2) * 2 * P:(t % 2 + 1) * 2 * P], lhs,
                              AR[hr[e], t, :, :].rearrange("p h c -> p (h c)"), start=True, stop=True)
            PEa.done(m, f"m{n}")

    def pe_x0(pe, j):
        for e in range(2):
            DVEa.wait(pe, j, f"xt{e}")
            PEa.done(pe_turn(pe, 4 + e, lambda t: XT[:, e, t, :]), f"x{e}")

    def pe_z(pe, j, b):
        for e in range(2):
            POOLb.wait(pe, j, f"m{b}_{e}")
            if b == 2:
                ACTa.wait(pe, j, f"x{e}")
                DVEa.wait(pe, j, f"e{4 + e}b")
            else:
                ACTb.wait(pe, j, f"x{b // 2}_{e}")
            for t in range(NT):
                m = pe.matmul(bank[e][:, t * P:(t + 1) * P], MTb[:, e, t, :], X[:, e, t, :], start=True, stop=True)
            PEb.done(m, f"z{b}_{e}")

    def pe_xt(pe, j, b):
        for e in range(2):
            ACTb.wait(pe, j, f"z{b}_{e}")
            if b == 2:
                DVEa.wait(pe, j, f"e{6 + e}b")
            for t in range(NT):
                m = pe.matmul(bank[2 + e][:, t * P:(t + 1) * P], Z[:, e, t, :], XT[:, e, t, :], start=True, stop=True)
            PEb.done(m, f"xt{b}_{e}")

    def pe_x(pe, j, b):
        for e in range(2):
            DVEb.wait(pe, j, f"xt{b}_{e}")
            PEb.done(pe_turn(pe, 4 + e, lambda t: XT[:, e, t, :]), f"x{b}_{e}")

    def pe_post_mean(pe, j, after):
        ACTb.wait(pe, j, "y")
        if after:
            ACTa.wait(pe, Round(j.i, j.off + 2), "sg")
        PEc.done(pe.matmul(bank[6][:, :], bones[:, :], y_sb[:, :], start=True, stop=True), "mean")

    def pe_post_var(pe, j):
        ACTc.wait(pe, j, "d2")
        PEc.done(pe_head_sums(pe, 6, d2), "var")

    def pe_post_spread(pe, j):
        DVEc.wait(pe, j, "spread")
        PEc.done(pe_head_spread(pe, 6, d2), "bc")

    def pe_post_gate(pe, j):
        wait(pe, lg_landed, j.plus(1) * 32)
        DVEc.wait(pe, j, "yn")
        pe.matmul(bank[6][:, :], lg[:, 0, :], g_hid[:, :], start=True, stop=False)
        PEc.done(pe.matmul(bank[6][:, :], lg[0:G_REST, 1, :], g_hid2[:, :], start=False, stop=True), "g")

    def pe_blocks(pe):
        def body(j, before, after):
            pre, post = nxt(j), prv(j)
            if after:
                pe_low(pe, pre)
            pe_z(pe, j, 2)
            pe_xt(pe, j, 2)
            pe_x(pe, j, 2)
            if before:
                pe_post_mean(pe, post, after)
            pe_z(pe, j, 4)
            pe_xt(pe, j, 4)
            if after:
                pe_kk_sum(pe, pre)
            pe_x(pe, j, 4)
            pe_z(pe, j, 8)
            pe_xt(pe, j, 8)
            if before:
                pe_post_var(pe, post)
            pe_x(pe, j, 8)
            pe_z(pe, j, 16)
            if after:
                pe_kk_spread(pe, pre)
            if before:
                pe_post_spread(pe, post)
            pe_xt(pe, j, 16)
            pe_x(pe, j, 16)
            pe_z(pe, j, 32)
            if before:
                pe_post_gate(pe, post)
            pe_xt(pe, j, 32)
            if after:
                pe_bonus(pe, pre)
            for e in range(2):
                for t in range(NT):
                    m = pe.matmul(bank[4 + e][:, t * CH:(t + 1) * CH], AK[:, e, t, :], V_k[:, t, hr[e]],
                                  start=True, stop=True)
                PEb.done(m, f"u{e}")
            for e in range(2):
                DVEb.wait(pe, j, f"xt32_{e}")
                ACTb.wait(pe, j, f"u{e}")
                for t in range(NT):
                    m = pe.matmul(bank[e][:, t * P:(t + 1) * P], XT[:, e, t, :], AU[:, t, e, :], start=True, stop=True)
                PEb.done(m, f"xau{e}")

            def local(t):
                cs = slice(t * P, (t + 1) * P)
                for e in range(2):
                    pe.matmul(bank[6][hr[e], cs], XAU[:, e, t, CH:P], RB[:, e, t, :], start=t == 0, stop=False,
                              skip_group_check=True)
                    pe.matmul(bank[6][hr[e], cs], V_k[:, t, hr[e]], RK[:, e, t, :], start=False, stop=False,
                              skip_group_check=True)

            if before:
                DVEc.wait(pe, post, "y")
            elif after:
                ACTa.wait(pe, pre, "sg")
            ACTb.wait(pe, j, "xau1")
            local(0)
            for out in ("gh", "rh"):
                for e in range(2):
                    for t in range(NT):
                        for p_ in range(2):
                            q, cs = hr[p_], slice(t * CH, (t + 1) * CH)
                            if out == "gh":
                                xa, xu = XAU[q, e, t, 0:CH], XAU[q, e, t, CH:P]
                                pe.matmul(bank[p_][hr[e], cs], xa, B_k[q, t, hr[e]], start=True, stop=True)
                                hs = slice(NT * CH + t * CH, NT * CH + (t + 1) * CH)
                                pe.matmul(bank[p_][hr[e], hs], B_k[q, t, hr[e]], xu, start=True, stop=False)
                                m = pe.matmul(bank[p_][hr[e], hs], K_k[q, t, hr[e]], V_k[q, t, hr[e]],
                                              start=False, stop=True)
                            else:
                                m = pe.matmul(bank[2 + p_][hr[e], cs], XAU[q, e, t, 0:CH], RB[q, e, t, hr[p_]],
                                              start=True, stop=True)
                PEb.done(m, out)
            for t in range(1, NT):
                local(t)
            if after:
                DVEa.wait(pe, pre, "bonus")
            for c in range(1, NCH):
                DVEb.wait(pe, j, f"S{c}")
                if c == 1:
                    DVEb.wait(pe, j, "rh1")
                if c < NCH - 1:
                    PEb.done(pe.matmul(bank[7][:, 0:CH], GT[:, c, :, :].rearrange("p e c -> p (e c)"), S[:, c, :],
                                       start=True, stop=True), f"s{c}")
                elif after:
                    pe_products(pe, pre, (5,))
                for e in range(2):
                    m = pe.matmul(bank[6][hr[e], c * CH:(c + 1) * CH], S[hr[e], c, :], RH[hr[e], c * CH:(c + 1) * CH],
                                  start=False, stop=c == NCH - 1, skip_group_check=True)
                if c == NCH - 1:
                    PEb.done(m, "y")
                if after:
                    if c == 1:
                        pe_turn_ab(pe, pre)
                    elif c == 2:
                        pe_turn_kv(pe, pre)
                    elif c < NCH - 1:
                        pe_products(pe, pre, {3: (0,), 4: (1,), 5: (2, 3), 6: (4,)}[c])
            if after:
                pe_x0(pe, pre)
                pe_products(pe, pre, (6, 7))

        pe.wait_ge(masks_ready, MASKS)
        pe.wait_ge(hid_ready, 4)
        j = Round(0)
        pe_low(pe, j)
        pe_kk_sum(pe, j)
        pe_kk_spread(pe, j)
        pe_bonus(pe, j)
        pe_turn_ab(pe, j)
        pe_turn_kv(pe, j)
        pe_products(pe, j, range(6))
        pe_x0(pe, j)
        pe_products(pe, j, (6, 7))
        over_tiles(pe, body)
        j = Round(KD - 1)
        pe_post_mean(pe, j, False)
        pe_post_var(pe, j)
        pe_post_spread(pe, j)
        pe_post_gate(pe, j)

    ys_hi_ready, ys_ready = count("ys_hi_ready"), count("ys_ready")

    class Project:

        def __init__(self, mem, tag, at0, w, hi, lo, y_split, gains):
            self.at0, self.w, self.hi, self.lo, self.y_split = at0, w, hi, lo, y_split
            self.end = at0.plus(KD)
            self.o = sbs(mem, f"po{tag}", [P, KD, T])
            self.o0 = o_ready.claim(KD)
            self.norm_o = Norm(lambda k: self.o[:, k, :], KD, lambda eng, k: eng.wait_ge(o_ready.sem, self.o0 + k + 1))
            self.res = Residual(lambda k: self.o[:, k, :], gains)
            self.ready = self.res.ready

        def sp(self, sp, outs=range(KD)):
            for o in outs:
                at = self.at0.plus(o)
                load(sp, at, unit_parts(at, self.w, (0, KD), (o * P, P)), (lo_ready, at.plus(-RAW).count))

        def act(self, act):
            for o in range(KD):
                at = self.at0.plus(o)
                split_hi(act, at.plus(2))
                act.wait_ge(unit_done, at.count)
                act.activation(self.o[:, o, :], bank[o % 2][:, :], ACT.Copy).then_inc(o_ready.sem, 1)
                self.norm_o.act_square(act, o)
            self.norm_o.act_root(act)

        def dve(self, dve):
            for o in range(KD):
                split_lo(dve, self.at0.plus(o + 2))
            self.norm_o.dve_rstd(dve)
            self.res.dve(dve)

        def pe(self, pe):
            for o in range(KD):
                wait(pe, o_ready.sem, self.o0 + o - 1)
                unit_products(pe, self.at0.plus(o), KD, bank[o % 2][:, :], lambda k: self.hi[:, k, :],
                              lambda k: self.lo[:, k, :], True, True,
                              (lambda k: self.y_split(pe, k)) if o == 0 else None)
            self.norm_o.pe_sums(pe)

    gains_of = lambda n: (lambda k: v("gains", n * KD + k))
    ys_hi = sbs(tm, "ys_hi", [P, KD, T], F32R)
    ys_lo = sbs(tm, "ys_lo", [P, KD, T], F32R)
    y0, yhi0 = ys_ready.claim(KD), ys_hi_ready.claim(KD)
    out_tm = Project(tm, "1", at_rkv0.plus(3 * KD), A["rwkv_w_o_2"].rearrange("a k n -> (a k) n"), ys_hi, ys_lo,
                     lambda eng, k: eng.wait_ge(ys_ready.sem, y0 + k + 1), gains_of(1))
    tm.close()

    def act_split_y(act):
        DVEc.wait(act, Round(KD - 1), "y")
        for k in range(KD):
            act.activation(ys_hi[:, k, :], rkv[:, k, :], ACT.Copy).then_inc(ys_hi_ready.sem, 1)

    def dve_split_y(dve):
        DVEc.wait(dve, Round(KD - 1), "y")
        for k in range(KD):
            dve.wait_ge(ys_hi_ready.sem, yhi0 + k + 1)
            dve.tensor_tensor(ys_lo[:, k, :], rkv[:, k, :], ys_hi[:, k, :].bitcast(F32), ALU.subtract)\
               .then_inc(ys_ready.sem, 1)

    wg2, wu2, wd2 = A["ffn_w_gate_2"], A["ffn_w_up_2"], A["ffn_w_down_2"]
    ffn1 = FFN("1", out_tm.end, out_tm.ready, gains_of(2), None, wg2[0], wu2[0], wd2[0], False, gains_of(3))

    gu = ExitStack()
    gh_hi = sbs(gu, "gh_hi", [P, KD, T], F32R)
    gh_lo = sbs(gu, "gh_lo", [P, KD, T], F32R)
    uv = sbs(gu, "uv", [P, 2 * KD, T])
    v_tk = sbs(gu, "v_tk", [P, NT, D])
    ws_in = sbs(gu, "ws_in", [P, KD, P])
    wsT = sbs(gu, "wsT", [P, KD, P])
    bs_row = sbs(gu, "bs_row", [1, KD * P])
    bs = sbs(gu, "bs", [P, KD, P])
    LN_EPS = 1e-5
    gs_landed, wsT_done, wsT_ready, bs_done, bs_ready = (sem(n) for n in (
        "gs_landed", "wsT_done", "wsT_ready", "bs_done", "bs_ready"))
    uv_ready, mean_done, v_centred, v_scaled, vn_ready = (sem(n) for n in (
        "uv_ready", "mean_done", "v_centred", "v_scaled", "vn_ready"))
    vt_done, vt_ready, s_done, s_biased = (sem(n) for n in ("vt_done", "vt_ready", "s_done", "s_biased"))
    us_ready, us_hi, us_split = sem("us_ready"), sem("us_hi"), sem("us_split")
    norm_g = Norm(x_tile, KD, ffn1.ready)
    split_g = Split(x_tile, KD, gains_of(4), None, lambda k: gh_hi[:, k, :], lambda k: gh_lo[:, k, :], lambda eng: None)
    norm_v = Norm(lambda k: uv[:, KD + k, :], KD, lambda eng, k: eng.wait_ge(v_centred, k + 1), eps=LN_EPS)
    at_g0 = ffn1.end
    at_g = lambda i, k: at_g0.plus(4 * i + k) if isinstance(i, int) else At(at_g0.c + k, at_g0.u + k, 4, i)
    w_gu = A["sgu_w_in_2"].rearrange("a k n -> (a k) n")
    N_GU = 2 * KD // 4
    out_gu = Project(gu, "2", at_g0.plus(2 * KD), A["sgu_w_out_2"].rearrange("a k n -> (a k) n"), gh_hi, gh_lo,
                     lambda eng, k: eng.wait_ge(us_split, k + 1), gains_of(5))
    gu.close()

    def sp_gate(sp):
        def body(i, last):
            for k in range(4):
                at = at_g(i, k)
                load(sp, at, unit_parts(at, w_gu, (0, KD), (i * 4 * P + k * P, P)), (lo_ready, at.plus(-RAW).count))

        body(0, False)
        sp.wait_ge(unit_done, ffn1.end.u)
        ffn1.ready(sp, KD - 1)
        sp.dma_start(ws_in[:, :, :], A["sgu_ws_2"].rearrange("a g i j -> i (a g) j")).then_inc(gs_landed, 16)
        sp.dma_start(bs_row[:, :], A["sgu_bs_2"].rearrange("a g i -> a (g i)")).then_inc(gs_landed, 16)
        with sp.Fori(1, N_GU) as i:
            body(i, False)

    def pe_gate(pe):
        norm_g.pe_sums(pe)
        pe.wait_ge(gs_landed, 32)
        for h in range(2):
            for g in range(KD // 2):
                tr = pe.transpose(bank[5 + h][:, g * P:(g + 1) * P], ws_in[:, h * (KD // 2) + g, :], ident[:, :])
            tr.then_inc(wsT_done, 1)
        for h in range(2):
            b = (7, 4)[h]
            if h:
                pe.wait_ge(var_ready.sem, norm_g.var0 + 1)
            pe.matmul(bank[b][:, :], ones[0:1, :], bs_row[:, h * T:(h + 1) * T], start=True, stop=True)\
              .then_inc(bs_done, 1)

        def body(i, last):
            for k in range(4):
                if not isinstance(i, int) or i:
                    pe.wait_ge(uv_ready, i * 4 + (k - 3))
                ready = split_g.pe_ready(pe) if isinstance(i, int) and i + k == 0 else None
                unit_products(pe, at_g(i, k), KD, bank[k][:, :], lambda k: gh_hi[:, k, :], lambda k: gh_lo[:, k, :],
                              True, True, ready)

        loop(pe, N_GU, body)
        for k in range(KD):
            pe.wait_ge(uv_ready, KD + k + 1)
            if k == 0:
                pe.wait_ge(wsT_ready, 2)
            mm = pe.matmul(bank[5][:, :], ones[:, :], uv[:, KD + k, :], start=k == 0, stop=k == KD - 1)
        mm.then_inc(mean_done, 1)
        norm_v.pe_sums(pe)
        for k in range(KD + 1):
            if k < KD:
                pe.wait_ge(vn_ready, k + 1)
                wait(pe, vt_ready, k - 1)
                for t in range(NT):
                    tr = pe.transpose(bank[k % 2][:, t * P:(t + 1) * P], uv[:, KD + k, t * P:(t + 1) * P], ident[:, :])
                tr.then_inc(vt_done, 1)
            if k:
                g = k - 1
                pe.wait_ge(vt_ready, g + 1)
                wait(pe, s_biased, g - 1)
                for t in range(NT):
                    mm = pe.matmul(bank[2 + g % 2][:, t * P:(t + 1) * P], v_tk[:, t, g * P:(g + 1) * P], wsT[:, g, :],
                                   start=True, stop=True)
                mm.then_inc(s_done, 1)
        out_gu.pe(pe)

    def act_gate(act):
        norm_g.act_squares(act)
        norm_g.act_root(act)
        split_g.act(act)
        for h in range(2):
            act.wait_ge(wsT_done, h + 1)
            act.activation(wsT[:, h * 4:(h + 1) * 4, :], bank[5 + h][:, :].rearrange("p (g c) -> p g c", c=P), ACT.Copy)\
               .then_inc(wsT_ready, 1)
        for h in range(2):
            act.wait_ge(bs_done, h + 1)
            act.activation(bs[:, h * 4:(h + 1) * 4, :], bank[(7, 4)[h]][:, :].rearrange("p (g c) -> p g c", c=P), ACT.Copy)\
               .then_inc(bs_ready, 1)

        def body(i, last):
            for k in range(4):
                split_hi(act, at_g(i, k).plus(2))
                act.wait_ge(unit_done, at_g(i, k).count)
                act.activation(tile_at(uv, i * 4 + k), bank[k][:, :], ACT.Gelu, bias=col_at(vecs, i * 4 + (col["sgu_b"] + k)))\
                   .then_inc(uv_ready, 1)

        loop(act, N_GU, body)
        norm_v.act_squares(act)
        norm_v.act_root(act)
        for k in range(KD):
            act.wait_ge(v_scaled, k + 1)
            act.activation(uv[:, KD + k, :], tmp[:, k % 3, :], ACT.Identity, bias=v("ln_b", k)).then_inc(vn_ready, 1)
        for k in range(KD + 1):
            if k < KD:
                act.wait_ge(vt_done, k + 1)
                act.activation(v_tk[:, :, k * P:(k + 1) * P], bank[k % 2][:, :].rearrange("p (t c) -> p t c", t=NT),
                               ACT.Copy).then_inc(vt_ready, 1)
            if k:
                g = k - 1
                act.wait_ge(us_ready, g + 1)
                act.activation(gh_hi[:, g, :], tmp[:, g % 3, :], ACT.Copy).then_inc(us_hi, 1)
        out_gu.act(act)

    def dve_gate(dve):
        norm_g.dve_rstd(dve)
        split_g.dve(dve)
        dve.wait_ge(wsT_ready, 2)
        dve.memset(wsT[CH:P, :, 0:CH], 0.0).then_inc(bs_ready, 1)

        def body(i, last):
            for k in range(4):
                split_lo(dve, at_g(i, k).plus(2))

        loop(dve, N_GU, body)
        dve.wait_ge(mean_done, 1)
        for k in range(KD):
            dve.scalar_tensor_tensor(uv[:, KD + k, :], bank[5][:, :], -1.0 / D, uv[:, KD + k, :], ALU.mult, ALU.add)\
               .then_inc(v_centred, 1)
        norm_v.dve_rstd(dve)
        for k in range(KD):
            wait(dve, vn_ready, k - 2)
            dve.scalar_tensor_tensor(tmp[:, k % 3, :], uv[:, KD + k, :], v("ln_w", k), rstd[:, :], ALU.mult, ALU.mult)\
               .then_inc(v_scaled, 1)
        dve.wait_ge(vn_ready, KD)
        dve.wait_ge(bs_ready, 3)

        def lower(g):
            dve.wait_ge(us_hi, g + 1)
            dve.tensor_tensor(gh_lo[:, g, :], tmp[:, g % 3, :], gh_hi[:, g, :].bitcast(F32), ALU.subtract)\
               .then_inc(us_split, 1)

        for g in range(KD):
            dve.wait_ge(s_done, g + 1)
            wait(dve, us_split, g - 2)
            t = tmp[:, g % 3, :].rearrange("p (t c) -> p t c", t=NT)
            dve.tensor_tensor(t, bank[2 + g % 2][:, :].rearrange("p (t c) -> p t c", t=NT),
                              bs[:, g:g + 1, :].to_broadcast([P, NT, P]), ALU.add).then_inc(s_biased, 1)
            dve.wait_ge(s_biased, g + 1)
            dve.tensor_tensor(tmp[:, g % 3, :], tmp[:, g % 3, :], uv[:, g, :], ALU.mult).then_inc(us_ready, 1)
            if g:
                lower(g - 1)
        dve.wait_ge(us_ready, KD)
        lower(KD - 1)
        out_gu.dve(dve)

    ffn2 = FFN("2", out_gu.end, out_gu.ready, gains_of(6), None, wg2[1], wu2[1], wd2[1], False, gains_of(7), final=True)

    with ExitStack() as part:
        x_out = sbs(part, "x_out", [P, NT, D])
    out_turned, out_copied, out_landed = sem("out_turned"), sem("out_copied"), sem("out_landed")

    def pe_out(pe):
        for n in range(2 * NT):
            t, h = divmod(n, 2)
            if n < 2:
                ffn2.ready(pe, (n + 1) * (KD // 2) - 1)
            wait(pe, out_copied, n - 3)
            for k in range(KD // 2):
                tr = pe.transpose(bank[n % 4][:, k * P:(k + 1) * P], x[:, h * (KD // 2) + k, t * P:(t + 1) * P], ident[:, :])
            tr.then_inc(out_turned, 1)

    def act_out(act):
        for n in range(2 * NT):
            act.wait_ge(out_turned, n + 1)
            act.activation(x_out[:, n // 2, n % 2 * T:(n % 2 + 1) * T], bank[n % 4][:, :], ACT.Copy).then_inc(out_copied, 1)

    def sp_out(sp):
        dst = out.rearrange("b (t p) d -> (b t) p d", p=P)
        for t in range(NT):
            sp.wait_ge(out_copied, 2 * t + 2)
            sp.dma_start(dst[t], x_out[:, t, :]).then_inc(out_landed, 16)
        sp.wait_ge(out_landed, 16 * NT)

    block = ctx.enter_context(nc.Block())

    @block.sync
    def _(sp):
        sp_first_units(sp)
        ffn0.sp(sp)
        sp_time_mix(sp)
        out_tm.sp(sp, range(RAW))
        sp_blocks(sp)
        out_tm.sp(sp, range(RAW, KD))
        ffn1.sp(sp)
        sp_gate(sp)
        out_gu.sp(sp)
        ffn2.sp(sp)
        sp_out(sp)

    @block.gpsimd
    def _(pool):
        pool_setup(pool)
        norm1.pool_sum(pool)
        for m in range(ADA_EARLY * KD, 6 * KD):
            if m == 2 * KD + N_IN:
                norm_cv.pool_sum(pool)
                norm_at.pool_sum(pool)
            ada_accumulate(pool, m)
        ffn0.norm.pool_sum(pool)
        norm_f.pool_sum(pool)
        norm_tm.pool_sum(pool)
        pool_masks(pool)
        pool_blocks(pool)
        for norm in (out_tm.norm_o, ffn1.norm, ffn1.norm_o, norm_g, norm_v, out_gu.norm_o, ffn2.norm, ffn2.norm_o):
            norm.pool_sum(pool)

    @block.scalar
    def _(act):
        act_setup_dmas(act)
        act_setup(act)
        act_mixer1(act)
        ffn0.act(act)
        act_time_mix(act)
        act_blocks(act)
        act_split_y(act)
        out_tm.act(act)
        ffn1.act(act)
        act_gate(act)
        ffn2.act(act)
        act_out(act)

    @block.vector
    def _(dve):
        dve_mixer1(dve)
        scaled_gain(dve, "norm2", 4)
        ffn0.dve(dve)
        dve_final(dve)
        dve_time_mix(dve)
        dve_blocks(dve)
        dve_split_y(dve)
        out_tm.dve(dve)
        ffn1.dve(dve)
        dve_gate(dve)
        ffn2.dve(dve)

    @block.tensor
    def _(pe):
        pe_setup(pe)
        pe_mixer1(pe)
        ffn0.pe(pe)
        pe_time_mix(pe)
        pe_blocks(pe)
        out_tm.pe(pe)
        ffn1.pe(pe)
        pe_gate(pe)
        ffn2.pe(pe)
        pe_out(pe)

    return ctx


_INS = ["x", "c", "positions", "ada_w", "ada_b", "norm1_g", "w_in", "b_in", "conv_w", "attn_sinks",
        "out_norm_attn_g", "out_norm_conv_g", "w_o", "norm2_g", "w_up", "ffn_conv_w", "ffn_conv_b", "w_down",
        "final_norm_g", "norm_gains_2", "rwkv_mix_2", "rwkv_w_rkv_2", "rwkv_w0_2", "rwkv_w1_2", "rwkv_w2_2",
        "rwkv_a0_2", "rwkv_a1_2", "rwkv_a2_2", "rwkv_g1_2", "rwkv_g2_2", "rwkv_k_k_2", "rwkv_k_a_2",
        "rwkv_r_k_2", "rwkv_gn_w_2", "rwkv_gn_b_2", "rwkv_w_o_2", "sgu_w_in_2", "sgu_b_in_2", "sgu_ln_w_2",
        "sgu_ln_b_2", "sgu_ws_2", "sgu_bs_2", "sgu_w_out_2", "ffn_w_gate_2", "ffn_w_up_2", "ffn_w_down_2"]
ROPE_THETA = 10000.0


def kernel(**inputs):
    import numpy as _np
    import concourse.bacc as _bacc
    from concourse import mybir as _mybir
    from concourse.bass_utils import run_bass_kernel_spmd as _run

    arrays = {name: _np.ascontiguousarray(inputs[name]) for name in _INS}
    half = HD // 2
    inv = ROPE_THETA ** (-_np.arange(half, dtype=_np.float32) / _np.float32(half))
    arrays["inv_freq"] = _np.tile(inv.astype(_np.float32), P // half).reshape(P, 1)

    nc = _bacc.Bacc("TRN2", target_bir_lowering=False, num_devices=1)
    A = {name: nc.dram_tensor(f"in_{name}_dram", a.shape, _mybir.dt.from_np(a.dtype), kind="ExternalInput").ap()
         for name, a in arrays.items()}
    out = nc.dram_tensor("out_0_dram", (1, T, D), F32, kind="ExternalOutput").ap()
    with build(nc, A, out):
        pass
    r = _run(nc, [{f"in_{name}_dram": a for name, a in arrays.items()}], core_ids=[0])
    return r.results[0]["out_0_dram"]
```

```python
from contextlib import ExitStack

import numpy as np

import concourse.bass as bass
from concourse import mybir

F32 = mybir.dt.float32
F32R = mybir.dt.float32r
I32 = mybir.dt.int32
ALU = mybir.AluOpType
ACT = mybir.ActivationFunctionType
AX_X = mybir.AxisListType.X

P = 128
T = 512
D = 1024
KD = D // P
NT = T // P
DFF = 2816
KF = DFF // P
HALF = KF // 2
HD = 64
NQ, NKV = 8, 2
DA = NQ * HD
KA = DA // P
RAW = 4
EPS = 1e-6
TWO_PI = 2 * np.pi
TURN1 = 6.28125
TURN2 = float(np.float32(round((TWO_PI - TURN1) * 2 ** 22) / 2 ** 22))
TURN3 = float(np.float32(TWO_PI - TURN1 - TURN2))
ROUND = float(1.5 * 2 ** 23)
MASKED = -1e30


class Count:

    def __init__(self, sem):
        self.sem, self.n = sem, 0

    def claim(self, n):
        self.n += n
        return self.n - n


class At:

    def __init__(self, c, u, step=0, i=0):
        self.c, self.u, self.step, self.i = c, u, step, i

    def plus(self, k):
        return At(self.c + k, self.u + k, self.step, self.i)

    @property
    def raw_slot(self):
        return self.c % RAW

    @property
    def slot(self):
        return self.u % 2

    @property
    def count(self):
        return self.u + 1 + self.i * self.step


def wait(eng, sem, value):
    if isinstance(value, int) and value <= 0:
        return
    eng.wait_ge(sem, value)


def loop(eng, n, body):
    body(0, False)
    with eng.Fori(1, n - 1) as i:
        body(i, False)
    body(n - 1, True)


def tile_at(t, k):
    if isinstance(k, int):
        return t[:, k, :]
    return t[:, bass.ds(k, 1), :].rearrange("p a n -> p (a n)")


def cols_at(t, start, n):
    return t[:, start:start + n] if isinstance(start, int) else t[:, bass.ds(start, n)]


def col_at(t, k):
    if isinstance(k, int):
        return t[:, k:k + 1]
    return t[:, bass.ds(k, 1)]


def build(nc, A, out):
    ctx = ExitStack()

    def sb(name, shape, dt=F32):
        return ctx.enter_context(nc.sbuf_tensor(name, shape, dt))

    def sem(name):
        return ctx.enter_context(nc.semaphore(name))

    def count(name):
        return Count(sem(name))

    x = sb("x", [P, KD, T])
    raw = sb("raw", [P, RAW, HALF * P])
    whi = sb("whi", [P, 2, HALF * P], F32R)
    wlo = sb("wlo", [P, 2, HALF * P], F32R)
    ident = sb("ident", [P, P])
    ones = sb("ones", [P, P])
    tmp = sb("tmp", [P, 3, T])
    sq = sb("sq", [P, 2, T])
    sq_sum = sb("sq_sum", [P, T])
    var = sb("var", [P, T])
    rstd = sb("rstd", [P, T])
    mod = sb("mod", [P, 6 * KD])
    gain = sb("gain", [P, KD])
    cact = sb("cact", [P, KD])
    bank = [ctx.enter_context(nc.psum_tensor(f"bank{i}", [P, T], F32)) for i in range(8)]
    NORM_BANK, ADA_BANKS = 4, (7, 6, 6)

    vec_src, col = [], {}

    def vec(name, sources, n):
        col[name] = sum(m for _, m in vec_src)
        vec_src.append((sources, n))

    def vec_rows(name, ap, n):
        vec(name, [(slice(0, P), ap)], n)

    def vec_pairs(name, ap):
        vec(name, [(slice(0, HD), ap[0:DA // 2].rearrange("(j p) -> j p", p=HD)),
                   (slice(HD, P), ap[DA // 2:DA].rearrange("(j p) -> j p", p=HD))], KA)

    flat = lambda ap: ap.rearrange("a n -> (a n)")
    rows = lambda ap: ap.rearrange("(k p) -> k p", p=P)
    vec_rows("ada_b", rows(flat(A["ada_b"])), 6 * KD)
    vec_rows("norm1", rows(flat(A["norm1_g"])), KD)
    vec_rows("b_in", rows(flat(A["b_in"])[DA:]), 14)
    vec_pairs("bq", flat(A["b_in"])[0:DA])
    vec_rows("conv_w", A["conv_w"].rearrange("a w (k p) -> (a w k) p", p=P), 12)
    vec_rows("ga", rows(flat(A["out_norm_attn_g"])), KA)
    vec_rows("gcv", rows(flat(A["out_norm_conv_g"])), 4)
    vec_rows("norm2", rows(flat(A["norm2_g"])), KD)
    vec_rows("final", rows(A["final_norm_g"]), KD)

    vec_rows("ffn_cw", A["ffn_conv_w"].rearrange("a w (k p) -> (a w k) p", p=P), 3 * KF)
    vec_rows("ffn_cb", rows(flat(A["ffn_conv_b"])), KF)

    vec_rows("w0", rows(flat(A["rwkv_w0_2"])), KD)
    vec_rows("a0", rows(flat(A["rwkv_a0_2"])), KD)
    vec_rows("k_k", rows(flat(A["rwkv_k_k_2"])), KD)
    vec_rows("k_a", rows(flat(A["rwkv_k_a_2"])), KD)
    vec_rows("mix", A["rwkv_mix_2"].rearrange("a m (k p) -> (a m k) p", p=P), 6 * KD)
    vec_rows("r_k", A["rwkv_r_k_2"].rearrange("a (k h) n -> (a k) (h n)", h=2), KD)
    vec_rows("gn_w", rows(flat(A["rwkv_gn_w_2"])), KD)
    vec_rows("gn_b", rows(flat(A["rwkv_gn_b_2"])), KD)
    vec_rows("gains", A["norm_gains_2"].rearrange("l m (k p) -> (l m k) p", p=P), 8 * KD)
    vec_rows("sgu_b", rows(flat(A["sgu_b_in_2"])), 2 * KD)
    vec_rows("ln_w", rows(flat(A["sgu_ln_w_2"])), KD)
    vec_rows("ln_b", rows(flat(A["sgu_ln_b_2"])), KD)
    n_vec = sum(m for _, m in vec_src)
    VB = -(-n_vec // P)
    vecs = sb("vecs", [P, VB * P])

    def v(name, k=0):
        return col_at(vecs, col[name] + k)

    landed = [sem(f"raw{s}_landed") for s in range(RAW)]
    hi_ready, lo_ready = sem("hi_ready"), sem("lo_ready")
    unit_done, ada_done, ada_pool_done = sem("unit_done"), sem("ada_done"), sem("ada_pool_done")
    n_units = [0, 0]

    def raw_unit(at, kts):
        return raw[:, at.raw_slot, 0:kts * P]

    def load(sp, at, parts, freed):
        if freed is not None:
            wait(sp, *freed)
        for dst, src in parts:
            sp.dma_start(dst, src).then_inc(landed[at.raw_slot], 16)

    def unit_parts(at, w, ks, cols):
        k0, kts = ks
        src = cols_at(w[k0 * P:(k0 + kts) * P, :], *cols).rearrange("(k p) n -> p k n", p=P)
        return [(raw[:, at.raw_slot, 0:kts * P].rearrange("p (k n) -> p k n", n=P), src)]

    def split_hi(act, at, kts=KD):
        act.wait_ge(landed[at.raw_slot], landed_at(at))
        wait(act, unit_done, at.plus(-2).count)
        act.activation(whi[:, at.slot, 0:kts * P], raw_unit(at, kts), ACT.Copy).then_inc(hi_ready, 1)

    def split_lo(dve, at, kts=KD):
        dve.wait_ge(landed[at.raw_slot], landed_at(at))
        dve.wait_ge(hi_ready, at.count)
        dve.tensor_tensor(wlo[:, at.slot, 0:kts * P], raw_unit(at, kts),
                          whi[:, at.slot, 0:kts * P].bitcast(F32), ALU.subtract).then_inc(lo_ready, 1)

    def unit_products(pe, at, kts, dst, rhs_hi, rhs_lo, first, last, k_ready=None, ks=None,
                      k_done=None):
        ks = range(kts) if ks is None else ks
        if ks[0] == 0:
            pe.wait_ge(lo_ready, at.count)
        for k in ks:
            if k_ready is not None:
                k_ready(k)
            hi, lo = (w[:, at.slot, k * P:(k + 1) * P] for w in (whi, wlo))
            pe.matmul(dst, hi, rhs_hi(k), start=first and k == 0, stop=False)
            pe.matmul(dst, hi, rhs_lo(k), start=False, stop=False)
            mm = pe.matmul(dst, lo, rhs_hi(k), start=False, stop=last and k == kts - 1)
            if k_done is not None and k < kts - 1:
                mm.then_inc(k_done, 1)
        if ks[-1] == kts - 1:
            mm.then_inc(unit_done, 1)

    sq_ready, acc_step, sum_step = count("sq_ready"), count("acc_step"), count("sum_step")
    var_ready, std_ready, rstd_ready = count("var_ready"), count("std_ready"), count("rstd_ready")
    tmp_ready, nhi_ready, h_ready = count("tmp_ready"), count("nhi_ready"), count("h_ready")
    x_ready, x_added = count("x_ready"), count("x_added")

    class Norm:

        def __init__(self, src, n, ready, eps=EPS, rstd_=None, var_=None, slots=None):
            self.src, self.n, self.ready, self.eps, self.slots = src, n, ready, eps, slots
            self.rstd = rstd[:, :] if rstd_ is None else rstd_
            self.var = var[:, :] if var_ is None else var_
            self.sq0, self.acc0 = sq_ready.claim(n), acc_step.claim(0 if slots else n - 2)
            self.sum0, self.var0, self.std0, self.rstd0 = (
                c.claim(1) for c in (sum_step, var_ready, std_ready, rstd_ready))

        def act_slot_free(self, act, k):
            if not isinstance(k, int):
                act.wait_ge(acc_step.sem, k + (self.acc0 - 1))
            elif k >= 2:
                act.wait_ge(acc_step.sem, self.acc0 + max(1, k - 2))
            else:
                wait(act, sum_step.sem, self.sum0)

        def act_square(self, act, k):
            self.ready(act, k)
            if self.slots is None:
                self.act_slot_free(act, k)
            act.activation(self.slots[k] if self.slots else sq[:, k % 2, :], self.src(k), ACT.Square)\
               .then_inc(sq_ready.sem, 1)

        def act_square_of(self, act, src, parity):
            act.activation(sq[:, parity, :], src, ACT.Square).then_inc(sq_ready.sem, 1)

        def act_squares(self, act):
            for k in range(self.n):
                self.act_square(act, k)

        def pool_add(self, pool, k):
            if k == 1:
                wait(pool, sum_step.sem, self.sum0)
            pool.wait_ge(sq_ready.sem, self.sq0 + k + 1)
            wait(pool, acc_step.sem, self.acc0 + k - 1)
            pool.tensor_tensor(sq_sum[:, :], sq[:, 0, :] if k == 1 else sq_sum[:, :], sq[:, k % 2, :], ALU.add)\
                .then_inc(acc_step.sem, 1)

        def pool_sum(self, pool):
            for k in range(1, self.n - 1):
                self.pool_add(pool, k)

        def act_root(self, act):
            act.wait_ge(var_ready.sem, self.var0 + 1)
            act.activation(self.var, self.var, ACT.Sqrt).then_inc(std_ready.sem, 1)

        def pe_sums(self, pe):
            wait(pe, var_ready.sem, self.var0)
            if self.slots is not None:
                for k in range(self.n):
                    pe.wait_ge(sq_ready.sem, self.sq0 + k + 1)
                    mm = pe.matmul(bank[NORM_BANK][:, :], ones[:, :], self.slots[k], start=k == 0, stop=k == self.n - 1)
                mm.then_inc(sum_step.sem, 1)
                return
            pe.wait_ge(acc_step.sem, self.acc0 + self.n - 2)
            pe.matmul(bank[NORM_BANK][:, :], ones[:, :], sq_sum[:, :], start=True, stop=False)
            pe.wait_ge(sq_ready.sem, self.sq0 + self.n)
            pe.matmul(bank[NORM_BANK][:, :], ones[:, :], sq[:, (self.n - 1) % 2, :], start=False, stop=True)\
              .then_inc(sum_step.sem, 1)

        def dve_mean(self, dve):
            dve.wait_ge(sum_step.sem, self.sum0 + 1)
            dve.tensor_scalar(self.var, bank[NORM_BANK][:, :], 1.0 / (self.n * P), self.eps,
                              ALU.mult, ALU.add).then_inc(var_ready.sem, 1)

        def dve_rstd(self, dve, mean=True):
            if mean:
                self.dve_mean(dve)
            dve.wait_ge(std_ready.sem, self.std0 + 1)
            dve.reciprocal(self.rstd, self.var).then_inc(rstd_ready.sem, 1)
            dve.wait_ge(rstd_ready.sem, self.rstd0 + 1)

    class Split:

        def __init__(self, src, n, gains, shift, dst_hi, dst_lo, free):
            self.src, self.n, self.gains, self.shift = src, n, gains, shift
            self.hi, self.lo, self.free = dst_hi, dst_lo, free
            self.t0, self.hi0, self.h0 = (c.claim(n) for c in (tmp_ready, nhi_ready, h_ready))

        def dve(self, dve):
            def lower(k):
                dve.wait_ge(nhi_ready.sem, self.hi0 + k + 1)
                if self.shift is None:
                    ins = dve.tensor_tensor(self.lo(k), tmp[:, (self.t0 + k) % 3, :],
                                            self.hi(k).bitcast(F32), ALU.subtract)
                else:
                    ins = dve.scalar_tensor_tensor(self.lo(k), tmp[:, (self.t0 + k) % 3, :], self.shift(k),
                                                   self.hi(k).bitcast(F32), ALU.add, ALU.subtract)
                ins.then_inc(h_ready.sem, 1)

            self.free(dve)
            for k in range(self.n):
                wait(dve, h_ready.sem, self.h0 + k - 2)
                dve.scalar_tensor_tensor(tmp[:, (self.t0 + k) % 3, :], self.src(k), self.gains(k),
                                         rstd[:, :], ALU.mult, ALU.mult).then_inc(tmp_ready.sem, 1)
                if k == 0:
                    dve.wait_ge(tmp_ready.sem, self.t0 + 1)
                if k:
                    dve.wait_ge(tmp_ready.sem, self.t0 + k)
                    lower(k - 1)
            lower(self.n - 1)

        def act(self, act):
            self.free(act)
            for k in range(self.n):
                act.wait_ge(tmp_ready.sem, self.t0 + k + 1)
                act.activation(self.hi(k), tmp[:, (self.t0 + k) % 3, :], ACT.Identity,
                               bias=0.0 if self.shift is None else self.shift(k))\
                   .then_inc(nhi_ready.sem, 1)

        def pe_ready(self, pe):
            return lambda k: pe.wait_ge(h_ready.sem, self.h0 + k + 1)

    class Halves:

        def __init__(self, src, n, gains, dst_hi, dst_lo, ready, free=None):
            self.src, self.n, self.gains, self.ready, self.free = src, n, gains, ready, free
            self.hi, self.lo = dst_hi, dst_lo
            self.hi0, self.h0 = nhi_ready.claim(n), h_ready.claim(n)

        def act_hi(self, act, k):
            self.ready(act, k)
            if k == 0 and self.free is not None:
                act.wait_ge(*self.free)
            act.activation(self.hi(k), self.src(k), ACT.Identity, scale=self.gains(k)).then_inc(nhi_ready.sem, 1)

        def dve_lo(self, dve, k):
            dve.wait_ge(nhi_ready.sem, self.hi0 + k + 1)
            dve.scalar_tensor_tensor(self.lo(k), self.src(k), self.gains(k), self.hi(k).bitcast(F32),
                                     ALU.mult, ALU.subtract).then_inc(h_ready.sem, 1)

        def pe_ready(self, pe):
            return lambda k: pe.wait_ge(h_ready.sem, self.h0 + k + 1)

    w_in, w_o, ada_w = (A[n].rearrange("a k n -> (a k) n") for n in ("w_in", "w_o", "ada_w"))
    N_IN, N_O = 18, KD
    EARLY = 2 * KD
    order = [("ada", m) for m in range(EARLY)]
    m = EARLY
    for u in range(N_IN):
        order.append(("in", u))
        for _ in range(2 - u % 2):
            order.append(("late", m))
            m += 1
    for u in range(N_O):
        order.append(("o", u))
        if m < 6 * KD:
            order.append(("late", m))
            m += 1
    at_in, at_ada, at_o, seq = {}, {}, {}, []
    u_next, plan = 0, []
    for kind, n in order:
        at = None
        if kind != "late":
            at = At(len(seq), u_next)
            seq.append((kind, n, at))
            {"in": at_in, "o": at_o, "ada": at_ada}[kind][n] = at
            u_next += kind != "ada"
        plan.append((kind, n, at))
    first = [at for kind, _, at in seq if kind != "ada"]
    for n in range(2):
        first.append(At(len(seq) + n, u_next + n))
    IN0 = {"q": 0, "k": 4, "v": 5, "conv": 6}

    def in_columns(u):
        if u < 6:
            return u * P, P
        j, part = divmod(u - 6, 3)
        start = DA + 2 * NKV * HD + part * (D - DA) + j * P
        return start, P

    fixed, slot_count = {}, [0] * RAW
    for kind, n, at in seq:
        slot_count[at.raw_slot] += 32 if kind == "in" and n < 4 else 16
        fixed[at.c] = slot_count[at.raw_slot]

    def landed_at(at):
        if at.c < len(seq):
            return fixed[at.c]
        more = (at.c // RAW + 1) - (len(seq) + RAW - 1 - at.raw_slot) // RAW
        return slot_count[at.raw_slot] + more * 16 + at.i * (at.step // RAW * 16)

    def ada_used(m):
        return (ada_done, m + 1) if m < EARLY else (ada_pool_done, m + 1 - EARLY)

    late_landed = [sem(f"late{s}_landed") for s in range(RAW)]

    def ada_rows(n):
        part, k = divmod(n, KD)
        return ada_w[k * P:(k + 1) * P, part * D:(part + 1) * D]

    def sp_first_units(sp):
        for kind, n, at in plan:
            if kind == "late":
                if n == EARLY:
                    sp.wait_ge(x_turned, KD)
                if n >= EARLY + RAW:
                    sp.wait_ge(*ada_used(n - RAW))
                sp.dma_start(late[:, n % RAW, :], ada_rows(n)).then_inc(late_landed[n % RAW], 16)
                continue
            freed = None
            if at.c >= RAW:
                was, m, old = seq[at.c - RAW]
                freed = (ada_done, m + 1) if was == "ada" else (lo_ready, old.count)
            if kind == "ada":
                parts = [(raw[:, at.raw_slot, 0:D], ada_rows(n))]
            elif kind == "o":
                parts = unit_parts(at, w_o, (0, KD), (n * P, P))
            elif n < 4:
                parts = [(raw[:, at.raw_slot, 0:KD * P].rearrange("p (k h d) -> p k h d", h=2, d=HD)[:, :, h, :],
                          w_in[:, (n + 4 * h) * HD:(n + 4 * h + 1) * HD].rearrange("(k p) d -> p k d", p=P))
                         for h in range(2)]
            else:
                parts = unit_parts(at, w_in, (0, KD), in_columns(n))
            load(sp, at, parts, freed)

    setup = ExitStack()

    def sbs(stage, name, shape, dt=F32):
        return stage.enter_context(nc.sbuf_tensor(name, shape, dt))

    mixer1 = ExitStack()
    h_hi = sbs(mixer1, "h_hi", [P, KD, T], F32R)
    h_lo = sbs(mixer1, "h_lo", [P, KD, T], F32R)
    rot = sbs(mixer1, "rot", [P, P])
    mask = sbs(mixer1, "mask", [P, 2 * P])
    cos_t = sbs(mixer1, "cos_t", [P, T])
    sin_t = sbs(mixer1, "sin_t", [P, T])
    sinks = sbs(mixer1, "sinks", [P, NQ])
    sinks_row = sbs(mixer1, "sinks_row", [1, NQ])
    c_row = sbs(mixer1, "c_row", [KD, P])
    invf = sbs(mixer1, "invf", [P, 1])
    pos_i = sbs(mixer1, "pos_i", [1, T], I32)
    pos_f = sbs(mixer1, "pos_f", [1, T])
    q_t = sbs(mixer1, "q_t", [P, KA, T])
    k_t = sbs(mixer1, "k_t", [P, T])
    v_tok = sbs(mixer1, "v_tok", [P, NT, P])
    prj = sbs(mixer1, "prj", [P, 2, T])
    s_sb = sbs(mixer1, "s_sb", [P, 2, 2, 2 * P])
    p_sb = sbs(mixer1, "p_sb", [P, 2, 2, 2 * P])
    p_t = sbs(mixer1, "p_t", [P, 2, 4 * P])
    st = sbs(mixer1, "st", [P, 2, 12])
    y_at = sbs(mixer1, "y_at", [P, KA, T])
    y_cv = sbs(mixer1, "y_cv", [P, 4, T])
    gb_sb = sbs(mixer1, "gb_sb", [P, 2, T])
    cbuf = sbs(mixer1, "cbuf", [P, 2, T + 2])
    cacc = sbs(mixer1, "cacc", [P, 2, T])
    ada_acc = sbs(mixer1, "ada_acc", [P, 2, D])
    x_tok = sbs(setup, "x_tok", [P, NT, D])
    vrow = sbs(setup, "vrow", [P, VB, P])
    setup.close()
    late = sbs(setup, "late", [P, RAW, D])
    setup.close()
    ang = [y_at[:, n, :] for n in range(4)] + [y_cv[:, n, :] for n in range(2)]

    x_landed, vec_landed, small_landed = sem("x_landed"), sem("vec_landed"), sem("small_landed")
    const_ready, x_turned, vec_turned = sem("const_ready"), sem("x_turned"), sem("vec_turned")
    vecs_ready, small_in, small_out, angle = sem("vecs_ready"), sem("small_in"), sem("small_out"), sem("angle")
    cact_ready, c_landed, c_turned = sem("cact_ready"), sem("c_landed"), sem("c_turned")
    n_vec_dmas = 0
    VEC_PLAN = []
    for sources, n in vec_src:
        row = sum(m for _, m in vec_src[:vec_src.index((sources, n))])
        done = 0
        while done < n:
            b, r = divmod(row + done, P)
            m = min(n - done, P - r)
            for cols, ap in sources:
                VEC_PLAN.append((vrow[r:r + m, b, cols], ap[done:done + m, :]))
            done += m
    LAST_ROWS = n_vec - (VB - 1) * P
    x_ready.claim(KD)

    def act_setup_dmas(act):
        x_in = A["x"].rearrange("b (t p) d -> (b t) p d", p=P)
        act.dma_start(c_row[:, :], A["c"].rearrange("b (k p) -> (b k) p", p=P)).then_inc(c_landed, 16)
        act.dma_start(pos_i[:, :], A["positions"]).then_inc(small_landed, 16)
        act.dma_start(sinks_row[:, :], A["attn_sinks"]).then_inc(small_landed, 16)
        act.dma_start(invf[:, :], A["inv_freq"]).then_inc(small_landed, 16)
        for t in range(NT):
            act.dma_start(x_tok[:, t, :], x_in[t]).then_inc(x_landed, 16)
        act.wait_ge(c_turned, 1)
        act.activation(cact[:, :], bank[4][:, 0:KD], ACT.Silu).then_inc(cact_ready, 1)
        for dst, src in VEC_PLAN:
            act.dma_start(dst, src).then_inc(vec_landed, 16)

    def pool_setup(pool):
        pool.memset(ident[:, :], 0.0).then_inc(const_ready, 1)
        pool.memset(ones[:, :], 1.0).then_inc(const_ready, 1)
        pool.memset(rot[:, :], 0.0).then_inc(const_ready, 1)
        pool.memset(mask[:, :], 0.0).then_inc(const_ready, 1)
        pool.wait_ge(const_ready, 4)
        pool.affine_select(out=ident[:, :], in_=ident[:, :], compare_op=ALU.not_equal, fill=1.0, base=0,
                           pattern=[[-1, P]], channel_multiplier=1).then_inc(const_ready, 1)
        lower = rot[:, :].rearrange("p (h s m) -> p h s m", h=2, s=2)
        pool.affine_select(out=lower[:, :, 0, :], in_=lower[:, :, 0, :], compare_op=ALU.not_equal, fill=-1.0,
                           base=-32, pattern=[[-HD, 2], [-1, 32]], channel_multiplier=1).then_inc(const_ready, 1)
        pool.wait_ge(const_ready, 6)
        pool.affine_select(out=lower[:, :, 1, :], in_=lower[:, :, 1, :], compare_op=ALU.not_equal, fill=1.0,
                           base=0, pattern=[[-HD, 2], [-1, 32]], channel_multiplier=1).then_inc(const_ready, 1)
        pool.affine_select(out=mask[:, :], in_=mask[:, :], compare_op=ALU.is_ge, fill=MASKED, base=P,
                           pattern=[[-1, 2 * P]], channel_multiplier=1).then_inc(const_ready, 1)
        pool.wait_ge(const_ready, 8)
        pool.affine_select(out=mask[:, :], in_=mask[:, :], compare_op=ALU.is_gt, fill=MASKED, base=0,
                           pattern=[[1, 2 * P]], channel_multiplier=-1).then_inc(const_ready, 1)
        pool.memset(cbuf[:, :, 0:2], 0.0).then_inc(const_ready, 1)

    CONSTS = 10

    def pe_setup(pe):
        pe.wait_ge(const_ready, CONSTS)
        pe.wait_ge(c_landed, 16)
        pe.transpose(bank[4][:, 0:KD], c_row[:, :], ident[0:KD, 0:KD]).then_inc(c_turned, 1)
        pe.wait_ge(small_in, 1)
        pe.matmul(bank[2][:, :], ones[0:1, :], pos_f[:, :], start=True, stop=True)
        pe.matmul(bank[3][:, 0:NQ], ones[0:1, :], sinks_row[:, :], start=True, stop=True).then_inc(small_out, 1)
        pe.wait_ge(x_landed, 16 * NT)
        for k in range(KD):
            wait(pe, x_ready.sem, k - 1)
            for t in range(NT):
                tr = pe.transpose(bank[k % 2][:, t * P:(t + 1) * P], x_tok[:, t, k * P:(k + 1) * P], ident[:, :])
            tr.then_inc(x_turned, 1)
        pe.wait_ge(vec_landed, 16 * len(VEC_PLAN))
        for b in range(VB):
            m = P if b < VB - 1 else LAST_ROWS
            tr = pe.transpose(bank[5][:, b * P:b * P + m], vrow[0:m, b, :], ident[0:m, 0:m])
        tr.then_inc(vec_turned, 1)

    def act_setup(act):
        for k in range(KD):
            act.wait_ge(x_turned, k + 1)
            act.activation(x[:, k, :], bank[k % 2][:, :], ACT.Copy).then_inc(x_ready.sem, 1)
        act.wait_ge(vec_turned, 1)
        act.activation(vecs[:, 0:n_vec], bank[5][:, 0:n_vec], ACT.Copy).then_inc(vecs_ready, 1)

    def dve_positions(dve):
        dve.wait_ge(small_landed, 48)
        dve.tensor_copy(pos_f[:, :], pos_i[:, :]).then_inc(small_in, 1)

    def dve_angles(dve):
        dve.wait_ge(small_out, 1)
        dve.tensor_copy(sinks[:, :], bank[3][:, 0:NQ]).then_inc(angle, 1)
        steps = [0]

        def step(ins):
            ins.then_inc(angle, 1)
            steps[0] += 1
            dve.wait_ge(angle, steps[0] + 1)

        a = lambda n: ang[n]
        step(dve.tensor_scalar(a(0), bank[2][:, :], invf[:, 0:1], None, ALU.mult))
        for n, quarter, shift, dst in ((1, 0.0, 0.0, a(4)), (2, 0.25, float(np.pi / 2), a(5))):
            step(dve.tensor_scalar(a(n), a(0), 1 / TWO_PI, quarter, ALU.mult, ALU.add))
            step(dve.tensor_scalar(a(3), a(n), ROUND, ROUND, ALU.add, ALU.subtract))
            step(dve.scalar_tensor_tensor(a(n), a(3), -TURN1, a(0), ALU.mult, ALU.add))
            step(dve.scalar_tensor_tensor(dst, a(3), -TURN2, a(n), ALU.mult, ALU.add))
            step(dve.scalar_tensor_tensor(a(n), a(3), -TURN3, dst, ALU.mult, ALU.add))
            step(dve.tensor_scalar(a(3), a(n), shift, 3.1415925, ALU.add, ALU.min))
            step(dve.tensor_scalar(dst, a(3), -3.1415925, None, ALU.max))

    ANGLES = 16

    def act_angles(act):
        act.wait_ge(angle, ANGLES)
        act.activation(sin_t[:, :], ang[4], ACT.Sin).then_inc(rope_ready, 1)
        act.activation(cos_t[:, :], ang[5], ACT.Sin).then_inc(rope_ready, 1)

    rope_ready = sem("rope_ready")

    ada_scaled, ada_evac, gain_ready = sem("ada_scaled"), sem("ada_evac"), count("gain_ready")
    ada_sum = sem("ada_sum")
    ADA_BATCH = [(0, 2), (2, 4), (4, 6)]

    def ada_accumulate(eng, m):
        part, k = divmod(m, KD)
        if m < EARLY:
            at = at_ada[m]
            rows_, there, value = raw[:, at.raw_slot, 0:D], landed[at.raw_slot], landed_at(at)
        else:
            rows_, there, value = late[:, m % RAW, :], late_landed[m % RAW], ((m - EARLY) // RAW + 1) * 16
        acc, c_ = ada_acc[:, part % 2, :], cact[:, k:k + 1]
        if m == 0:
            eng.wait_ge(cact_ready, 1)
        if k == 0 and part >= 2:
            eng.wait_ge(ada_sum, part - 1)
        eng.wait_ge(there, value)
        if k:
            eng.wait_ge(*ada_used(m - 1))
        if k == 0:
            ins = eng.tensor_scalar(acc, rows_, c_, None, ALU.mult)
        elif m < EARLY:
            ins = eng.scalar_tensor_tensor(acc, rows_, c_, acc, ALU.mult, ALU.add)
        else:
            n = (part - 2) * (KD - 1) + k
            eng.tensor_scalar(rows_, rows_, c_, None, ALU.mult).then_inc(ada_scaled, 1)
            eng.wait_ge(ada_scaled, n)
            ins = eng.tensor_tensor(acc, acc, rows_, ALU.add)
        ins.then_inc(ada_used(m)[0], 1)

    def ada_sums(pe, part):
        pe.wait_ge(*ada_used((part + 1) * KD - 1))
        batch = part // 2
        if batch == 2:
            pe.wait_ge(ada_evac, 2)
        for n in range(KD):
            m = part * KD + n
            mm = pe.matmul(bank[ADA_BANKS[batch]][:, m:m + 1], ada_acc[:, part % 2, n * P:(n + 1) * P],
                           ones[:, 0:1], start=True, stop=True)
        mm.then_inc(ada_sum, 1)

    def ada_add(dve, batch):
        a, b = ADA_BATCH[batch]
        dve.wait_ge(ada_sum, b)
        if batch == 0:
            dve.wait_ge(vecs_ready, 1)
        ab, a, b = col["ada_b"], a * KD, b * KD
        dve.tensor_tensor(mod[:, a:b], bank[ADA_BANKS[batch]][:, a:b], vecs[:, ab + a:ab + b], ALU.add)\
           .then_inc(ada_evac, 1)
        dve.wait_ge(ada_evac, batch + 1)

    def scaled_gain(dve, name, scale):
        g0 = gain_ready.claim(1)
        dve.scalar_tensor_tensor(gain[:, :], mod[:, scale * KD:(scale + 1) * KD], 1.0,
                                 vecs[:, col[name]:col[name] + KD], ALU.add, ALU.mult).then_inc(gain_ready.sem, 1)
        dve.wait_ge(gain_ready.sem, g0 + 1)

    def mod_col(part):
        return lambda k: mod[:, part * KD + k:part * KD + k + 1]

    def from_start(eng, k):
        eng.wait_ge(x_ready.sem, k + 1)

    x_tile = lambda k: x[:, k, :]
    norm1 = Norm(x_tile, KD, from_start)
    split1 = Split(x_tile, KD, lambda k: gain[:, k:k + 1], mod_col(0), lambda k: h_hi[:, k, :],
                   lambda k: h_lo[:, k, :], lambda eng: None)
    N_PRE = 6
    prj_ready, rot_done, rope_done = sem("prj_ready"), sem("rot_done"), sem("rope_done")
    vT_done, v_ready = sem("vT_done"), sem("v_ready")
    gb_ready, conv_p, conv_done = sem("gb_ready"), sem("conv_p"), sem("conv_done")
    sc_done, s_ready, stat, e_ready = sem("sc_done"), sem("s_ready"), sem("stat"), sem("e_ready")
    probs_ready, pT_done, pT_ready, pv_done, y_ready = (sem(n) for n in (
        "probs_ready", "pT_done", "pT_ready", "pv_done", "y_ready"))
    STEPS = [(2 * jj + js, n) for jj in range(2) for n in range(NT) for js in range(2)]
    SC, PT, PV, MIX = (3, 4), 7, 5, (0, 1, 2)

    def act_ahead(act, u, kts=KD):
        split_hi(act, first[u + 2], kts)

    def pe_in(pe, u, ks=range(KD)):
        if u < N_PRE:
            b = u % 2
            if u >= 2:
                pe.wait_ge(prj_ready, u - 1)
        else:
            j, part = divmod(u - N_PRE, 3)
            b = MIX[part]
            if j >= 1:
                pe.wait_ge(conv_done, j)
            elif part < 2:
                pe.wait_ge(prj_ready, N_PRE)
        unit_products(pe, at_in[u], KD, bank[b][:, :], lambda k: h_hi[:, k, :], lambda k: h_lo[:, k, :],
                      True, True, split1.pe_ready(pe) if u == 0 else None, ks)

    def act_in(act, u):
        act_ahead(act, u)
        at = at_in[u]
        if u < N_PRE:
            bias = v("bq", u) if u < 4 else v("b_in", u - 4)
            act.wait_ge(unit_done, at.count)
            if u >= 2:
                act.wait_ge(rope_done, u - 1)
            act.activation(prj[:, u % 2, :], bank[u % 2][:, :], ACT.Identity, bias=bias).then_inc(prj_ready, 1)
        elif (u - N_PRE) % 3 == 0:
            j = (u - N_PRE) // 3
            act.wait_ge(unit_done, at.count)
            wait(act, conv_p, j - 1)
            act.activation(gb_sb[:, j % 2, :], bank[MIX[0]][:, :], ACT.Identity, bias=v("b_in", 2 + j))\
               .then_inc(gb_ready, 1)

    def dve_in(dve, u):
        split_lo(dve, first[u + 2])
        at = at_in[u]
        if u >= N_PRE and (u - N_PRE) % 3 == 2:
            j = (u - N_PRE) // 3
            dve.wait_ge(unit_done, at.count)
            dve.wait_ge(gb_ready, j + 1)
            wait(dve, conv_done, j - 1)
            if j == 0:
                dve.wait_ge(rope_done, 5)
            c, acc = cbuf[:, j % 2, :], cacc[:, j % 2, :]
            dve.scalar_tensor_tensor(c[:, 2:T + 2], bank[MIX[2]][:, :], v("b_in", 10 + j), gb_sb[:, j % 2, :],
                                     ALU.add, ALU.mult).then_inc(conv_p, 1)
            dve.wait_ge(conv_p, j + 1)
            conv_taps(dve, acc, c, lambda w: v("conv_w", 4 * w + j), conv_t, 3 * j)
            dve.scalar_tensor_tensor(y_cv[:, j, :], bank[MIX[1]][:, :], v("b_in", 6 + j), acc,
                                     ALU.add, ALU.mult).then_inc(conv_done, 1)

    conv_t = sem("conv_t")

    def conv_taps(dve, acc, c, w, sem_t, base):
        dve.tensor_scalar(acc, c[:, 0:T], w(0), None, ALU.mult).then_inc(sem_t, 1)
        dve.wait_ge(sem_t, base + 1)
        dve.scalar_tensor_tensor(acc, c[:, 1:T + 1], w(1), acc, ALU.mult, ALU.add).then_inc(sem_t, 1)
        dve.wait_ge(sem_t, base + 2)
        dve.scalar_tensor_tensor(acc, c[:, 2:T + 2], w(2), acc, ALU.mult, ALU.add).then_inc(sem_t, 1)
        dve.wait_ge(sem_t, base + 3)

    def pe_rotate(pe, u):
        pe.wait_ge(prj_ready, u + 1)
        if u == 5:
            for t in range(NT):
                tr = pe.transpose(bank[PT][:, t * P:(t + 1) * P], prj[:, 1, t * P:(t + 1) * P], ident[:, :])
            tr.then_inc(vT_done, 1)
            return
        wait(pe, rope_done, u - 1)
        pe.matmul(bank[2 + u % 2][:, :], rot[:, :], prj[:, u % 2, :], start=True, stop=True).then_inc(rot_done, 1)

    def dve_rotate(dve, u):
        dve.wait_ge(rot_done, u + 1)
        if u == 0:
            dve.wait_ge(rope_ready, 2)
        dst = q_t[:, u, :] if u < 4 else k_t[:, :]
        r0 = 2 * u
        wait(dve, rope_done, u)
        dve.tensor_tensor(tmp2[:, 0, :], prj[:, u % 2, :], cos_t[:, :], ALU.mult).then_inc(rope_step, 1)
        dve.tensor_tensor(tmp2[:, 1, :], bank[2 + u % 2][:, :], sin_t[:, :], ALU.mult).then_inc(rope_step, 1)
        dve.wait_ge(rope_step, r0 + 2)
        dve.tensor_tensor(dst, tmp2[:, 0, :], tmp2[:, 1, :], ALU.add).then_inc(rope_done, 1)

    rope_step = sem("rope_step")
    tmp2 = cacc

    def pe_scores(pe, i):
        j, n = STEPS[i]
        if i == 0:
            pe.wait_ge(rope_done, 5)
        wait(pe, s_ready, 2 * i)
        k0 = max(n - 1, 0) * P
        keys = (n + 1) * P - k0
        for h in range(2):
            r = slice(h * HD, (h + 1) * HD)
            mm = pe.matmul(bank[SC[h]][:, 2 * P - keys:2 * P], q_t[r, j, n * P:(n + 1) * P],
                           k_t[r, k0:k0 + keys], start=True, stop=True)
        mm.then_inc(sc_done, 1)

    def key_range(n):
        return slice(P if n == 0 else 0, 2 * P)

    def dve_softmax_a(dve, i):
        j, n = STEPS[i]
        kr = key_range(n)
        s, m = s_sb[:, i % 2, :, kr], st[:, i % 2, :]
        dve.wait_ge(sc_done, i + 1)
        wait(dve, e_ready, 3 * (i - 1))
        wait(dve, probs_ready, 2 * (i - 1))
        for h in range(2):
            dve.scalar_tensor_tensor(s[:, h, :], bank[SC[h]][:, kr], HD ** -0.5, mask[:, kr],
                                     ALU.mult, ALU.add).then_inc(s_ready, 1)
        dve.wait_ge(s_ready, 2 * i + 2)
        dve.tensor_reduce(m[:, 0:2], s, AX_X, ALU.max).then_inc(stat, 1)
        dve.wait_ge(stat, 4 * i + 1)
        snk = sinks[:, j:j + 5:4]
        dve.tensor_tensor(m[:, 0:2], m[:, 0:2], snk, ALU.max).then_inc(stat, 1)
        dve.wait_ge(stat, 4 * i + 2)
        dve.tensor_scalar(m[:, 2:4], m[:, 0:2], -1.0, None, ALU.mult).then_inc(stat, 1)
        dve.tensor_tensor(m[:, 4:6], snk, m[:, 0:2], ALU.subtract).then_inc(stat, 1)

    def act_exp(act, i):
        j, n = STEPS[i]
        kr = key_range(n)
        m = st[:, i % 2, :]
        act.wait_ge(stat, 4 * i + 4)
        wait(act, pT_done, i - 1)
        for h in range(2):
            act.activation(p_sb[:, i % 2, h, kr], s_sb[:, i % 2, h, kr], ACT.Exp, bias=m[:, 2 + h:3 + h],
                           accum_out=m[:, 8 + h:9 + h]).then_inc(e_ready, 1)
        act.activation(m[:, 6:8], m[:, 4:6], ACT.Exp).then_inc(e_ready, 1)

    den_step = sem("den_step")

    def dve_softmax_b(dve, i):
        j, n = STEPS[i]
        kr = key_range(n)
        m = st[:, i % 2, :]
        dve.wait_ge(e_ready, 3 * i + 3)
        dve.tensor_tensor(m[:, 10:12], m[:, 8:10], m[:, 6:8], ALU.add).then_inc(den_step, 1)
        dve.wait_ge(den_step, 2 * i + 1)
        dve.reciprocal(m[:, 8:10], m[:, 10:12]).then_inc(den_step, 1)
        dve.wait_ge(den_step, 2 * i + 2)
        for h in range(2):
            dve.tensor_scalar(p_sb[:, i % 2, h, kr], p_sb[:, i % 2, h, kr], m[:, 8 + h:9 + h], None,
                              ALU.mult).then_inc(probs_ready, 1)

    def pe_turn_probs(pe, i):
        j, n = STEPS[i]
        pe.wait_ge(probs_ready, 2 * i + 2)
        if i == 0:
            pe.wait_ge(v_ready, 1)
        wait(pe, pT_ready, i)
        for h in range(2):
            for b in range(1 if n == 0 else 0, 2):
                s = 2 * h + b
                tr = pe.transpose(bank[PT][:, s * P:(s + 1) * P], p_sb[:, i % 2, h, b * P:(b + 1) * P], ident[:, :])
        tr.then_inc(pT_done, 1)

    def act_probs(act, i):
        j, n = STEPS[i]
        act.wait_ge(pT_done, i + 1)
        wait(act, pv_done, i - 1)
        kr = key_range(n)
        act.activation(p_t[:, i % 2, :].rearrange("p (h k) -> p h k", h=2)[:, :, kr],
                       bank[PT][:, :].rearrange("p (h k) -> p h k", h=2)[:, :, kr], ACT.Copy).then_inc(pT_ready, 1)

    def pe_values(pe, i):
        j, n = STEPS[i]
        pe.wait_ge(pT_ready, i + 1)
        if i % 2 == 0:
            wait(pe, y_ready, i // 2)
        r = slice(j % 2 * HD, (j % 2 + 1) * HD)
        for h in range(2):
            for b in range(1 if n == 0 else 0, 2):
                s = 2 * h + b
                mm = pe.matmul(bank[PV][r, h * P:(h + 1) * P], v_tok[:, n - 1 + b, h * HD:(h + 1) * HD],
                               p_t[:, i % 2, s * P:(s + 1) * P], start=b == 0 or n == 0, stop=b == 1)
        mm.then_inc(pv_done, 1)

    def act_values(act, i):
        if i % 2 == 1:
            j, n = STEPS[i]
            act.wait_ge(pv_done, i + 1)
            act.activation(y_at[:, j // 2:j // 2 + 3:2, n * P:(n + 1) * P],
                           bank[PV][:, 0:2 * P].rearrange("p (h t) -> p h t", h=2), ACT.Copy).then_inc(y_ready, 1)

    KS = (N_IN - N_PRE) * KD // len(STEPS)

    def pieces(i):
        tiles = [divmod(s, KD) for s in range(i * KS, (i + 1) * KS)]
        return [(N_PRE + u, [k for n, k in tiles if n == u]) for u in sorted({n for n, _ in tiles})]

    def ended(i):
        return [u for u, ks in pieces(i) if ks[-1] == KD - 1]

    def pe_mixer1(pe):
        for part in range(2):
            ada_sums(pe, part)
        norm1.pe_sums(pe)
        for u in range(N_PRE):
            pe_in(pe, u)
            if u >= 1:
                pe_rotate(pe, u - 1)
        pe_rotate(pe, N_PRE - 1)
        pe_scores(pe, 0)
        for i in range(len(STEPS)):
            for u, ks in pieces(i):
                pe_in(pe, u, ks)
            if i + 1 < len(STEPS):
                pe_scores(pe, i + 1)
            if i:
                pe_values(pe, i - 1)
            pe_turn_probs(pe, i)
            if i == 7:
                ada_sums(pe, 2)
            if i == 13:
                ada_sums(pe, 3)
        pe_values(pe, len(STEPS) - 1)
        for u in range(N_O):
            pe_out_unit(pe, u)
            if u == 0:
                norm_cv.pe_sums(pe)
                norm_at.pe_sums(pe)
            if u == 2:
                ada_sums(pe, 4)
            if u == 6:
                ada_sums(pe, 5)

    def pe_out_unit(pe, u):
        at = at_o[u]
        pe.wait_ge(lo_ready, at.count)
        wait(pe, o_used, u - 1)
        for n, (half, k0) in enumerate(((half_cv, KA), (half_at, 0))):
            dst = bank[2 * (u % 2) + n][:, :]
            for k in range(k0, k0 + half.n):
                if u == 0:
                    pe.wait_ge(h_ready.sem, half.h0 + k - k0 + 1)
                w_hi, w_lo = (w[:, at.slot, k * P:(k + 1) * P] for w in (whi, wlo))
                pe.matmul(dst, w_hi, h_hi[:, k, :], start=k == k0, stop=False)
                pe.matmul(dst, w_hi, h_lo[:, k, :], start=False, stop=False)
                mm = pe.matmul(dst, w_lo, h_hi[:, k, :], start=False, stop=k == k0 + half.n - 1)
        mm.then_inc(unit_done, 1)

    def act_mixer1(act):
        split_hi(act, first[0])
        split_hi(act, first[1])
        norm1.act_squares(act)
        norm1.act_root(act)
        act_angles(act)
        split1.act(act)
        for u in range(N_PRE):
            act_in(act, u)
        act.wait_ge(vT_done, 1)
        act.activation(v_tok[:, :, :], bank[PT][:, :].rearrange("p (t c) -> p t c", t=NT), ACT.Copy)\
           .then_inc(v_ready, 1)
        act_exp(act, 0)
        for i in range(len(STEPS)):
            for u in ended(i):
                act_in(act, u)
            if i + 1 < len(STEPS):
                act_exp(act, i + 1)
            if i:
                act_values(act, i - 1)
            act_probs(act, i)
        act_values(act, len(STEPS) - 1)
        for half, norm in ((half_cv, norm_cv), (half_at, norm_at)):
            for k in range(half.n):
                half.act_hi(act, k)
            norm.act_squares(act)
        norm_cv.act_root(act)
        norm_at.act_root(act)
        split_hi(act, first[N_IN + 2])
        for u in range(N_O):
            if u:
                split_hi(act, first[N_IN + u + 2])
            ffn0.norm.act_square(act, u)

    def dve_mixer1(dve):
        dve_positions(dve)
        for m in range(2 * KD):
            if m == KD:
                dve_angles(dve)
            ada_accumulate(dve, m)
        split_lo(dve, first[0])
        ada_add(dve, 0)
        scaled_gain(dve, "norm1", 1)
        norm1.dve_rstd(dve)
        split_lo(dve, first[1])
        split1.dve(dve)
        for u in range(N_PRE):
            dve_in(dve, u)
            if u >= 1:
                dve_rotate(dve, u - 1)
        dve_softmax_a(dve, 0)
        dve_softmax_b(dve, 0)
        for i in range(len(STEPS)):
            for u in ended(i):
                dve_in(dve, u)
            if i + 1 < len(STEPS):
                dve_softmax_a(dve, i + 1)
                dve_softmax_b(dve, i + 1)
        for half in (half_cv, half_at):
            for k in range(half.n):
                half.dve_lo(dve, k)
        norm_cv.dve_mean(dve)
        norm_at.dve_mean(dve)
        split_lo(dve, first[N_IN + 2])
        norm_cv.dve_rstd(dve, mean=False)
        norm_at.dve_rstd(dve, mean=False)
        ada_add(dve, 1)
        for u in range(N_O):
            if u:
                split_lo(dve, first[N_IN + u + 2])
            dve.wait_ge(unit_done, at_o[u].count)
            wait(dve, o_used, u)
            b, s = 2 * (u % 2), out_step_n * u
            dve.tensor_tensor(tmp[:, 0, :], bank[b][:, :], rstd[:, :], ALU.mult).then_inc(out_step, 1)
            dve.tensor_tensor(tmp[:, 1, :], bank[b + 1][:, :], rstd_at, ALU.mult).then_inc(out_step, 1)
            dve.wait_ge(out_step, s + 2)
            dve.tensor_tensor(tmp[:, 0, :], tmp[:, 0, :], tmp[:, 1, :], ALU.add).then_inc(out_step, 1)
            dve.wait_ge(out_step, s + 3)
            dve.scalar_tensor_tensor(x[:, u, :], tmp[:, 0, :], mod[:, 2 * KD + u:2 * KD + u + 1], x[:, u, :],
                                     ALU.mult, ALU.add).then_inc(o_used, 1)
        ada_add(dve, 2)
        dve.wait_ge(ada_evac, 3)

    o_used = sem("o_used")
    norm_cv = Norm(lambda k: y_cv[:, k, :], 4, lambda eng, k: eng.wait_ge(conv_done, k + 1),
                   slots=[sq[:, 0, :], sq[:, 1, :], sq_sum[:, :], prj[:, 0, :]])
    rstd_at, out_step, out_step_n = tmp[:, 2, :], sem("out_step"), 3
    norm_at = Norm(lambda k: y_at[:, k, :], KA, lambda eng, k: eng.wait_ge(y_ready, 2 * NT), rstd_=rstd_at,
                   var_=prj[:, 1, :],
                   slots=[gb_sb[:, 0, :], gb_sb[:, 1, :], cacc[:, 0, :], cacc[:, 1, :]])
    half_cv = Halves(lambda k: y_cv[:, k, :], 4, lambda k: v("gcv", k), lambda k: h_hi[:, KA + k, :],
                     lambda k: h_lo[:, KA + k, :], norm_cv.ready, (unit_done, N_IN))
    half_at = Halves(lambda k: y_at[:, k, :], KA, lambda k: v("ga", k), lambda k: h_hi[:, k, :],
                     lambda k: h_lo[:, k, :], norm_at.ready)

    mixer1.close()

    g_copied, taps, conv_c, s_act = (count(n) for n in ("g_copied", "taps", "conv_c", "s_act"))
    g_scaled, s_scaled = count("g_scaled"), count("s_scaled")
    ft_ready, fhi_ready, f_ready = count("ft_ready"), count("fhi_ready"), count("f_ready")
    o_ready, x_step, x_new = count("o_ready"), count("x_step"), count("x_new")
    N_UP, N_DOWN = KF // 2, KD // 2

    class Residual:

        def __init__(self, o, gains):
            self.o, self.gains = o, gains
            self.s0, self.x0 = x_step.claim(KD), x_new.claim(KD)

        def dve(self, dve):
            for k in range(KD):
                self.scale(dve, k)
                if k:
                    self.add(dve, k - 1)
            self.add(dve, KD - 1)

        def scale(self, dve, k):
            wait(dve, x_new.sem, self.x0 + k - 2)
            dve.scalar_tensor_tensor(tmp[:, k % 3, :], self.o(k), self.gains(k), rstd[:, :],
                                     ALU.mult, ALU.mult).then_inc(x_step.sem, 1)

        def add(self, dve, k):
            dve.wait_ge(x_step.sem, self.s0 + k + 1)
            dve.tensor_tensor(x[:, k, :], x[:, k, :], tmp[:, k % 3, :], ALU.add).then_inc(x_new.sem, 1)

        def ready(self, eng, k):
            eng.wait_ge(x_new.sem, self.x0 + k + 1)

    class Lead:

        def __init__(self, res, gains, hi, lo, norm):
            self.res, self.norm = res, norm
            self.half = Halves(x_tile, KD, gains, hi, lo, res.ready)

        def dve(self, dve):
            for k in range(KD):
                self.res.scale(dve, k)
                if k >= 1:
                    self.res.add(dve, k - 1)
                if k >= 2:
                    self.half.dve_lo(dve, k - 2)
            self.res.add(dve, KD - 1)
            self.half.dve_lo(dve, KD - 2)
            self.half.dve_lo(dve, KD - 1)

        def act(self, act):
            for k in range(KD):
                self.half.act_hi(act, k)
                self.norm.act_square(act, k)

    class FFN:

        def __init__(self, tag, at0, before, gains, shift, w_gate, w_up, w_down, conv, out_gains, final=False):
            self.at0, self.conv, self.final = at0, conv, final
            self.w_gate, self.w_up, self.w_down = w_gate, w_up, w_down
            self.at1 = at0.plus(2 * KF)
            self.end = self.at1.plus(2 * KD)
            mem = ExitStack()
            self.f_hi = sbs(mem, f"f_hi{tag}", [P, KF, T], F32R)
            self.f_lo = sbs(mem, f"f_lo{tag}", [P, KF, T], F32R)
            if conv:
                self.gbuf = sbs(mem, "gbuf", [P, 2, T + 2])
            with ExitStack() as part:
                h_hi = sbs(part, f"fh_hi{tag}", [P, KD, T], F32R)
                h_lo = sbs(part, f"fh_lo{tag}", [P, KD, T], F32R)
            if not conv:
                self.o = sbs(mem, f"fo{tag}", [P, KD, T])
            mem.close()
            self.h_hi, self.h_lo = h_hi, h_lo
            hi, lo = lambda k: h_hi[:, k, :], lambda k: h_lo[:, k, :]
            if conv:
                self.norm = Norm(x_tile, KD, before)
                self.split = Split(x_tile, KD, gains, shift, hi, lo, lambda eng: None)
                self.pe_ready = self.split.pe_ready
            else:
                self.norm = Norm(x_tile, KD, before.ready)
                self.lead = Lead(before, gains, hi, lo, self.norm)
                self.pe_ready = self.lead.half.pe_ready
            self.c0 = {c: c.claim(n) for c, n in (
                (g_copied, KF), (taps, 2 * KF), (conv_c, KF), (s_act, KF), (ft_ready, KF), (fhi_ready, KF),
                (f_ready, KF), (o_ready, KD), (g_scaled, 0 if conv else KF), (s_scaled, 0 if conv else KF))}
            if not conv:
                self.norm_o = Norm(lambda k: tile_at(self.o, k), KD, self.o_tile_ready)
                self.res = Residual(lambda k: self.o[:, k, :], out_gains)
                self.ready = self.res.ready
            else:
                self.ready = self.o_tile_ready
                self.norm_o = Norm(lambda k: tile_at(x, k), KD, self.o_tile_ready)
                self.out_gate = out_gains

        def o_tile_ready(self, eng, k):
            eng.wait_ge(o_ready.sem, k + (self.c0[o_ready] + 1))

        def at_up(self, i, k):
            return At(self.at0.c + k, self.at0.u + k, 4, i) if not isinstance(i, int) else self.at0.plus(4 * i + k)

        def at_down(self, i, k):
            return At(self.at1.c + k, self.at1.u + k, 4, i) if not isinstance(i, int) else self.at1.plus(4 * i + k)

        def sp(self, sp):
            def up(i, last):
                for k in range(4):
                    at = self.at_up(i, k)
                    w = (self.w_gate, self.w_up)[k % 2]
                    load(sp, at, unit_parts(at, w, (0, KD), (i * 2 * P + k // 2 * P, P)),
                         (lo_ready, at.plus(-RAW).count))

            def down(i, last):
                for k in range(4):
                    at = self.at_down(i, k)
                    load(sp, at, unit_parts(at, self.w_down, (k % 2 * HALF, HALF), (i * 2 * P + k // 2 * P, P)),
                         (lo_ready, at.plus(-RAW).count))

            loop(sp, N_UP, up)
            loop(sp, N_DOWN, down)

        def pe(self, pe):
            c = self.c0
            if self.conv:
                self.norm.pe_sums(pe)

            def up(i, last):
                for q in range(2):
                    p = i * 2 + q
                    if not isinstance(i, int) or p >= 2:
                        pe.wait_ge(ft_ready.sem, p + (c[ft_ready] - 1))
                    for g in range(2):
                        ready = self.pe_ready(pe) if isinstance(i, int) and i + q + g == 0 else None
                        unit_products(pe, self.at_up(i, 2 * q + g), KD, bank[2 * q + g][:, :],
                                      lambda k: self.h_hi[:, k, :], lambda k: self.h_lo[:, k, :], True, True, ready)
                        if ready is not None and not self.conv:
                            self.norm.pe_sums(pe)

            def down(i, last):
                for q in range(2):
                    o = i * 2 + q
                    if not isinstance(i, int) or o >= 2:
                        pe.wait_ge(o_ready.sem, o + (c[o_ready] - 1))
                        if not self.conv:
                            pe.wait_ge(sq_ready.sem, o + (self.norm_o.sq0 - 1))
                    for g in range(2):
                        ready = None
                        if isinstance(i, int) and i + q == 0:
                            ready = lambda k, g=g: pe.wait_ge(f_ready.sem, c[f_ready] + g * HALF + k + 1)
                        unit_products(pe, self.at_down(i, 2 * q + g), HALF, bank[q][:, :],
                                      lambda k: self.f_hi[:, g * HALF + k, :], lambda k: self.f_lo[:, g * HALF + k, :],
                                      g == 0, g == 1, ready)

            loop(pe, N_UP, up)
            loop(pe, N_DOWN, down)
            self.norm_o.pe_sums(pe)

        def act(self, act):
            c = self.c0
            if self.conv:
                self.norm.act_root(act)
                self.split.act(act)
            else:
                self.lead.act(act)
            acc, ft = sq, tmp

            def up(i, last):
                kts = HALF if last else KD
                for q in range(2):
                    p = i * 2 + q
                    far = q == 1
                    gate, up_ = self.at_up(i, 2 * q), self.at_up(i, 2 * q + 1)
                    split_hi(act, gate.plus(2), HALF if last and far else KD)
                    if not self.conv and isinstance(p, int) and p == 0:
                        self.norm.act_root(act)
                    if self.conv:
                        act.wait_ge(unit_done, gate.count)
                        if not isinstance(i, int) or p >= 2:
                            act.wait_ge(conv_c.sem, p + (c[conv_c] - 1))
                        act.activation(self.gbuf[:, q, 2:T + 2], bank[2 * q][:, :], ACT.Copy)\
                           .then_inc(g_copied.sem, 1)
                    split_hi(act, up_.plus(2), HALF if last and far else KD)
                    if self.conv:
                        act.wait_ge(conv_c.sem, p + (c[conv_c] + 1))
                        act.activation(acc[:, q, :], acc[:, q, :], ACT.Silu,
                                       bias=col_at(vecs, p + col["ffn_cb"])).then_inc(s_act.sem, 1)
                    else:
                        act.wait_ge(g_scaled.sem, p + (c[g_scaled] + 1))
                        act.activation(acc[:, q, :], acc[:, q, :], ACT.Silu).then_inc(s_act.sem, 1)
                    act.wait_ge(ft_ready.sem, p + (c[ft_ready] + 1))
                    act.activation(tile_at(self.f_hi, p), ft[:, q, :], ACT.Copy).then_inc(fhi_ready.sem, 1)

            def down(i, last):
                for q in range(2):
                    o = i * 2 + q
                    lagging = self.conv and not (isinstance(o, int) and o == 0)
                    if lagging:
                        self.o_tile_ready(act, o - 1)
                        self.norm_o.act_slot_free(act, o - 1)
                    for g in range(2):
                        at = self.at_down(i, 2 * q + g)
                        ends = last and q == 1
                        if not (ends and self.final):
                            split_hi(act, at.plus(2), KD if ends else HALF)
                    if lagging:
                        self.norm_o.act_square_of(act, tile_at(x, o - 1), 1 - q)
                    if not self.conv:
                        act.wait_ge(unit_done, at.count)
                        act.activation(tile_at(self.o, o), bank[q][:, :], ACT.Copy).then_inc(o_ready.sem, 1)
                        self.norm_o.act_slot_free(act, o)
                        self.norm_o.act_square_of(act, bank[q][:, :], q)
                if last and self.conv:
                    self.norm_o.act_square(act, KD - 1)

            loop(act, N_UP, up)
            loop(act, N_DOWN, down)
            self.norm_o.act_root(act)

        def dve(self, dve):
            c = self.c0
            acc, ft = sq, tmp
            if self.conv:
                dve.memset(self.gbuf[:, :, 0:2], 0.0).then_inc(gpad_ready, 1)
                dve.wait_ge(gpad_ready, 1)
            if self.conv:
                self.norm.dve_rstd(dve)
                self.split.dve(dve)
            else:
                self.lead.dve(dve)

            def up(i, last):
                for q in range(2):
                    p = i * 2 + q
                    later = not isinstance(i, int) or p >= 2
                    gate, up_ = self.at_up(i, 2 * q), self.at_up(i, 2 * q + 1)
                    split_lo(dve, gate.plus(2), HALF if last and q == 1 else KD)
                    if self.conv:
                        dve.wait_ge(g_copied.sem, p + (c[g_copied] + 1))
                        if later:
                            dve.wait_ge(ft_ready.sem, p + (c[ft_ready] - 1))
                        b, t0 = self.gbuf[:, q, :], p * 2 + c[taps]
                        w = lambda n: col_at(vecs, p + (col["ffn_cw"] + n * KF))
                        a = acc[:, q, :]
                        dve.tensor_scalar(a, b[:, 0:T], w(0), None, ALU.mult).then_inc(taps.sem, 1)
                        dve.wait_ge(taps.sem, t0 + 1)
                        dve.scalar_tensor_tensor(a, b[:, 1:T + 1], w(1), a, ALU.mult, ALU.add).then_inc(taps.sem, 1)
                        dve.wait_ge(taps.sem, t0 + 2)
                        dve.scalar_tensor_tensor(a, b[:, 2:T + 2], w(2), a, ALU.mult, ALU.add).then_inc(conv_c.sem, 1)
                    else:
                        if isinstance(p, int) and p == 0:
                            self.norm.dve_rstd(dve)
                        dve.wait_ge(unit_done, gate.count)
                        if later:
                            dve.wait_ge(ft_ready.sem, p + (c[ft_ready] - 1))
                        dve.tensor_tensor(acc[:, q, :], bank[2 * q][:, :], rstd[:, :], ALU.mult)\
                           .then_inc(g_scaled.sem, 1)
                    split_lo(dve, up_.plus(2), HALF if last and q == 1 else KD)
                    if self.conv:
                        dve.wait_ge(s_act.sem, p + (c[s_act] + 1))
                    else:
                        dve.wait_ge(s_scaled.sem, p + (c[s_scaled] + 1))
                    dve.wait_ge(unit_done, up_.count)
                    if later:
                        dve.wait_ge(f_ready.sem, p + (c[f_ready] - 1))
                    dve.tensor_tensor(ft[:, q, :], bank[2 * q + 1][:, :], acc[:, q, :], ALU.mult)\
                       .then_inc(ft_ready.sem, 1)
                    dve.wait_ge(fhi_ready.sem, p + (c[fhi_ready] + 1))
                    dve.tensor_tensor(tile_at(self.f_lo, p), ft[:, q, :], tile_at(self.f_hi, p).bitcast(F32),
                                      ALU.subtract).then_inc(f_ready.sem, 1)

            def down(i, last):
                for q in range(2):
                    for g in range(2):
                        at = self.at_down(i, 2 * q + g)
                        ends = last and q == 1
                        if not (ends and self.final):
                            split_lo(dve, at.plus(2), KD if ends else HALF)
                    if self.conv:
                        o = i * 2 + q
                        dve.wait_ge(unit_done, at.count)
                        dve.scalar_tensor_tensor(tile_at(x, o), bank[q][:, :], col_at(mod, o + self.out_gate),
                                                 tile_at(x, o), ALU.mult, ALU.add).then_inc(o_ready.sem, 1)

            loop(dve, N_UP, up)
            loop(dve, N_DOWN, down)
            if not self.conv:
                self.norm_o.dve_rstd(dve)
            if self.final:
                self.res.dve(dve)

        def pool(self, pool):
            c = self.c0
            self.norm.pool_sum(pool)

            def up(i, last):
                for q in range(2):
                    p = i * 2 + q
                    pool.wait_ge(s_act.sem, p + (c[s_act] + 1))
                    pool.tensor_tensor(sq[:, q, :], sq[:, q, :], rstd[:, :], ALU.mult).then_inc(s_scaled.sem, 1)

            loop(pool, N_UP, up)
            self.norm_o.pool_sum(pool)

    gpad_ready = sem("gpad_ready")
    w_up0 = A["w_up"].rearrange("a k n -> (a k) n")
    ffn0 = FFN("0", At(len(seq), u_next), lambda eng, k: eng.wait_ge(o_used, k + 1),
               lambda k: gain[:, k:k + 1], mod_col(3), w_up0[:, 0:DFF], w_up0[:, DFF:2 * DFF],
               A["w_down"].rearrange("a k n -> (a k) n"), True, 5 * KD)

    norm_f = ffn0.norm_o
    x_normed = sem("x_normed")

    def dve_final(dve):
        norm_f.dve_rstd(dve)
        dve.wait_ge(std_ready.sem, norm_f.std0 + 1)
        for k in range(KD):
            dve.scalar_tensor_tensor(x[:, k, :], x[:, k, :], v("final", k), rstd[:, :], ALU.mult, ALU.mult)\
               .then_inc(x_normed, 1)

    def normed(eng, k):
        eng.wait_ge(x_normed, k + 1)

    W_LORA, A_LORA, G_LORA = A["rwkv_w1_2"].shape[2], A["rwkv_a1_2"].shape[2], A["rwkv_g1_2"].shape[2]
    G_REST = G_LORA - P
    CH, NCH = 64, T // 64
    tm = ExitStack()
    rkv = sbs(tm, "rkv", [P, 3 * KD, T])
    wa_hid = sbs(tm, "wa_hid", [P, T])
    g_hid = sbs(tm, "g_hid", [P, T])
    g_hid2 = sbs(tm, "g_hid2", [G_REST, T])
    cmask = sbs(tm, "cmask", [P, T])
    bones = sbs(tm, "bones", [P, P])
    eye2 = sbs(tm, "eye2", [P, CH])
    m_strict = sbs(tm, "m_strict", [P, P])
    m_incl = sbs(tm, "m_incl", [P, P])
    m_level = sbs(tm, "m_level", [P, 6, P])
    shift_mem = ExitStack()
    hb = sbs(shift_mem, "hb", [P, KD, T + 1])
    xx = sbs(shift_mem, "xx", [P, KD, T])
    xs_hi = sbs(shift_mem, "xs_hi", [P, KD, T], F32R)
    xs_lo = sbs(shift_mem, "xs_lo", [P, KD, T], F32R)
    shift_mem.close()
    N_LOW = W_LORA + A_LORA + G_LORA
    assert KD * N_LOW <= KD * T
    loras = rkv[:, 2 * KD:3 * KD, :].rearrange("p k t -> p (k t)")[:, 0:KD * N_LOW].rearrange("p (k n) -> p k n", n=N_LOW)
    w1, a1, g1 = (loras[:, :, s:s + n] for s, n in (
        (0, W_LORA), (W_LORA, A_LORA), (W_LORA + A_LORA, G_LORA)))
    assert W_LORA == A_LORA == HD

    loras_landed, h2_ready, xx_ready = sem("loras_landed"), sem("h2_ready"), sem("xx_ready")
    mixed, lora_used, hid_ready = sem("mixed"), sem("lora_used"), sem("hid_ready")
    xs_mixed, xs_hi_ready, xs_ready, rkv_ready = (sem(n) for n in ("xs_mixed", "xs_hi_ready", "xs_ready", "rkv_ready"))
    norm_tm = Norm(x_tile, KD, normed, slots=[xx[:, k, :] for k in range(KD)])
    xs_free = sem("xs_free")
    LORA_MIX = (3, 4, 5)
    at_rkv0 = ffn0.end
    w_rkv = A["rwkv_w_rkv_2"].rearrange("a c k n -> (a c k) n")

    def at_rkv(p, o):
        return at_rkv0.plus(8 * p + o) if isinstance(p, int) else At(at_rkv0.c + o, at_rkv0.u + o, KD, p)

    def over_projections(eng, body):
        body(0)
        with eng.Fori(1, 3) as p:
            body(p)

    def sp_time_mix(sp):
        def body(p, outs=range(KD)):
            for o in outs:
                at = at_rkv(p, o)
                if isinstance(p, int):
                    src = w_rkv[p * D:(p + 1) * D, o * P:(o + 1) * P].rearrange("(k p) n -> p k n", p=P)
                else:
                    src = w_rkv[bass.ds(p * D, D), o * P:(o + 1) * P].rearrange("(k p) n -> p k n", p=P)
                load(sp, at, [(raw[:, at.raw_slot, 0:KD * P].rearrange("p (k n) -> p k n", n=P), src)],
                     (lo_ready, at.plus(-RAW).count))

        body(0, range(RAW))
        sp.wait_ge(f_ready.sem, ffn0.c0[f_ready] + KF)
        sp.wait_ge(unit_done, ffn0.end.u)
        for src, dst in ((A["rwkv_w1_2"], w1), (A["rwkv_a1_2"], a1), (A["rwkv_g1_2"], g1)):
            sp.dma_start(dst, src.rearrange("a (k p) n -> p (a k) n", p=P)).then_inc(loras_landed, 16)
        body(0, range(RAW, KD))
        with sp.Fori(1, 3) as p:
            body(p)

    def dve_time_mix(dve):
        dve.memset(hb[:, :, 0:1], 0.0).then_inc(h2_ready, 1)
        norm_tm.dve_rstd(dve)

        def mix(p, k):
            if not isinstance(p, int) or k >= 2:
                dve.wait_ge(xs_ready, p * KD + (k - 1))
            dve.scalar_tensor_tensor(sq[:, k % 2, :], xx[:, k, :], col_at(vecs, p * KD + (col["mix"] + k)),
                                     hb[:, k, 1:T + 1], ALU.mult, ALU.add).then_inc(xs_mixed, 1)
            if k:
                lower(p, k - 1)

        def lower(p, k):
            dve.wait_ge(xs_hi_ready, p * KD + (k + 1))
            dve.wait_ge(xs_mixed, p * KD + (k + 1))
            dve.tensor_tensor(xs_lo[:, k, :], sq[:, k % 2, :], xs_hi[:, k, :].bitcast(F32), ALU.subtract)\
               .then_inc(xs_ready, 1)

        for k in range(KD):
            dve.scalar_tensor_tensor(hb[:, k, 1:T + 1], x[:, k, :], v("gains", k), rstd[:, :], ALU.mult, ALU.mult)\
               .then_inc(h2_ready, 1)
            dve.wait_ge(h2_ready, k + 2)
            dve.tensor_tensor(xx[:, k, :], hb[:, k, 0:T], hb[:, k, 1:T + 1], ALU.subtract).then_inc(xx_ready, 1)
            dve.wait_ge(xx_ready, k + 1)
            for n, m in enumerate(LORA_MIX):
                s = 3 * k + n
                wait(dve, lora_used, s - 2)
                dve.scalar_tensor_tensor(tmp[:, n, :], xx[:, k, :], v("mix", m * KD + k), hb[:, k, 1:T + 1],
                                         ALU.mult, ALU.add).then_inc(mixed, 1)
            mix(0, k)
        lower(0, KD - 1)

        def body(p):
            if not isinstance(p, int):
                for k in range(KD):
                    if k < KD - 1:
                        dve.wait_ge(xs_free, p * (KD - 1) + (k + 2 - KD))
                    else:
                        dve.wait_ge(unit_done, at_rkv(p, 0).plus(-1).count)
                    mix(p, k)
                lower(p, KD - 1)
            for o in range(KD):
                split_lo(dve, at_rkv(p, o).plus(2))

        over_projections(dve, body)

    def act_time_mix(act):
        norm_tm.act_squares(act)
        norm_tm.act_root(act)

        def upper(p, k):
            act.wait_ge(xs_mixed, p * KD + (k + 1))
            if not isinstance(p, int):
                if k < KD - 1:
                    act.wait_ge(xs_free, p * (KD - 1) + (k + 2 - KD))
                else:
                    act.wait_ge(unit_done, at_rkv(p, 0).plus(-1).count)
            act.activation(xs_hi[:, k, :], sq[:, k % 2, :], ACT.Copy).then_inc(xs_hi_ready, 1)

        for k in range(KD):
            upper(0, k)
        act.wait_ge(lora_used, 3 * KD)
        act.activation(wa_hid[0:HD, :], bank[0][0:HD, :], ACT.Tanh).then_inc(hid_ready, 1)
        act.activation(wa_hid[HD:P, :], bank[1][HD:P, :], ACT.Copy).then_inc(hid_ready, 1)
        act.activation(g_hid[:, :], bank[2][:, :], ACT.Sigmoid).then_inc(hid_ready, 1)
        act.activation(g_hid2[:, :], bank[3][0:G_REST, :], ACT.Sigmoid).then_inc(hid_ready, 1)

        def body(p):
            if not isinstance(p, int):
                for k in range(KD):
                    upper(p, k)
            for o in range(KD):
                split_hi(act, at_rkv(p, o).plus(2))
                act.wait_ge(unit_done, at_rkv(p, o).count)
                act.activation(tile_at(rkv, p * KD + o), bank[4 + o % 2][:, :], ACT.Copy).then_inc(rkv_ready, 1)

        over_projections(act, body)

    def pe_time_mix(pe):
        norm_tm.pe_sums(pe)
        pe.wait_ge(loras_landed, 48)
        for k in range(KD):
            for n, parts in enumerate((((bank[0][0:W_LORA, :], w1),), ((bank[1][HD:P, :], a1),),
                                       ((bank[2][:, :], g1[:, :, 0:P]), (bank[3][0:G_REST, :], g1[:, :, P:G_LORA])))):
                pe.wait_ge(mixed, 3 * k + n + 1)
                for dst, w in parts:
                    mm = pe.matmul(dst, w[:, k, :], tmp[:, n, :], start=k == 0, stop=k == KD - 1)
                mm.then_inc(lora_used, 1)

        def body(p):
            for o in range(KD):
                at = at_rkv(p, o)
                if not isinstance(p, int) or o >= 2:
                    pe.wait_ge(rkv_ready, p * KD + (o - 1))
                unit_products(pe, at, KD, bank[4 + o % 2][:, :], lambda k: xs_hi[:, k, :], lambda k: xs_lo[:, k, :],
                              True, True, (lambda k: pe.wait_ge(xs_ready, p * KD + (k + 1))) if o == 0 else None,
                              k_done=xs_free if o == KD - 1 else None)

        over_projections(pe, body)

    GN_EPS = 64e-5
    DECAY = -float(np.exp(-0.5))
    LEVELS = (2, 4, 8, 16, 32)
    bm = ExitStack()
    lw = sbs(bm, "lw", [P, P])
    lg = sbs(bm, "lg", [P, 2, P])
    L_t = sbs(bm, "L_t", [P, T])
    E_t = sbs(bm, "E_t", [P, T])
    y_sb = sbs(bm, "y_sb", [P, T])
    ends = sbs(bm, "ends", [P, NCH])
    nk_sb = sbs(bm, "nk_sb", [P, 2 * NT])
    ng_sb = sbs(bm, "ng_sb", [P, 2 * NT])
    AR = sbs(bm, "AR", [P, NT, 2, P])
    B_t = sbs(bm, "B_t", [P, T])
    K_t = sbs(bm, "K_t", [P, T])
    AU = sbs(bm, "AU", [P, NT, 2, P])
    B_k = sbs(bm, "B_k", [P, NT, P])
    K_k = sbs(bm, "K_k", [P, NT, P])
    V_k = sbs(bm, "V_k", [P, NT, P])
    MT = sbs(bm, "MT", [P, 2, NT, P])
    MTb = sbs(bm, "MTb", [P, 2, NT, P])
    XT = sbs(bm, "XT", [P, 2, NT, P])
    X = sbs(bm, "X", [P, 2, NT, P])
    Z = sbs(bm, "Z", [P, 2, NT, P])
    RB = sbs(bm, "RB", [P, 2, NT, P])
    AK = sbs(bm, "AK", [P, 2, NT, P])
    RK = sbs(bm, "RK", [P, 2, NT, P])
    XAU = Z
    GT = sbs(bm, "GT", [P, NCH, 2, CH])
    HP = sbs(bm, "HP", [P, NCH, CH])
    RH = sbs(bm, "RH", [P, T])
    S = sbs(bm, "S", [P, NCH, CH])
    bm.close()

    class Round:

        def __init__(self, i, off=0):
            self.i, self.off = i, off

        def plus(self, n):
            return self.i + (self.off + n)

    class Steps:

        def __init__(self, sem_name, names):
            self.sem, self.names, self.seen = sem(sem_name), names.split(), 0

        def done(self, ins, name):
            ins.then_inc(self.sem, 1)
            assert name == self.names[self.seen % len(self.names)], (name, self.names[self.seen % len(self.names)])
            self.seen += 1

        def wait(self, eng, j, name, before=0):
            n = (j.off - before) * len(self.names) + self.names.index(name) + 1
            wait(eng, self.sem, j.i * len(self.names) + n)

    masks_ready, lw_landed, lg_landed = sem("masks_ready"), sem("lw_landed"), sem("lg_landed")
    turned = "tA tB tK tV"
    PEa = Steps("pe_pre", f"lora kk_sum kk_bc bonus_sum {turned} " + " ".join(f"m{n}" for n in range(6)) + " x0 x1 m6 m7")
    PEb = Steps("pe_core", " ".join(f"z{b}_0 z{b}_1 xt{b}_0 xt{b}_1" + ("" if b == 32 else f" x{b}_0 x{b}_1")
                                    for b in LEVELS)
                + " u0 u1 xau0 xau1 gh rh " + " ".join(f"s{c}" for c in range(1, NCH - 1)) + " y")
    PEc = Steps("pe_post", "mean var bc g")
    ACTa = Steps("act_pre", "sg a kk2 eE eN eL root ktB ktV x0 x1")
    ACTb = Steps("act_core", " ".join(f"z{b}_0 z{b}_1" + ("" if b == 32 else f" x{b}_0 x{b}_1") for b in LEVELS)
                 + " u0 u1 xau0 xau1 y")
    ACTc = Steps("act_post", "d2 root")
    DVEa = Steps("dve_pre", "kk scan E u kp nk rn spread kkn t2 bon AT BT KT bonus RT tA tK "
                 + " ".join(f"e{n}a e{n}b" for n in range(4)) + " l0 l1 xt0 xt1 "
                + " ".join(f"e{n}a e{n}b" for n in range(4, 8)))
    DVEb = Steps("dve_core", " ".join(f"xt{b}_0 xt{b}_1" for b in LEVELS)
                 + " gt00 gt01 gt10 gt11 hp0 hp1 rh0 rh1 S1 " + " ".join(f"S{c}" for c in range(2, NCH)))
    DVEc = Steps("dve_post", "d gvar grstd spread yn yb y")
    POOLa, POOLb = Steps("pool_pre", "v"), Steps("pool_core", " ".join(f"m{b}_0 m{b}_1" for b in LEVELS))
    sg, a_, kk = tmp[:, 0, :], tmp[:, 1, :], tmp[:, 2, :]
    kk2, eN = sq[:, 0, :], sq[:, 1, :]
    d2, kp, v_c = var[:, :], rstd[:, :], sq_sum
    w2, a2, g2 = (A[n].rearrange("a k n -> (a k) n") for n in ("rwkv_w2_2", "rwkv_a2_2", "rwkv_g2_2"))

    def pool_masks(pool):
        pool.wait_ge(unit_done, ffn0.end.u)
        n = [0]

        def step(ins):
            ins.then_inc(masks_ready, 1)
            n[0] += 1
            pool.wait_ge(masks_ready, n[0])

        step(pool.memset(cmask[:, :], 1.0))
        step(pool.memset(cmask[:, :].rearrange("p (c t) -> p c t", t=CH)[:, :, 0:1], 0.0))
        step(pool.memset(bones[:, :], 0.0))
        step(pool.memset(bones[0:HD, 0:HD], 1.0))
        step(pool.memset(bones[HD:P, HD:P], 1.0))
        step(pool.tensor_copy(eye2[0:HD, :], ident[0:HD, 0:HD]))
        step(pool.tensor_copy(eye2[HD:P, :], ident[HD:P, HD:P]))
        step(pool.affine_select(out=m_strict[:, :], in_=bones[:, :], compare_op=ALU.is_gt, fill=0.0, base=0,
                                pattern=[[1, P]], channel_multiplier=-1))
        step(pool.affine_select(out=m_incl[:, :], in_=bones[:, :], compare_op=ALU.is_ge, fill=0.0, base=0,
                                pattern=[[1, P]], channel_multiplier=-1))
        for n_, b in enumerate((1,) + LEVELS):
            m = m_level[:, n_, :].rearrange("p (g h t) -> p g h t", h=2, t=b)
            step(pool.memset(m_level[:, n_, :], 0.0))
            step(pool.memset(m[:, :, 1, :], 1.0))
            step(pool.affine_select(out=m[:, :, 1, :], in_=m[:, :, 1, :], compare_op=ALU.is_ge, fill=0.0, base=0,
                                    pattern=[[-2 * b, P // (2 * b)], [0, b]], channel_multiplier=1))
            step(pool.affine_select(out=m[:, :, 1, :], in_=m[:, :, 1, :], compare_op=ALU.is_ge, fill=0.0, base=b - 1,
                                    pattern=[[2 * b, P // (2 * b)], [0, b]], channel_multiplier=-1))

    MASKS = 9 + 4 * 6

    REGION_FREE = lambda eng: eng.wait_ge(unit_done, at_rkv(2, KD - 1).count)

    def over_tiles(eng, body):
        body(Round(0), False, True)
        with eng.Fori(1, KD - 1) as j:
            body(Round(j), True, True)
        body(Round(KD - 1), True, False)

    def r_k_v(j):
        return tile_at(rkv, j.plus(0)), tile_at(rkv, j.plus(KD)), tile_at(rkv, j.plus(2 * KD))

    def nxt(j):
        return Round(j.i, j.off + 1)

    def prv(j):
        return Round(j.i, j.off - 1)

    by_tile = lambda t_: t_.rearrange("p (t c) -> p t c", t=NT)
    bank4 = lambda b: by_tile(bank[b][:, :])
    hr = [slice(0, HD), slice(HD, P)]
    M_BANK = (2, 3, 4, 5, 0, 1, 2, 3)

    def sp_blocks(sp):
        def low(j):
            PEa.wait(sp, j, "lora", before=1)
            for w, dst in ((w2, lw[0:HD, :]), (a2, lw[HD:P, :])):
                sp.dma_start(dst, cols_at(w, j.plus(0) * P, P)).then_inc(lw_landed, 16)

        def body(j, before, after):
            if after:
                low(nxt(j))
            PEc.wait(sp, j, "g", before=1)
            for r0, r1, n in ((0, P, 0), (P, G_LORA, 1)):
                sp.dma_start(lg[0:r1 - r0, n, :], cols_at(g2[r0:r1, :], j.plus(0) * P, P)).then_inc(lg_landed, 16)

        REGION_FREE(sp)
        low(Round(0))
        over_tiles(sp, body)

    def pool_blocks(pool):
        REGION_FREE(pool)
        pool.wait_ge(rkv_ready, 3 * KD)

        def pre(j):
            PEa.wait(pool, j, "tV", before=1)
            POOLa.done(pool.tensor_copy(v_c[:, :], r_k_v(j)[2]), "v")

        def body(j, before, after):
            if after:
                pre(nxt(j))
            for n, b in enumerate(LEVELS):
                for e in range(2):
                    if n == 0:
                        DVEa.wait(pool, j, "e3b")
                        PEb.wait(pool, j, f"z32_{e}", before=1)
                    else:
                        PEb.wait(pool, j, f"z{LEVELS[n - 1]}_{e}")
                    POOLb.done(pool.tensor_tensor(MTb[:, e, :, :], MT[:, e, :, :],
                                                  m_level[:, n + 1:n + 2, :].to_broadcast([P, NT, P]), ALU.mult),
                               f"m{b}_{e}")

        pre(Round(0))
        over_tiles(pool, body)

    def act_sigmoids(act, j):
        PEa.wait(act, j, "lora")
        for out, b, name, c in ((sg, 6, "sg", "w0"), (a_, 7, "a", "a0")):
            DVEa.wait(act, j, "t2" if name == "sg" else "t2", before=1)
            ACTa.done(act.activation(out, bank[b][:, :], ACT.Sigmoid, bias=col_at(vecs, j.plus(col[c]))), name)
        DVEa.wait(act, j, "kk")
        PEa.wait(act, j, "bonus_sum", before=1)
        ACTa.done(act.activation(kk2, kk, ACT.Square), "kk2")

    def act_exps(act, j):
        DVEa.wait(act, j, "E")
        DVEa.wait(act, j, "KT", before=1)
        for out, src, scale, name in ((E_t[:, :], E_t[:, :], DECAY, "eE"), (eN, L_t[:, :], -DECAY, "eN"),
                                      (L_t[:, :], L_t[:, :], DECAY, "eL")):
            if name == "eL":
                ACTa.wait(act, j, "eN")
            ACTa.done(act.activation(out, src, ACT.Exp, scale=scale), name)

    def act_pre_root(act, j):
        DVEa.wait(act, j, "nk")
        ACTa.done(act.activation(nk_sb[:, :], nk_sb[:, :], ACT.Sqrt), "root")

    def act_turned(act, j):
        PEa.wait(act, j, "tB")
        ACTa.done(act.activation(B_k[:, :, :], bank4(5), ACT.Copy), "ktB")
        PEa.wait(act, j, "tV")
        ACTa.done(act.activation(V_k[:, :, :], bank4(1), ACT.Copy), "ktV")

    def act_x0(act, j):
        for e in range(2):
            PEa.wait(act, j, f"x{e}")
            ACTa.done(act.activation(X[:, e, :, :], bank4(4 + e), ACT.Copy), f"x{e}")

    def act_z(act, j, b):
        for e in range(2):
            PEb.wait(act, j, f"z{b}_{e}")
            ACTb.done(act.activation(Z[:, e, :, :], bank4(e), ACT.Copy), f"z{b}_{e}")

    def act_x(act, j, b):
        for e in range(2):
            PEb.wait(act, j, f"x{b}_{e}")
            ACTb.done(act.activation(X[:, e, :, :], bank4(4 + e), ACT.Copy), f"x{b}_{e}")

    def act_post_square(act, j):
        DVEc.wait(act, j, "d")
        ACTc.done(act.activation(d2, y_sb[:, :], ACT.Square), "d2")

    def act_post_root(act, j):
        DVEc.wait(act, j, "gvar")
        ACTc.done(act.activation(ng_sb[:, :], ng_sb[:, :], ACT.Sqrt), "root")

    def act_blocks(act):
        def body(j, before, after):
            act_z(act, j, 2)
            if after:
                act_sigmoids(act, nxt(j))
            act_x(act, j, 2)
            act_z(act, j, 4)
            if after:
                act_exps(act, nxt(j))
            act_x(act, j, 4)
            if before:
                act_post_square(act, prv(j))
            act_z(act, j, 8)
            if after:
                act_pre_root(act, nxt(j))
            act_x(act, j, 8)
            if before:
                act_post_root(act, prv(j))
            act_z(act, j, 16)
            act_x(act, j, 16)
            act_z(act, j, 32)
            for e in range(2):
                PEb.wait(act, j, f"u{e}")
                ACTb.done(act.activation(AU[:, :, e, CH:P], by_tile(bank[4 + e][:, 0:NT * CH]), ACT.Copy), f"u{e}")
            for e in range(2):
                PEb.wait(act, j, f"xau{e}")
                ACTb.done(act.activation(XAU[:, e, :, :], bank4(e), ACT.Copy), f"xau{e}")
            if after:
                act_turned(act, nxt(j))
            PEb.wait(act, j, "y")
            DVEc.wait(act, j, "y", before=1)
            ACTb.done(act.activation(y_sb[:, :], bank[6][:, :], ACT.Copy), "y")
            if after:
                act_x0(act, nxt(j))

        first_ = Round(0)
        act_sigmoids(act, first_)
        act_exps(act, first_)
        act_pre_root(act, first_)
        act_turned(act, first_)
        act_x0(act, first_)
        over_tiles(act, body)
        act_post_square(act, Round(KD - 1))
        act_post_root(act, Round(KD - 1))

    by_head = lambda t_: t_.rearrange("p (n c) -> p n c", c=HD)
    over_head = lambda t_: t_[:, :].rearrange("p (n o) -> p n o", o=1).to_broadcast([P, 2 * NT, HD])

    def dve_kk(dve, j):
        DVEa.done(dve.tensor_scalar(kk, r_k_v(j)[1], col_at(vecs, j.plus(col["k_k"])), None, ALU.mult), "kk")

    def dve_decay(dve, j):
        ACTa.wait(dve, j, "sg")
        DVEa.done(dve.tensor_tensor_scan(L_t[:, :], cmask[:, :], sg, 0.0, ALU.mult, ALU.add), "scan")
        DVEa.wait(dve, j, "scan")
        DVEa.done(dve.tensor_tensor(E_t[:, :], L_t[:, :], sg, ALU.subtract), "E")
        ACTa.wait(dve, j, "a")
        DVEa.done(dve.tensor_scalar(kp, a_, 1.0, col_at(vecs, j.plus(col["k_a"])), ALU.subtract, ALU.mult), "u")
        DVEa.wait(dve, j, "u")
        DVEa.done(dve.scalar_tensor_tensor(kp, kp, 1.0, r_k_v(j)[1], ALU.add, ALU.mult), "kp")

    def dve_kk_square(dve, j):
        PEa.wait(dve, j, "kk_sum")
        DVEa.done(dve.tensor_scalar(nk_sb[:, :], bank[7][:, 0:2 * NT], 1e-24, None, ALU.max), "nk")

    def dve_kk_rstd(dve, j):
        ACTa.wait(dve, j, "root")
        DVEa.done(dve.reciprocal(nk_sb[:, :], nk_sb[:, :]), "rn")
        DVEa.wait(dve, j, "rn")
        DVEa.done(dve.tensor_copy(by_head(sg), over_head(nk_sb)), "spread")

    def dve_normed(dve, j):
        PEa.wait(dve, j, "kk_bc")
        DVEa.done(dve.tensor_tensor(kk, kk, bank[7][:, :], ALU.mult), "kkn")
        DVEa.wait(dve, j, "kkn")
        DVEa.done(dve.tensor_tensor(sg, kk, a_, ALU.mult), "t2")
        PEa.wait(dve, j, "kk_sum")
        DVEa.done(dve.scalar_tensor_tensor(kk2, r_k_v(j)[0], col_at(vecs, j.plus(col["r_k"])), kp,
                                           ALU.mult, ALU.mult), "bon")

    def dve_scaled(dve, j):
        ACTa.wait(dve, j, "eL")
        DVEa.done(dve.scalar_tensor_tensor(AR[:, :, 0, :], by_tile(kk), -1.0, by_tile(E_t[:, :]),
                                           ALU.mult, ALU.mult), "AT")
        DVEa.wait(dve, j, "t2")
        DVEa.done(dve.tensor_tensor(B_t[:, :], sg, eN, ALU.mult), "BT")
        DVEa.done(dve.tensor_tensor(K_t[:, :], kp, eN, ALU.mult), "KT")

    def dve_bonus(dve, j):
        v = r_k_v(j)[2]
        PEa.wait(dve, j, "bonus_sum")
        POOLa.wait(dve, j, "v")
        DVEa.done(dve.tensor_tensor(v, bank[7][:, :], v, ALU.mult), "bonus")

    def dve_r(dve, j):
        DVEa.done(dve.tensor_tensor(AR[:, :, 1, :], by_tile(r_k_v(j)[0]), by_tile(L_t[:, :]), ALU.mult), "RT")

    def dve_turned(dve, j, name):
        PEa.wait(dve, j, name)
        if name == "tA":
            ins = dve.tensor_copy(AU[:, :, :, 0:CH], bank[4][:, :].rearrange("p (t e c) -> p t e c", t=NT, e=2))
        else:
            ins = dve.tensor_copy(K_k[:, :, :], bank4(0))
        DVEa.done(ins, name)

    def dve_masked(dve, j, ns):
        for n in ns:
            of_b, e, pair = n < 4, n // 2 % 2, n % 2
            PEa.wait(dve, j, f"m{n}")
            two = bank[M_BANK[n]][:, :].rearrange("p (t h c) -> p t h c", t=2, h=2)
            ts = slice(2 * pair, 2 * pair + 2)
            for h, dst, m, name in ((0, MT if of_b else AK, m_strict, "a"), (1, RB if of_b else RK, m_incl, "b")):
                DVEa.done(dve.tensor_tensor(dst[:, e, ts, :], two[:, :, h, :],
                                            m[:, :].rearrange("p (o c) -> p o c", o=1).to_broadcast([P, 2, P]),
                                            ALU.mult), f"e{n}{name}")

    def dve_level1(dve, j):
        DVEa.wait(dve, j, "e3b")
        for e in range(2):
            DVEa.done(dve.tensor_tensor(XT[:, e, :, :], MT[:, e, :, :], m_level[:, 0:1, :].to_broadcast([P, NT, P]),
                                        ALU.mult), f"l{e}")
        for e in range(2):
            DVEa.wait(dve, j, f"l{e}")
            DVEa.done(dve.tensor_tensor(XT[:, e, :, :], XT[:, e, :, :],
                                        ident[:, :].rearrange("p (o c) -> p o c", o=1).to_broadcast([P, NT, P]),
                                        ALU.add), f"xt{e}")

    def dve_xt(dve, j, b):
        for e in range(2):
            PEb.wait(dve, j, f"xt{b}_{e}")
            DVEb.done(dve.tensor_tensor(XT[:, e, :, :], bank4(2 + e), XT[:, e, :, :], ALU.add), f"xt{b}_{e}")

    def dve_post_centre(dve, j):
        PEc.wait(dve, j, "mean")
        DVEc.done(dve.scalar_tensor_tensor(y_sb[:, :], bank[6][:, :], -1.0 / HD, y_sb[:, :], ALU.mult, ALU.add), "d")

    def dve_post_var(dve, j):
        PEc.wait(dve, j, "var")
        DVEc.done(dve.tensor_scalar(ng_sb[:, :], bank[6][:, 0:2 * NT], 1.0 / HD, GN_EPS, ALU.mult, ALU.add), "gvar")

    def dve_post_rstd(dve, j):
        ACTc.wait(dve, j, "root")
        DVEc.done(dve.reciprocal(ng_sb[:, :], ng_sb[:, :]), "grstd")
        DVEc.wait(dve, j, "grstd")
        DVEc.done(dve.tensor_copy(by_head(d2), over_head(ng_sb)), "spread")

    def dve_post_norm(dve, j):
        PEc.wait(dve, j, "bc")
        vc = lambda name: col_at(vecs, j.plus(col[name]))
        DVEc.done(dve.scalar_tensor_tensor(y_sb[:, :], y_sb[:, :], vc("gn_w"), bank[6][:, :], ALU.mult, ALU.mult), "yn")
        DVEc.wait(dve, j, "yn")
        DVEc.done(dve.scalar_tensor_tensor(y_sb[:, :], y_sb[:, :], vc("gn_b"), r_k_v(j)[2], ALU.add, ALU.add), "yb")

    def dve_post_gate(dve, j):
        PEc.wait(dve, j, "g")
        DVEc.wait(dve, j, "yb")
        DVEc.done(dve.tensor_tensor(r_k_v(j)[0], y_sb[:, :], bank[6][:, :], ALU.mult), "y")

    def dve_ends(dve, j):
        ACTa.wait(dve, j, "eL")
        DVEb.wait(dve, j, f"S{NCH - 1}", before=1)
        dve.tensor_copy(ends[:, :], L_t[:, :].rearrange("q (c t) -> q c t", c=NCH)[:, :, CH - 1])\
           .then_inc(ends_ready, 1)

    def dve_blocks(dve):
        def body(j, before, after):
            if after:
                dve_kk(dve, nxt(j))
            dve_xt(dve, j, 2)
            if after:
                dve_decay(dve, nxt(j))
            if before:
                dve_post_centre(dve, prv(j))
            dve_xt(dve, j, 4)
            if after:
                dve_kk_square(dve, nxt(j))
            dve_xt(dve, j, 8)
            if before:
                dve_post_var(dve, prv(j))
            if after:
                dve_kk_rstd(dve, nxt(j))
            if before:
                dve_post_rstd(dve, prv(j))
            dve_xt(dve, j, 16)
            if after:
                dve_normed(dve, nxt(j))
            if before:
                dve_post_norm(dve, prv(j))
            dve_xt(dve, j, 32)
            if after:
                dve_scaled(dve, nxt(j))
            if before:
                dve_post_gate(dve, prv(j))
            if after:
                dve_bonus(dve, nxt(j))
            half = lambda t_, p_: t_[:, :, :].rearrange("q (t p) c -> q t p c", p=2)[:, :, p_, :]
            PEb.wait(dve, j, "gh")
            for p_ in range(2):
                for e in range(2):
                    q = hr[e]
                    eye = eye2[q, :].rearrange("p (o c) -> p o c", o=1).to_broadcast([HD, NT, CH])
                    DVEb.done(dve.tensor_tensor(GT[q, :, e, :].rearrange("q (t p) c -> q t p c", p=2)[:, :, p_, :],
                                                by_tile(bank[p_][q, 0:NT * CH]), eye, ALU.add), f"gt{p_}{e}")
            dve.wait_ge(ends_ready, j.plus(1))
            for p_ in range(2):
                e_ = ends[:, :].rearrange("q (t p o) -> q t p o", p=2, o=1)[:, :, p_, :]
                DVEb.done(dve.tensor_tensor(half(HP, p_), by_tile(bank[p_][:, NT * CH:]),
                                            e_.to_broadcast([P, NT, CH]), ALU.mult), f"hp{p_}")
            PEb.wait(dve, j, "rh")
            for p_ in range(2):
                cols = slice(p_ * CH, (p_ + 1) * CH)
                DVEb.done(dve.tensor_tensor(by_tile(RH[:, :])[:, :, cols], by_tile(bank[2 + p_][:, 0:NT * CH]),
                                            AR[:, :, 1, cols], ALU.add), f"rh{p_}")
            DVEb.wait(dve, j, "hp1")
            DVEb.done(dve.tensor_copy(S[:, 1, :], HP[:, 0, :]), "S1")
            DVEb.wait(dve, j, "rh1")
            if after:
                dve_r(dve, nxt(j))
            for c in range(1, NCH - 1):
                PEb.wait(dve, j, f"s{c}")
                DVEb.done(dve.scalar_tensor_tensor(S[:, c + 1, :], bank[7][:, 0:CH], ends[:, c:c + 1], HP[:, c, :],
                                                   ALU.mult, ALU.add), f"S{c + 1}")
                if after:
                    if c == 1:
                        dve_turned(dve, nxt(j), "tA")
                    elif c == 2:
                        dve_turned(dve, nxt(j), "tK")
                    elif c < NCH - 2:
                        dve_masked(dve, nxt(j), {3: (0,), 4: (1,), 5: (2, 3)}[c])
            if after:
                dve_ends(dve, nxt(j))
                dve_level1(dve, nxt(j))
                dve_masked(dve, nxt(j), (4, 5, 6, 7))

        dve.wait_ge(masks_ready, MASKS)
        REGION_FREE(dve)
        dve.wait_ge(rkv_ready, 3 * KD)
        dve.memset(GT[:, :, :, :], 0.0).then_inc(gt_zero, 1)
        dve.wait_ge(gt_zero, 1)
        j = Round(0)
        dve_kk(dve, j)
        dve_decay(dve, j)
        dve_kk_square(dve, j)
        dve_kk_rstd(dve, j)
        dve_normed(dve, j)
        dve_scaled(dve, j)
        dve_bonus(dve, j)
        dve_r(dve, j)
        dve_turned(dve, j, "tA")
        dve_turned(dve, j, "tK")
        dve_ends(dve, j)
        dve_masked(dve, j, range(4))
        dve_level1(dve, j)
        dve_masked(dve, j, range(4, 8))
        over_tiles(dve, body)
        j = Round(KD - 1)
        dve_post_centre(dve, j)
        dve_post_var(dve, j)
        dve_post_rstd(dve, j)
        dve_post_norm(dve, j)
        dve_post_gate(dve, j)

    ends_ready, gt_zero = sem("ends_ready"), sem("gt_zero")

    def pe_low(pe, j):
        ACTb.wait(pe, j, "y", before=2)
        DVEb.wait(pe, j, f"S{NCH - 1}", before=2)
        wait(pe, lw_landed, j.plus(1) * 32)
        pe.matmul(bank[6][:, :], lw[0:HD, :], wa_hid[0:HD, :], start=True, stop=True)
        PEa.done(pe.matmul(bank[7][:, :], lw[HD:P, :], wa_hid[HD:P, :], start=True, stop=True), "lora")

    def pe_head_sums(pe, b, src):
        for t in range(NT):
            mm = pe.matmul(bank[b][:, 2 * t:2 * t + 2], src[:, t * P:(t + 1) * P], bones[:, 0:P:HD], start=True, stop=True)
        return mm

    def pe_head_spread(pe, b, src):
        for t in range(NT):
            mm = pe.matmul(bank[b][:, t * P:(t + 1) * P], src[:, t * P:(t + 1) * P], ident[:, :],
                           start=True, stop=True)
        return mm

    def pe_kk_sum(pe, j):
        ACTa.wait(pe, j, "kk2")
        PEa.done(pe_head_sums(pe, 7, kk2), "kk_sum")

    def pe_kk_spread(pe, j):
        DVEa.wait(pe, j, "spread")
        PEa.done(pe_head_spread(pe, 7, sg), "kk_bc")

    def pe_bonus(pe, j):
        DVEa.wait(pe, j, "bon")
        PEa.done(pe.matmul(bank[7][:, :], bones[:, :], kk2, start=True, stop=True), "bonus_sum")

    def pe_turn(pe, b, src):
        for t in range(NT):
            tr = pe.transpose(bank[b][:, t * P:(t + 1) * P], src(t), ident[:, :])
        return tr

    def pe_turn_ab(pe, j):
        DVEa.wait(pe, j, "KT")
        ACTb.wait(pe, j, "u1", before=1)
        PEa.done(pe_turn(pe, 4, lambda t: AR[:, t, 0, :]), "tA")
        PEa.done(pe_turn(pe, 5, lambda t: B_t[:, t * P:(t + 1) * P]), "tB")

    def pe_turn_kv(pe, j):
        DVEb.wait(pe, j, "hp1", before=1)
        POOLa.wait(pe, j, "v")
        PEa.done(pe_turn(pe, 0, lambda t: K_t[:, t * P:(t + 1) * P]), "tK")
        PEa.done(pe_turn(pe, 1, lambda t: v_c[:, t * P:(t + 1) * P]), "tV")

    def pe_products(pe, j, ns):
        for n in ns:
            of_b, e, pair = n < 4, n // 2 % 2, n % 2
            if n == 0:
                DVEa.wait(pe, j, "RT")
                DVEb.wait(pe, j, "rh1", before=1)
            engine, name = ((None, None), (None, None), (DVEa, "tA"), (ACTa, "ktB"), (DVEa, "tK"), (ACTa, "ktV"),
                            (DVEa, "e0b"), (DVEa, "e1b"))[n]
            if engine is not None:
                engine.wait(pe, j, name)
            for t in range(2 * pair, 2 * pair + 2):
                lhs = (B_t if of_b else K_t)[hr[e], t * P:(t + 1) * P]
                m = pe.matmul(bank[M_BANK[n]][:, (t % 2) * 2 * P:(t % 2 + 1) * 2 * P], lhs,
                              AR[hr[e], t, :, :].rearrange("p h c -> p (h c)"), start=True, stop=True)
            PEa.done(m, f"m{n}")

    def pe_x0(pe, j):
        for e in range(2):
            DVEa.wait(pe, j, f"xt{e}")
            PEa.done(pe_turn(pe, 4 + e, lambda t: XT[:, e, t, :]), f"x{e}")

    def pe_z(pe, j, b):
        for e in range(2):
            POOLb.wait(pe, j, f"m{b}_{e}")
            if b == 2:
                ACTa.wait(pe, j, f"x{e}")
                DVEa.wait(pe, j, f"e{4 + e}b")
            else:
                ACTb.wait(pe, j, f"x{b // 2}_{e}")
            for t in range(NT):
                m = pe.matmul(bank[e][:, t * P:(t + 1) * P], MTb[:, e, t, :], X[:, e, t, :], start=True, stop=True)
            PEb.done(m, f"z{b}_{e}")

    def pe_xt(pe, j, b):
        for e in range(2):
            ACTb.wait(pe, j, f"z{b}_{e}")
            if b == 2:
                DVEa.wait(pe, j, f"e{6 + e}b")
            for t in range(NT):
                m = pe.matmul(bank[2 + e][:, t * P:(t + 1) * P], Z[:, e, t, :], XT[:, e, t, :], start=True, stop=True)
            PEb.done(m, f"xt{b}_{e}")

    def pe_x(pe, j, b):
        for e in range(2):
            DVEb.wait(pe, j, f"xt{b}_{e}")
            PEb.done(pe_turn(pe, 4 + e, lambda t: XT[:, e, t, :]), f"x{b}_{e}")

    def pe_post_mean(pe, j, after):
        ACTb.wait(pe, j, "y")
        if after:
            ACTa.wait(pe, Round(j.i, j.off + 2), "sg")
        PEc.done(pe.matmul(bank[6][:, :], bones[:, :], y_sb[:, :], start=True, stop=True), "mean")

    def pe_post_var(pe, j):
        ACTc.wait(pe, j, "d2")
        PEc.done(pe_head_sums(pe, 6, d2), "var")

    def pe_post_spread(pe, j):
        DVEc.wait(pe, j, "spread")
        PEc.done(pe_head_spread(pe, 6, d2), "bc")

    def pe_post_gate(pe, j):
        wait(pe, lg_landed, j.plus(1) * 32)
        DVEc.wait(pe, j, "yn")
        pe.matmul(bank[6][:, :], lg[:, 0, :], g_hid[:, :], start=True, stop=False)
        PEc.done(pe.matmul(bank[6][:, :], lg[0:G_REST, 1, :], g_hid2[:, :], start=False, stop=True), "g")

    def pe_blocks(pe):
        def body(j, before, after):
            pre, post = nxt(j), prv(j)
            if after:
                pe_low(pe, pre)
            pe_z(pe, j, 2)
            pe_xt(pe, j, 2)
            pe_x(pe, j, 2)
            if before:
                pe_post_mean(pe, post, after)
            pe_z(pe, j, 4)
            pe_xt(pe, j, 4)
            if after:
                pe_kk_sum(pe, pre)
            pe_x(pe, j, 4)
            pe_z(pe, j, 8)
            pe_xt(pe, j, 8)
            if before:
                pe_post_var(pe, post)
            pe_x(pe, j, 8)
            pe_z(pe, j, 16)
            if after:
                pe_kk_spread(pe, pre)
            if before:
                pe_post_spread(pe, post)
            pe_xt(pe, j, 16)
            pe_x(pe, j, 16)
            pe_z(pe, j, 32)
            if before:
                pe_post_gate(pe, post)
            pe_xt(pe, j, 32)
            if after:
                pe_bonus(pe, pre)
            for e in range(2):
                for t in range(NT):
                    m = pe.matmul(bank[4 + e][:, t * CH:(t + 1) * CH], AK[:, e, t, :], V_k[:, t, hr[e]],
                                  start=True, stop=True)
                PEb.done(m, f"u{e}")
            for e in range(2):
                DVEb.wait(pe, j, f"xt32_{e}")
                ACTb.wait(pe, j, f"u{e}")
                for t in range(NT):
                    m = pe.matmul(bank[e][:, t * P:(t + 1) * P], XT[:, e, t, :], AU[:, t, e, :], start=True, stop=True)
                PEb.done(m, f"xau{e}")

            def local(t):
                cs = slice(t * P, (t + 1) * P)
                for e in range(2):
                    pe.matmul(bank[6][hr[e], cs], XAU[:, e, t, CH:P], RB[:, e, t, :], start=t == 0, stop=False,
                              skip_group_check=True)
                    pe.matmul(bank[6][hr[e], cs], V_k[:, t, hr[e]], RK[:, e, t, :], start=False, stop=False,
                              skip_group_check=True)

            if before:
                DVEc.wait(pe, post, "y")
            elif after:
                ACTa.wait(pe, pre, "sg")
            ACTb.wait(pe, j, "xau1")
            local(0)
            for out in ("gh", "rh"):
                for e in range(2):
                    for t in range(NT):
                        for p_ in range(2):
                            q, cs = hr[p_], slice(t * CH, (t + 1) * CH)
                            if out == "gh":
                                xa, xu = XAU[q, e, t, 0:CH], XAU[q, e, t, CH:P]
                                pe.matmul(bank[p_][hr[e], cs], xa, B_k[q, t, hr[e]], start=True, stop=True)
                                hs = slice(NT * CH + t * CH, NT * CH + (t + 1) * CH)
                                pe.matmul(bank[p_][hr[e], hs], B_k[q, t, hr[e]], xu, start=True, stop=False)
                                m = pe.matmul(bank[p_][hr[e], hs], K_k[q, t, hr[e]], V_k[q, t, hr[e]],
                                              start=False, stop=True)
                            else:
                                m = pe.matmul(bank[2 + p_][hr[e], cs], XAU[q, e, t, 0:CH], RB[q, e, t, hr[p_]],
                                              start=True, stop=True)
                PEb.done(m, out)
            for t in range(1, NT):
                local(t)
            if after:
                DVEa.wait(pe, pre, "bonus")
            for c in range(1, NCH):
                DVEb.wait(pe, j, f"S{c}")
                if c == 1:
                    DVEb.wait(pe, j, "rh1")
                if c < NCH - 1:
                    PEb.done(pe.matmul(bank[7][:, 0:CH], GT[:, c, :, :].rearrange("p e c -> p (e c)"), S[:, c, :],
                                       start=True, stop=True), f"s{c}")
                elif after:
                    pe_products(pe, pre, (5,))
                for e in range(2):
                    m = pe.matmul(bank[6][hr[e], c * CH:(c + 1) * CH], S[hr[e], c, :], RH[hr[e], c * CH:(c + 1) * CH],
                                  start=False, stop=c == NCH - 1, skip_group_check=True)
                if c == NCH - 1:
                    PEb.done(m, "y")
                if after:
                    if c == 1:
                        pe_turn_ab(pe, pre)
                    elif c == 2:
                        pe_turn_kv(pe, pre)
                    elif c < NCH - 1:
                        pe_products(pe, pre, {3: (0,), 4: (1,), 5: (2, 3), 6: (4,)}[c])
            if after:
                pe_x0(pe, pre)
                pe_products(pe, pre, (6, 7))

        pe.wait_ge(masks_ready, MASKS)
        pe.wait_ge(hid_ready, 4)
        j = Round(0)
        pe_low(pe, j)
        pe_kk_sum(pe, j)
        pe_kk_spread(pe, j)
        pe_bonus(pe, j)
        pe_turn_ab(pe, j)
        pe_turn_kv(pe, j)
        pe_products(pe, j, range(6))
        pe_x0(pe, j)
        pe_products(pe, j, (6, 7))
        over_tiles(pe, body)
        j = Round(KD - 1)
        pe_post_mean(pe, j, False)
        pe_post_var(pe, j)
        pe_post_spread(pe, j)
        pe_post_gate(pe, j)

    ys_hi_ready, ys_ready = count("ys_hi_ready"), count("ys_ready")

    class Project:

        def __init__(self, mem, at0, w, hi, lo, y_split, gains):
            self.at0, self.w, self.hi, self.lo, self.y_split = at0, w, hi, lo, y_split
            self.end = at0.plus(KD)
            self.o = mem
            self.o0 = o_ready.claim(KD)
            self.norm_o = Norm(lambda k: self.o[:, k, :], KD, lambda eng, k: eng.wait_ge(o_ready.sem, self.o0 + k + 1))
            self.res = Residual(lambda k: self.o[:, k, :], gains)
            self.ready = self.res.ready

        def sp(self, sp, outs=range(KD)):
            for o in outs:
                at = self.at0.plus(o)
                load(sp, at, unit_parts(at, self.w, (0, KD), (o * P, P)), (lo_ready, at.plus(-RAW).count))

        def act(self, act):
            for o in range(KD):
                at = self.at0.plus(o)
                split_hi(act, at.plus(2))
                act.wait_ge(unit_done, at.count)
                act.activation(self.o[:, o, :], bank[o % 2][:, :], ACT.Copy).then_inc(o_ready.sem, 1)
                self.norm_o.act_square(act, o)
            self.norm_o.act_root(act)

        def dve(self, dve):
            for o in range(KD):
                split_lo(dve, self.at0.plus(o + 2))
            self.norm_o.dve_rstd(dve)

        def pe(self, pe):
            for o in range(KD):
                wait(pe, o_ready.sem, self.o0 + o - 1)
                unit_products(pe, self.at0.plus(o), KD, bank[o % 2][:, :], lambda k: self.hi[:, k, :],
                              lambda k: self.lo[:, k, :], True, True,
                              (lambda k: self.y_split(pe, k)) if o == 0 else None)
            self.norm_o.pe_sums(pe)

    gains_of = lambda n: (lambda k: v("gains", n * KD + k))
    o_tm = sbs(tm, "o_tm", [P, KD, T])
    ys_hi = sbs(tm, "ys_hi", [P, KD, T], F32R)
    ys_lo = sbs(tm, "ys_lo", [P, KD, T], F32R)
    y0, yhi0 = ys_ready.claim(KD), ys_hi_ready.claim(KD)
    out_tm = Project(o_tm, at_rkv0.plus(3 * KD), A["rwkv_w_o_2"].rearrange("a k n -> (a k) n"), ys_hi, ys_lo,
                     lambda eng, k: eng.wait_ge(ys_ready.sem, y0 + k + 1), gains_of(1))
    tm.close()

    def act_split_y(act):
        DVEc.wait(act, Round(KD - 1), "y")
        for k in range(KD):
            act.activation(ys_hi[:, k, :], rkv[:, k, :], ACT.Copy).then_inc(ys_hi_ready.sem, 1)

    def dve_split_y(dve):
        DVEc.wait(dve, Round(KD - 1), "y")
        for k in range(KD):
            dve.wait_ge(ys_hi_ready.sem, yhi0 + k + 1)
            dve.tensor_tensor(ys_lo[:, k, :], rkv[:, k, :], ys_hi[:, k, :].bitcast(F32), ALU.subtract)\
               .then_inc(ys_ready.sem, 1)

    wg2, wu2, wd2 = A["ffn_w_gate_2"], A["ffn_w_up_2"], A["ffn_w_down_2"]
    ffn1 = FFN("1", out_tm.end, out_tm.res, gains_of(2), None, wg2[0], wu2[0], wd2[0], False, gains_of(3))

    gu = ExitStack()
    gh_hi = sbs(gu, "gh_hi", [P, KD, T], F32R)
    gh_lo = sbs(gu, "gh_lo", [P, KD, T], F32R)
    o_gu = sbs(gu, "o_gu", [P, KD, T])
    uv = sbs(gu, "uv", [P, 2 * KD, T])
    v_tk = sbs(gu, "v_tk", [P, NT, D])
    ws_in = sbs(gu, "ws_in", [P, KD, P])
    wsT = sbs(gu, "wsT", [P, KD, P])
    bs_row = sbs(gu, "bs_row", [1, KD * P])
    bs = sbs(gu, "bs", [P, KD, P])
    LN_EPS = 1e-5
    gs_landed, wsT_done, wsT_ready, bs_done, bs_ready = (sem(n) for n in (
        "gs_landed", "wsT_done", "wsT_ready", "bs_done", "bs_ready"))
    uv_ready, mean_done, v_centred, v_scaled, vn_ready = (sem(n) for n in (
        "uv_ready", "mean_done", "v_centred", "v_scaled", "vn_ready"))
    vt_done, vt_ready, s_done, s_biased = (sem(n) for n in ("vt_done", "vt_ready", "s_done", "s_biased"))
    us_ready, us_hi, us_split = sem("us_ready"), sem("us_hi"), sem("us_split")
    norm_g = Norm(x_tile, KD, ffn1.ready)
    lead_g = Lead(ffn1.res, gains_of(4), lambda k: gh_hi[:, k, :], lambda k: gh_lo[:, k, :], norm_g)
    uv_scaled = sem("uv_scaled")
    norm_v = Norm(lambda k: uv[:, KD + k, :], KD, lambda eng, k: eng.wait_ge(v_centred, k + 1), eps=LN_EPS,
                  slots=[v_tk[:, k // 2, k % 2 * T:(k % 2 + 1) * T] for k in range(KD)])
    at_g0 = ffn1.end
    at_g = lambda i, k: at_g0.plus(4 * i + k) if isinstance(i, int) else At(at_g0.c + k, at_g0.u + k, 4, i)
    w_gu = A["sgu_w_in_2"].rearrange("a k n -> (a k) n")
    N_GU = 2 * KD // 4
    out_gu = Project(o_gu, at_g0.plus(2 * KD), A["sgu_w_out_2"].rearrange("a k n -> (a k) n"), gh_hi, gh_lo,
                     lambda eng, k: eng.wait_ge(us_split, k + 1), gains_of(5))
    gu.close()

    def sp_gate(sp):
        def body(i, last):
            for k in range(4):
                at = at_g(i, k)
                load(sp, at, unit_parts(at, w_gu, (0, KD), (i * 4 * P + k * P, P)), (lo_ready, at.plus(-RAW).count))

        body(0, False)
        sp.wait_ge(unit_done, ffn1.end.u)
        ffn1.ready(sp, KD - 1)
        sp.dma_start(ws_in[:, :, :], A["sgu_ws_2"].rearrange("a g i j -> i (a g) j")).then_inc(gs_landed, 16)
        sp.dma_start(bs_row[:, :], A["sgu_bs_2"].rearrange("a g i -> a (g i)")).then_inc(gs_landed, 16)
        with sp.Fori(1, N_GU) as i:
            body(i, False)

    def pe_gate(pe):
        def body(i, last):
            for k in range(4):
                if not isinstance(i, int) or i:
                    pe.wait_ge(uv_scaled, i * 4 + (k - 3))
                ready = lead_g.half.pe_ready(pe) if isinstance(i, int) and i + k == 0 else None
                unit_products(pe, at_g(i, k), KD, bank[k][:, :], lambda k: gh_hi[:, k, :], lambda k: gh_lo[:, k, :],
                              True, True, ready)
                if ready is not None:
                    norm_g.pe_sums(pe)

        body(0, False)
        pe.wait_ge(gs_landed, 32)
        for h in range(2):
            for g in range(KD // 2):
                tr = pe.transpose(bank[5 + h][:, g * P:(g + 1) * P], ws_in[:, h * (KD // 2) + g, :], ident[:, :])
            tr.then_inc(wsT_done, 1)
        for h in range(2):
            b = (7, 4)[h]
            if h:
                pe.wait_ge(var_ready.sem, norm_g.var0 + 1)
            pe.matmul(bank[b][:, :], ones[0:1, :], bs_row[:, h * T:(h + 1) * T], start=True, stop=True)\
              .then_inc(bs_done, 1)
        with pe.Fori(1, N_GU) as i:
            body(i, False)
        for k in range(KD):
            pe.wait_ge(uv_ready, KD + k + 1)
            if k == 0:
                pe.wait_ge(wsT_ready, 2)
            mm = pe.matmul(bank[5][:, :], ones[:, :], uv[:, KD + k, :], start=k == 0, stop=k == KD - 1)
        mm.then_inc(mean_done, 1)
        norm_v.pe_sums(pe)
        for k in range(KD + 1):
            if k < KD:
                pe.wait_ge(vn_ready, k + 1)
                wait(pe, vt_ready, k - 1)
                for t in range(NT):
                    tr = pe.transpose(bank[k % 2][:, t * P:(t + 1) * P], uv[:, KD + k, t * P:(t + 1) * P], ident[:, :])
                tr.then_inc(vt_done, 1)
            if k:
                g = k - 1
                pe.wait_ge(vt_ready, g + 1)
                wait(pe, s_biased, g - 1)
                for t in range(NT):
                    mm = pe.matmul(bank[2 + g % 2][:, t * P:(t + 1) * P], v_tk[:, t, g * P:(g + 1) * P], wsT[:, g, :],
                                   start=True, stop=True)
                mm.then_inc(s_done, 1)
        out_gu.pe(pe)

    def act_gate(act):
        lead_g.act(act)

        def body(i, last):
            for k in range(4):
                split_hi(act, at_g(i, k).plus(2))
                if isinstance(i, int) and i + k == 0:
                    norm_g.act_root(act)
                act.wait_ge(uv_scaled, i * 4 + (k + 1))
                act.activation(tile_at(uv, i * 4 + k), tmp[:, k % 2, :], ACT.Gelu,
                               bias=col_at(vecs, i * 4 + (col["sgu_b"] + k))).then_inc(uv_ready, 1)

        body(0, False)
        for h in range(2):
            act.wait_ge(wsT_done, h + 1)
            act.activation(wsT[:, h * 4:(h + 1) * 4, :], bank[5 + h][:, :].rearrange("p (g c) -> p g c", c=P), ACT.Copy)\
               .then_inc(wsT_ready, 1)
        for h in range(2):
            act.wait_ge(bs_done, h + 1)
            act.activation(bs[:, h * 4:(h + 1) * 4, :], bank[(7, 4)[h]][:, :].rearrange("p (g c) -> p g c", c=P), ACT.Copy)\
               .then_inc(bs_ready, 1)
        with act.Fori(1, N_GU) as i:
            body(i, False)
        norm_v.act_squares(act)
        norm_v.act_root(act)
        for k in range(KD):
            act.wait_ge(v_scaled, k + 1)
            act.activation(uv[:, KD + k, :], tmp[:, k % 3, :], ACT.Identity, bias=v("ln_b", k)).then_inc(vn_ready, 1)
        for k in range(KD + 1):
            if k < KD:
                act.wait_ge(vt_done, k + 1)
                act.activation(v_tk[:, :, k * P:(k + 1) * P], bank[k % 2][:, :].rearrange("p (t c) -> p t c", t=NT),
                               ACT.Copy).then_inc(vt_ready, 1)
            if k:
                g = k - 1
                act.wait_ge(us_ready, g + 1)
                act.activation(gh_hi[:, g, :], tmp[:, g % 3, :], ACT.Copy).then_inc(us_hi, 1)
        out_gu.act(act)

    def dve_gate(dve):
        lead_g.dve(dve)

        def body(i, last):
            for k in range(4):
                split_lo(dve, at_g(i, k).plus(2))
                if isinstance(i, int) and i + k == 0:
                    norm_g.dve_rstd(dve)
                dve.wait_ge(unit_done, at_g(i, k).count)
                if not isinstance(i, int) or k >= 2:
                    dve.wait_ge(uv_ready, i * 4 + (k - 1))
                dve.tensor_tensor(tmp[:, k % 2, :], bank[k][:, :], rstd[:, :], ALU.mult).then_inc(uv_scaled, 1)

        body(0, False)
        dve.wait_ge(wsT_ready, 2)
        dve.memset(wsT[CH:P, :, 0:CH], 0.0).then_inc(bs_ready, 1)
        with dve.Fori(1, N_GU) as i:
            body(i, False)
        dve.wait_ge(mean_done, 1)
        for k in range(KD):
            dve.scalar_tensor_tensor(uv[:, KD + k, :], bank[5][:, :], -1.0 / D, uv[:, KD + k, :], ALU.mult, ALU.add)\
               .then_inc(v_centred, 1)
        norm_v.dve_rstd(dve)
        for k in range(KD):
            if k == 0:
                dve.wait_ge(uv_ready, 2 * KD)
            wait(dve, vn_ready, k - 2)
            dve.scalar_tensor_tensor(tmp[:, k % 3, :], uv[:, KD + k, :], v("ln_w", k), rstd[:, :], ALU.mult, ALU.mult)\
               .then_inc(v_scaled, 1)
        dve.wait_ge(vn_ready, KD)
        dve.wait_ge(bs_ready, 3)

        def lower(g):
            dve.wait_ge(us_hi, g + 1)
            dve.tensor_tensor(gh_lo[:, g, :], tmp[:, g % 3, :], gh_hi[:, g, :].bitcast(F32), ALU.subtract)\
               .then_inc(us_split, 1)

        for g in range(KD):
            dve.wait_ge(s_done, g + 1)
            wait(dve, us_split, g - 2)
            t = tmp[:, g % 3, :].rearrange("p (t c) -> p t c", t=NT)
            dve.tensor_tensor(t, bank[2 + g % 2][:, :].rearrange("p (t c) -> p t c", t=NT),
                              bs[:, g:g + 1, :].to_broadcast([P, NT, P]), ALU.add).then_inc(s_biased, 1)
            dve.wait_ge(s_biased, g + 1)
            dve.tensor_tensor(tmp[:, g % 3, :], tmp[:, g % 3, :], uv[:, g, :], ALU.mult).then_inc(us_ready, 1)
            if g:
                lower(g - 1)
        dve.wait_ge(us_ready, KD)
        lower(KD - 1)
        out_gu.dve(dve)

    ffn2 = FFN("2", out_gu.end, out_gu.res, gains_of(6), None, wg2[1], wu2[1], wd2[1], False, gains_of(7), final=True)

    with ExitStack() as part:
        x_out = sbs(part, "x_out", [P, NT, D])
    out_turned, out_landed = sem("out_turned"), sem("out_landed")
    out_copied, out_copied_too = sem("out_copied"), sem("out_copied_too")

    def pe_out(pe):
        for k in range(KD):
            ffn2.ready(pe, k)
            h, n = divmod(k, KD // 2)
            for t in range(NT):
                tr = pe.transpose(bank[4 * h + t][:, n * P:(n + 1) * P], x[:, k, t * P:(t + 1) * P], ident[:, :])
            if n == KD // 2 - 1:
                tr.then_inc(out_turned, 1)

    def act_out(act):
        for h in range(2):
            act.wait_ge(out_turned, h + 1)
            for t in range(0, NT, 2):
                act.activation(x_out[:, t, h * T:(h + 1) * T], bank[4 * h + t][:, :], ACT.Copy).then_inc(out_copied, 1)

    def dve_out(dve):
        for h in range(2):
            dve.wait_ge(out_turned, h + 1)
            for t in range(1, NT, 2):
                dve.tensor_copy(x_out[:, t, h * T:(h + 1) * T], bank[4 * h + t][:, :]).then_inc(out_copied_too, 1)

    def sp_out(sp):
        dst = out.rearrange("b (t p) d -> (b t) p d", p=P)
        for t in range(NT):
            sp.wait_ge((out_copied, out_copied_too)[t % 2], 3 + t // 2)
            sp.dma_start(dst[t], x_out[:, t, :]).then_inc(out_landed, 16)
        sp.wait_ge(out_landed, 16 * NT)

    N_ADD = 4
    block = ctx.enter_context(nc.Block())

    @block.sync
    def _(sp):
        sp_first_units(sp)
        ffn0.sp(sp)
        sp_time_mix(sp)
        out_tm.sp(sp, range(RAW))
        sp_blocks(sp)
        out_tm.sp(sp, range(RAW, KD))
        ffn1.sp(sp)
        sp_gate(sp)
        out_gu.sp(sp)
        ffn2.sp(sp)
        sp_out(sp)

    @block.gpsimd
    def _(pool):
        pool_setup(pool)
        norm1.pool_sum(pool)
        for m in range(EARLY, 6 * KD - N_ADD):
            ada_accumulate(pool, m)
        for k in range(1, KD - 1):
            if k <= N_ADD:
                ada_accumulate(pool, 6 * KD - N_ADD + k - 1)
            ffn0.norm.pool_add(pool, k)
        norm_f.pool_sum(pool)
        pool_masks(pool)
        pool_blocks(pool)
        out_tm.norm_o.pool_sum(pool)
        ffn1.pool(pool)
        norm_g.pool_sum(pool)
        out_gu.norm_o.pool_sum(pool)
        ffn2.pool(pool)

    @block.scalar
    def _(act):
        act_setup_dmas(act)
        act_setup(act)
        act_mixer1(act)
        ffn0.act(act)
        act_time_mix(act)
        act_blocks(act)
        act_split_y(act)
        out_tm.act(act)
        ffn1.act(act)
        act_gate(act)
        ffn2.act(act)
        act_out(act)

    @block.vector
    def _(dve):
        dve_mixer1(dve)
        scaled_gain(dve, "norm2", 4)
        ffn0.dve(dve)
        dve_final(dve)
        dve_time_mix(dve)
        dve_blocks(dve)
        dve_split_y(dve)
        out_tm.dve(dve)
        ffn1.dve(dve)
        dve_gate(dve)
        ffn2.dve(dve)
        dve_out(dve)

    @block.tensor
    def _(pe):
        pe_setup(pe)
        pe_mixer1(pe)
        ffn0.pe(pe)
        pe_time_mix(pe)
        pe_blocks(pe)
        out_tm.pe(pe)
        ffn1.pe(pe)
        pe_gate(pe)
        ffn2.pe(pe)
        pe_out(pe)

    return ctx


_INS = ["x", "c", "positions", "ada_w", "ada_b", "norm1_g", "w_in", "b_in", "conv_w", "attn_sinks",
        "out_norm_attn_g", "out_norm_conv_g", "w_o", "norm2_g", "w_up", "ffn_conv_w", "ffn_conv_b", "w_down",
        "final_norm_g", "norm_gains_2", "rwkv_mix_2", "rwkv_w_rkv_2", "rwkv_w0_2", "rwkv_w1_2", "rwkv_w2_2",
        "rwkv_a0_2", "rwkv_a1_2", "rwkv_a2_2", "rwkv_g1_2", "rwkv_g2_2", "rwkv_k_k_2", "rwkv_k_a_2",
        "rwkv_r_k_2", "rwkv_gn_w_2", "rwkv_gn_b_2", "rwkv_w_o_2", "sgu_w_in_2", "sgu_b_in_2", "sgu_ln_w_2",
        "sgu_ln_b_2", "sgu_ws_2", "sgu_bs_2", "sgu_w_out_2", "ffn_w_gate_2", "ffn_w_up_2", "ffn_w_down_2"]
ROPE_THETA = 10000.0


def kernel(**inputs):
    import numpy as _np
    import concourse.bacc as _bacc
    from concourse import mybir as _mybir
    from concourse.bass_utils import run_bass_kernel_spmd as _run

    arrays = {name: _np.ascontiguousarray(inputs[name]) for name in _INS}
    half = HD // 2
    inv = ROPE_THETA ** (-_np.arange(half, dtype=_np.float32) / _np.float32(half))
    arrays["inv_freq"] = _np.tile(inv.astype(_np.float32), P // half).reshape(P, 1)

    nc = _bacc.Bacc("TRN2", target_bir_lowering=False, num_devices=1)
    A = {name: nc.dram_tensor(f"in_{name}_dram", a.shape, _mybir.dt.from_np(a.dtype), kind="ExternalInput").ap()
         for name, a in arrays.items()}
    out = nc.dram_tensor("out_0_dram", (1, T, D), F32, kind="ExternalOutput").ap()
    with build(nc, A, out):
        pass
    r = _run(nc, [{f"in_{name}_dram": a for name, a in arrays.items()}], core_ids=[0])
    return r.results[0]["out_0_dram"]
```
